# Optimizing a Trainium2 kernel written in Bass

```python
import jax, jax.numpy as jnp
from jax import lax
import numpy as np

D_MODEL = 1024
BATCH = 1
SEQ = 256
DEPTH = 1
DEC_BATCH = 8
DEC_SEQ = 4
PAST_LEN = 2048
PAGE_SIZE = 128

D_RNN = D_MODEL
N_GATE_BLOCKS = 8
GATE_BLOCK = D_RNN // N_GATE_BLOCKS
CONV_A_WIDTH = 4
RG_C = 8.0
D_CONF = D_MODEL
CONF_WIDTH = 31
N_EXPERTS = 32
TOP_K = 4
D_EXPERT = D_MODEL
SWIGLU_LIMIT = 7.0
SWIGLU_ALPHA = 1.702
EPS = 1e-6
D_IN = D_RNN + 2 * D_CONF + 2 * D_MODEL

kernel_name = 'hawk_conformer_moe_parallel_step'

def rmsnorm(x, g):
    x32 = x.astype(jnp.float32)
    y = x32 * lax.rsqrt(jnp.mean(x32 * x32, axis=-1, keepdims=True) + EPS)
    return (y * g.astype(jnp.float32)).astype(x.dtype)

def layernorm(x, g, b):
    x32 = x.astype(jnp.float32)
    mu = jnp.mean(x32, axis=-1, keepdims=True)
    xc = x32 - mu
    y = xc * lax.rsqrt(jnp.mean(xc * xc, axis=-1, keepdims=True) + EPS)
    return (y * g.astype(jnp.float32) + b.astype(jnp.float32)).astype(x.dtype)

def causal_dwconv(x, buf, w, b):
    k = w.shape[0]
    xcat = jnp.concatenate([buf.astype(x.dtype), x], axis=1)
    y = lax.conv_general_dilated(xcat, w[:, None, :].astype(x.dtype), window_strides=(1,),
                                 padding='VALID', dimension_numbers=('NWC', 'WIO', 'NWC'),
                                 feature_group_count=x.shape[-1])
    return y + b, xcat[:, xcat.shape[1] - (k - 1):]

def block_diag(x, w, b):
    bsz, t, _ = x.shape
    xb = x.reshape(bsz, t, N_GATE_BLOCKS, GATE_BLOCK)
    y = jnp.einsum('btnc,ncd->btnd', xb, w)
    return y.reshape(bsz, t, D_RNN) + b

def rglru(x, h0, w_a, b_a, w_x, b_x, lam):
    r = jax.nn.sigmoid(block_diag(x, w_a, b_a).astype(jnp.float32))
    i = jax.nn.sigmoid(block_diag(x, w_x, b_x).astype(jnp.float32))
    log_a = -RG_C * r * jax.nn.softplus(-lam.astype(jnp.float32))
    a = jnp.exp(log_a)
    u = jnp.sqrt(-jnp.expm1(2.0 * log_a)) * (i * x.astype(jnp.float32))

    def step(h, au):
        a_t, u_t = au
        h = a_t * h + u_t
        return h, h

    h_last, hs = lax.scan(step, h0.astype(jnp.float32),
                          (jnp.swapaxes(a, 0, 1), jnp.swapaxes(u, 0, 1)))
    return jnp.swapaxes(hs, 0, 1).astype(x.dtype), h_last

def moe(x, w_router, b_router, w_gate, b_gate, w_up, b_up, w_down, b_down):
    bsz, t, d = x.shape
    xf = x.reshape(-1, d)
    logits = (xf @ w_router).astype(jnp.float32) + b_router.astype(jnp.float32)
    vals, idx = lax.top_k(logits, TOP_K)
    probs = jax.nn.softmax(vals, axis=-1)
    combine = jnp.einsum('nk,nke->ne', probs, jax.nn.one_hot(idx, N_EXPERTS, dtype=jnp.float32))
    out = jnp.zeros((xf.shape[0], d), jnp.float32)
    for e in range(N_EXPERTS):
        g = jnp.minimum(xf @ w_gate[e] + b_gate[e], SWIGLU_LIMIT)
        u = jnp.clip(xf @ w_up[e] + b_up[e], -SWIGLU_LIMIT, SWIGLU_LIMIT)
        hdn = (u + 1.0) * (g * jax.nn.sigmoid(SWIGLU_ALPHA * g))
        out = out + combine[:, e:e + 1] * (hdn @ w_down[e] + b_down[e]).astype(jnp.float32)
    return out.astype(x.dtype).reshape(bsz, t, d)

def layer(x, conv_a_buf, h0, conf_buf, g_mix, w_in, w_conv_a, b_conv_a, w_rg_a, b_rg_a,
          w_rg_x, b_rg_x, rg_lambda, w_conf_dw, b_conf_dw, g_conf_ln, b_conf_ln, w_conf_pw,
          b_conf_pw, w_out, g_ffn, w_router, b_router, w_gate, b_gate, w_up, b_up, w_down, b_down):
    hn = rmsnorm(x, g_mix)
    z = hn @ w_in
    o1 = D_RNN
    o2 = o1 + 2 * D_CONF
    o3 = o2 + D_MODEL
    xa, u_glu, gate_a, gate_b = z[..., :o1], z[..., o1:o2], z[..., o2:o3], z[..., o3:]
    xa_c, new_conv_a = causal_dwconv(xa, conv_a_buf, w_conv_a, b_conv_a)
    y_a, h_last = rglru(xa_c, h0, w_rg_a, b_rg_a, w_rg_x, b_rg_x, rg_lambda)
    v = u_glu[..., :D_CONF] * jax.nn.sigmoid(u_glu[..., D_CONF:])
    v_c, new_conf = causal_dwconv(v, conf_buf, w_conf_dw, b_conf_dw)
    y_b = jax.nn.silu(layernorm(v_c, g_conf_ln, b_conf_ln)) @ w_conf_pw + b_conf_pw
    m = jax.nn.sigmoid(gate_a) * y_a + jax.nn.sigmoid(gate_b) * y_b
    h = x + m @ w_out
    y = h + moe(rmsnorm(h, g_ffn), w_router, b_router, w_gate, b_gate, w_up, b_up, w_down, b_down)
    return y, new_conv_a, h_last, new_conf

def setup_inputs(seed: int = 0) -> dict:
    key = jax.random.key(seed)
    ks = jax.random.split(key, 40)
    f32 = jnp.float32
    nrm = lambda k, shape, s: jax.random.normal(k, shape, f32) * s
    L = DEPTH
    lam_u = jax.random.uniform(ks[10], (L, D_RNN), f32, minval=0.9, maxval=0.999)
    lam_s = lam_u ** (1.0 / RG_C)
    return {
        'x_prompt': nrm(ks[0], (BATCH, SEQ, D_MODEL), 1.0),
        'x_sample': nrm(ks[1], (DEC_BATCH, DEC_SEQ, D_MODEL), 1.0),
        'state_conv_a': nrm(ks[2], (L, DEC_BATCH, CONV_A_WIDTH - 1, D_RNN), 1.0),
        'state_h': nrm(ks[3], (L, DEC_BATCH, D_RNN), 0.5),
        'state_conf': nrm(ks[4], (L, DEC_BATCH, CONF_WIDTH - 1, D_CONF), 0.5),
        'g_mix': 1.0 + nrm(ks[5], (L, D_MODEL), 0.02),
        'w_in': nrm(ks[6], (L, D_MODEL, D_IN), D_MODEL ** -0.5),
        'w_conv_a': nrm(ks[7], (L, CONV_A_WIDTH, D_RNN), CONV_A_WIDTH ** -0.5),
        'b_conv_a': nrm(ks[8], (L, D_RNN), 0.02),
        'w_rg_a': nrm(ks[9], (L, N_GATE_BLOCKS, GATE_BLOCK, GATE_BLOCK), GATE_BLOCK ** -0.5),
        'b_rg_a': nrm(ks[11], (L, D_RNN), 0.02),
        'w_rg_x': nrm(ks[12], (L, N_GATE_BLOCKS, GATE_BLOCK, GATE_BLOCK), GATE_BLOCK ** -0.5),
        'b_rg_x': nrm(ks[13], (L, D_RNN), 0.02),
        'rg_lambda': jnp.log(lam_s) - jnp.log1p(-lam_s),
        'w_conf_dw': nrm(ks[14], (L, CONF_WIDTH, D_CONF), CONF_WIDTH ** -0.5),
        'b_conf_dw': nrm(ks[15], (L, D_CONF), 0.02),
        'g_conf_ln': 1.0 + nrm(ks[16], (L, D_CONF), 0.02),
        'b_conf_ln': nrm(ks[17], (L, D_CONF), 0.02),
        'w_conf_pw': nrm(ks[18], (L, D_CONF, D_MODEL), D_CONF ** -0.5),
        'b_conf_pw': nrm(ks[19], (L, D_MODEL), 0.02),
        'w_out': nrm(ks[20], (L, D_MODEL, D_MODEL), D_MODEL ** -0.5),
        'g_ffn': 1.0 + nrm(ks[21], (L, D_MODEL), 0.02),
        'w_router': nrm(ks[22], (L, D_MODEL, N_EXPERTS), D_MODEL ** -0.5),
        'b_router': nrm(ks[23], (L, N_EXPERTS), 0.01),
        'w_gate': nrm(ks[24], (L, N_EXPERTS, D_MODEL, D_EXPERT), D_MODEL ** -0.5),
        'b_gate': nrm(ks[25], (L, N_EXPERTS, D_EXPERT), 0.02),
        'w_up': nrm(ks[26], (L, N_EXPERTS, D_MODEL, D_EXPERT), D_MODEL ** -0.5),
        'b_up': nrm(ks[27], (L, N_EXPERTS, D_EXPERT), 0.02),
        'w_down': nrm(ks[28], (L, N_EXPERTS, D_EXPERT, D_MODEL), D_EXPERT ** -0.5),
        'b_down': nrm(ks[29], (L, N_EXPERTS, D_MODEL), 0.02),
        'g_final': 1.0 + nrm(ks[30], (D_MODEL,), 0.02),
    }

def reference(x_prompt, x_sample, state_conv_a, state_h, state_conf, g_mix, w_in, w_conv_a,
              b_conv_a, w_rg_a, b_rg_a, w_rg_x, b_rg_x, rg_lambda, w_conf_dw, b_conf_dw,
              g_conf_ln, b_conf_ln, w_conf_pw, b_conf_pw, w_out, g_ffn, w_router, b_router,
              w_gate, b_gate, w_up, b_up, w_down, b_down, g_final):
    layer_params = (g_mix, w_in, w_conv_a, b_conv_a, w_rg_a, b_rg_a, w_rg_x, b_rg_x, rg_lambda,
                    w_conf_dw, b_conf_dw, g_conf_ln, b_conf_ln, w_conf_pw, b_conf_pw, w_out,
                    g_ffn, w_router, b_router, w_gate, b_gate, w_up, b_up, w_down, b_down)
    bp = x_prompt.shape[0]
    hp, hs = x_prompt, x_sample
    p_conv_a, p_h, p_conf, s_conv_a, s_h, s_conf = [], [], [], [], [], []
    for l in range(DEPTH):
        lp = [p[l] for p in layer_params]
        hp, ca, hh, cf = layer(hp,
                               jnp.zeros((bp, CONV_A_WIDTH - 1, D_RNN), hp.dtype),
                               jnp.zeros((bp, D_RNN), jnp.float32),
                               jnp.zeros((bp, CONF_WIDTH - 1, D_CONF), hp.dtype),
                               *lp)
        p_conv_a.append(ca)
        p_h.append(hh)
        p_conf.append(cf)
        hs, ca, hh, cf = layer(hs, state_conv_a[l], state_h[l], state_conf[l], *lp)
        s_conv_a.append(ca)
        s_h.append(hh)
        s_conf.append(cf)
    y_prompt = rmsnorm(hp, g_final)
    y_sample = rmsnorm(hs, g_final)
    return (y_prompt, y_sample, jnp.stack(p_conv_a), jnp.stack(p_h), jnp.stack(p_conf),
            jnp.stack(s_conv_a), jnp.stack(s_h), jnp.stack(s_conf))


_drawn_inputs = setup_inputs


def setup_inputs(seed=0):
    import zlib

    import numpy as np

    out = dict(_drawn_inputs(seed))
    spreads = {}
    factors = {'b_rg_a': 12.833,
     'b_conf_ln': 3.131,
     'b_router': 3.109,
     'b_gate': 6.605,
     'b_up': 8.0,
     'b_down': 6.285,
     'g_final': 21.28,
     'b_rg_x': 5.056}
    for name, (base, spread) in spreads.items():
        noise = np.random.default_rng([zlib.crc32(name.encode()), seed]).standard_normal(out[name].shape)
        drawn = base * np.exp(spread * noise) if base else spread * noise
        out[name] = __import__('jax').numpy.asarray(drawn.astype(out[name].dtype))
    for name, factor in factors.items():
        out[name] = (out[name] * factor).astype(out[name].dtype)
    return out
```

```python
from contextlib import ExitStack

import numpy as np

import concourse.bass as bass
from concourse import mybir
from concourse.alu_op_type import AluOpType as ALU

ACT = mybir.ActivationFunctionType
F32 = mybir.dt.float32
BF16 = mybir.dt.bfloat16
I32 = mybir.dt.int32
AX_X = mybir.AxisListType.X

P = 128
D = 1024
NT = D // P
T_P = 256
SEQS, STEPS = 8, 4
T_S = SEQS * STEPS
T = T_P + T_S
TILES = 3
T_PAD = TILES * P
KA, KC = 4, 31
HA, HC = KA - 1, KC - 1
E = 32
CAP = 64
EPS = 1e-6
RG_C = 8.0
LIMIT, ALPHA = 7.0, 1.702

W_DW, W_CA, B_CA, B_RA, B_RX, LAM, B_DW, G_LN, B_LN, B_PW = 0, 31, 35, 36, 37, 38, 39, 40, 41, 42
N_PAR = 43

SLOTS = 6
SLOT = 4096
MIX_CHUNKS = 14

BK_GU, BK_D, BK_X, BK_SEL, BK_HT, BK_OUT = 0, 2, 3, 4, 5, 6


def mixer_jobs():
    jobs = [("par", "v"), ("sta", "v")] + [(f"stc{i}", "a") for i in range(4)]
    jobs += [(f"hn{k}", "av"[k % 2]) for k in range(NT)]
    for c in range(NT):
        jobs += [(f"va{c}", "a"), (f"vb{c}", "a")]
    jobs += [(f"xa{c}", "a") for c in range(NT)]
    jobs += [(f"{n}{h}", "a") for n in ("vp", "vs", "xp", "xs") for h in range(2)]
    jobs += [(f"ga{c}", "a") for c in range(NT)]
    jobs += [("mean", "v")]
    for c in range(NT):
        jobs += [(f"r{c}", "a"), (f"i{c}", "a")]
    jobs += [(f"gb{c}", "a") for c in range(NT)]
    jobs += [("var", "v")]
    jobs += [(f"pw{c}", "v") for c in range(NT)]
    jobs += [(f"ho{h}", "a") for h in range(2)]
    jobs += [(f"out{i}{h}", "v") for i in range(2) for h in range(2)] + [("out2", "v")]
    jobs += [(f"ht{k}", "av"[k % 2]) for k in range(NT)]
    jobs += [("logits", "v"), ("rank", "v")]
    return jobs


JOBS = mixer_jobs()
JOB = {name: j for j, (name, _) in enumerate(JOBS)}


def emptied_before(j, who):
    return sum(w == who for _, w in JOBS[:j + 1])


def build(nc, A, O):
    with ExitStack() as ctx:
        def sb(name, shape, dt=F32):
            return ctx.enter_context(nc.sbuf_tensor(name, shape, dt))

        def sem(name):
            return ctx.enter_context(nc.semaphore(name))

        ring = sb("ring", [P, SLOTS, SLOT])
        acc = sb("acc", [P, TILES, D])
        par = sb("par", [P, NT, N_PAR])
        w_rg = sb("w_rg", [P, 2, NT, P])
        w_rt = sb("w_rt", [P, NT, E])
        b_rt = sb("b_rt", [P, E])
        g_mix = sb("g_mix_c", [P, NT])
        g_ffn = sb("g_ffn_c", [P, NT])
        ident = sb("ident", [P, P])
        ones = sb("ones", [P, P])
        slot_no = sb("slot_no", [P, 2, CAP])
        tri = sb("tri", [P, P], BF16)
        ones_h = sb("ones_h", [P, P], BF16)
        h0 = sb("h0", [P, NT, SEQS])
        stat = sb("stat", [P, 8 * TILES])
        lamw = sb("lamw", [P, 6, NT])
        lg = sb("lg", [P, TILES, E + 4])
        lgr = sb("lgr", [P, TILES, E + 4])
        top = sb("top", [P, TILES, 8])
        mask = sb("mask", [P, TILES, E])
        mask_h = sb("mask_h", [P, TILES, E], BF16)
        comb = sb("comb", [P, TILES, E])
        rank = sb("rank", [P, TILES, E])
        rnk2 = sb("rnk2", [P, TILES, E])
        counts = sb("counts", [P, E + 1], I32)
        cntf = sb("cntf", [P, E + 1])

        WS = 21400
        ws = sb("ws", [P, WS])
        at = [0]

        def take(words):
            at[0] += words
            assert at[0] <= WS, at
            return ws[:, at[0] - words:at[0]]

        TW = NT * T
        XA_W, VX_W = HA + T_P + SEQS * (HA + STEPS), HC + T_P + SEQS * (HC + STEPS)
        hn_w = take(TW)
        xa_w = take(NT * XA_W)
        vx_w = take(NT * VX_W)
        ga_w = take(2 * TW)
        vc_w = take(TW)
        xc_w = take(TW)
        ig_w = take(TW)
        sg_w = take(2 * T)

        def by_tile(w, n=T):
            return w[:, 0:NT * n].rearrange("p (c t) -> p c t", c=NT)

        hn = by_tile(hn_w)
        xa = by_tile(xa_w, XA_W)
        vx = by_tile(vx_w, VX_W)
        gate_a = by_tile(ga_w[:, 0:TW])
        gate_b = by_tile(ga_w[:, TW:2 * TW])
        vc = by_tile(vc_w)
        xc = by_tile(xc_w)
        ig = by_tile(ig_w)
        sg = sg_w.rearrange("p (b t) -> p b t", b=2)
        rt = by_tile(vx_w)
        aa = by_tile(xa_w)
        mt = by_tile(xa_w)
        x_tok = ga_w[:, 0:TILES * D].rearrange("p (i d) -> p i d", i=TILES)
        junk = vc_w[:, 0:D]
        par_rows = xc_w[:, 0:D]
        sta_rows = xc_w[:, D:2 * D]
        stc_rows = ig_w[:, 0:2 * D].rearrange("p (h d) -> p h d", h=2)
        st_v = ga_w[:, TW:TW + 2 * D].rearrange("p (b d) -> p b d", b=2)
        st_x = ig_w[:, 0:2 * D].rearrange("p (b d) -> p b d", b=2)
        v_new = ig_w[:, 2 * D:2 * D + NT * T_S].rearrange("p (c t) -> p c t", c=NT)
        xa_new = ga_w[:, TW + 2 * D:TW + 2 * D + NT * SEQS * HA].rearrange("p (c t) -> p c t", c=NT)
        st_h = hn_w[:, 0:D]

        at[0] = 0
        h_tok = take(TILES * D).rearrange("p (i d) -> p i d", i=TILES)
        h_cm_w = take(NT * T_PAD)
        h_cm = h_cm_w.rearrange("p (k t) -> p k t", k=NT)
        g_fin = h_cm_w[:, 0:D]
        h_split = take(3 * TILES * D // 2).bitcast(BF16).rearrange("p (s i d) -> p s i d", s=3, i=TILES)
        x_e = take(2 * NT * CAP).rearrange("p (b k s) -> p b k s", b=2, k=NT)
        hid_t = take(2 * NT * CAP).rearrange("p (b k s) -> p b k s", b=2, k=NT)
        y_e = take(2 * D // 2).rearrange("p (b n) -> p b n", b=2)
        g_e = take(D)[0:CAP]
        sig_e = take(D)[0:CAP]
        u_e = take(D)[0:CAP]
        hid = take(D)[0:CAP]
        sel = take(2 * TILES * CAP // 2).bitcast(BF16).rearrange("p (b i s) -> p b i s", b=2, i=TILES)
        sel_w = take(2 * TILES * 2 * CAP).rearrange("p (b i d s) -> p b i d s", b=2, i=TILES, d=2)
        sel_t = take(2 * T_PAD).rearrange("p (b t) -> p b t", b=2)
        pick = take(2 * 3 * CAP).rearrange("p (b m s) -> p b m s", b=2, m=3)
        at[0] = max(at[0], WS - 2 * T - D)
        bias = take(D)
        ps = ctx.enter_context(nc.psum_tensor("ps", [P, 8, 512], F32))

        def bank(j):
            return ps[:, j % 8, :]

        s_x = sem("x_loaded")
        s_par = sem("params_loaded")
        s_sta = sem("conv_a_and_h_state_loaded")
        s_stc = sem("conf_state_loaded")
        s_gain = sem("gains_loaded")
        s_rt = sem("router_loaded")
        s_bias = sem("bias_loaded")
        s_gfin = sem("g_final_loaded")
        s_wrg = sem("gate_blocks_loaded")
        landed = [sem(f"slot{s}_landed") for s in range(SLOTS)]
        used = sem("chunks_used")
        filled = sem("psum_filled")
        empt_a = sem("psum_emptied_by_scalar")
        empt_v = sem("psum_emptied_by_vector")
        s_zero = sem("zeros_ready")
        s_const = sem("constants_ready")
        s_seed = sem("constant_seeds_ready")
        ord_v = sem("vector_order")
        ord_a = sem("scalar_order")
        s_sq = sem("squares_summed")
        s_ms = sem("mean_squares_ready")
        s_root = sem("roots_ready")
        s_xn = sem("x_normed")
        s_v = sem("v_ready")
        s_conv = sem("conf_conv_steps")
        s_xc = sem("conv_a_steps")
        s_new = sem("new_columns_packed")
        s_store = sem("output_rows_stored")
        s_sqv = sem("centred_squared")
        s_squ = sem("centred_squares_used")
        s_lam = sem("decay_exponent_ready")
        s_lexp = sem("decay_exponential_ready")
        s_sp = sem("decay_scales_ready")
        s_aw = sem("decay_and_tanh_ready")
        s_w = sem("tanh_used")
        s_rtt = sem("root_of_tanh_ready")
        s_hs = sem("states_ready")
        s_ln = sem("layer_norm_ready")
        s_sil = sem("silu_gate_ready")
        s_s = sem("silu_ready")
        s_m = sem("merged_ready")
        s_hn = sem("h_normed")
        s_split = sem("h_parts_cast")
        s_rest = sem("h_rest_ready")
        s_neg = sem("router_shift_ready")
        s_exp = sem("router_exponentials_ready")
        s_mask = sem("mask_ready")
        s_cnt = sem("counts_ready")
        s_sel = sem("selections_ready")
        s_selw = sem("weighted_selections_ready")
        s_pick = sem("gate_up_bias_picks_ready")
        s_pickd = sem("down_bias_picks_ready")
        s_xg = sem("piece_inputs_gathered")
        s_xe = sem("piece_inputs_in_sbuf")
        s_gc = sem("gate_clamped")
        s_uc = sem("up_clamped")
        s_sig = sem("gate_sigmoid_ready")
        s_prod = sem("gate_up_product_ready")
        s_hid = sem("hidden_ready")
        s_htp = sem("hidden_turned")
        s_hts = sem("hidden_t_in_sbuf")
        s_stp = sem("selection_turned")
        s_sts = sem("selection_t_in_sbuf")
        s_y = sem("piece_output_in_sbuf")
        s_sc = sem("output_spread_to_tokens")
        s_add = sem("output_added")
        s_sum = sem("output_complete")
        s_fin = sem("final_rows_ready")
        s_end = sem("results_stored")

        def flat(ap):
            n = len(ap.shape)
            return ap if n == 2 else ap.rearrange({3: "a b c -> (a b) c", 4: "a b c d -> (a b c) d"}[n])

        w_in = A["w_in"][0].rearrange("(p k) n -> p k n", k=NT)
        w_pw = A["w_conf_pw"][0].rearrange("(k p) n -> p k n", p=P)
        w_out = A["w_out"][0].rearrange("(k p) n -> p k n", p=P)
        w_gate = A["w_gate"][0].rearrange("e (p k) n -> e p (k n)", k=NT)
        w_up = A["w_up"][0].rearrange("e (p k) n -> e p (k n)", k=NT)
        w_down = A["w_down"][0].rearrange("e (p k) n -> e p (k n)", k=NT)
        HALF = SLOT // 2

        def slot_half(n, h):
            return ring[:, n % SLOTS, h * HALF:(h + 1) * HALF]

        def w_in_cols(n, h):
            if n < 4:
                return D + h * D + n * 256
            return [0, 0, 3 * D, 3 * D, 4 * D, 4 * D][n - 4] + (n % 2) * 512 + h * 256

        def gu_chunk(e, q):
            return 6 * e - 2 + q

        def d_chunk(e, q):
            return 6 * e + 8 + q

        LAST_D = 6 * (E - 1) + 4
        N_CHUNKS = LAST_D + 2

        def slot_of(m):
            return (MIX_CHUNKS + m) % SLOTS

        def landed_by(m0, e=0):
            return 32 * ((MIX_CHUNKS + m0) // SLOTS + 1) + 32 * e

        LAST_FILL = ["vb1", "vb3", "vb5", "vb7", "xa3", "xa7", "ga3", "ga7", "gb3", "gb7", "pw7", "pw7", "out2", "out2"]
        EA = lambda name: emptied_before(JOB[name], "a")
        EV = lambda name: emptied_before(JOB[name], "v")
        N_STORES = 16 * 14
        N_CONV, N_XC = 2 * NT * KC, 2 * NT * KA

        def more_pieces(eng, piece, before=None):
            eng.wait_ge(s_cnt, 1)
            most = eng.value_load(counts[0:1, E:E + 1], min_val=0, max_val=T)
            with eng.If(most > CAP):
                done = eng.alloc_register("pieces_done")
                eng.reg_mov(done, 0)
                with eng.Fori(1, -(-T // CAP)) as r:
                    if before is not None:
                        before(r)
                    with eng.Fori(0, E) as e:
                        count = eng.value_load(counts[0:1, bass.ds(e, 1)], min_val=0, max_val=T)
                        with eng.If(count > r * CAP):
                            piece(e, eng.snap(done), r)
                            eng.reg_add(done, done, 1)

        with nc.Block() as block:

            @block.sync
            def _(sp):
                sp.dma_start(acc[:, 0:2, :], A["x_prompt"][0].rearrange("(i p) d -> p i d", p=P)).then_inc(s_x, 16)
                sp.wait_ge(s_zero, 1)
                sp.dma_start(acc[0:T_S, 2, :], flat(A["x_sample"])).then_inc(s_x, 16)
                for n in range(MIX_CHUNKS):
                    if n == 2:
                        for m, name in enumerate(("w_rg_a", "w_rg_x")):
                            sp.dma_start(w_rg[:, m], A[name][0].rearrange("n c d -> c n d")).then_inc(s_wrg, 16)
                    if n >= SLOTS:
                        sp.wait_ge(filled, JOB[LAST_FILL[n - SLOTS]] + 1)
                    for h in range(2):
                        if n < 10:
                            c = w_in_cols(n, h)
                            dst = slot_half(n, h).rearrange("p (k n) -> p k n", k=NT)
                            sp.dma_start(dst, w_in[:, :, c:c + 256]).then_inc(landed[n % SLOTS], 16)
                        else:
                            w, q = (w_pw, n - 10) if n < 12 else (w_out, n - 12)
                            dst = slot_half(n, h).rearrange("p (k n) -> p k n", k=2)
                            k = 4 * q + 2 * h
                            sp.dma_start(dst, w[:, k:k + 2, :]).then_inc(landed[n % SLOTS], 16)

                def load(e, m, slot, kind, q):
                    if type(m) is int and m < SLOTS:
                        sp.wait_ge(filled, JOB[LAST_FILL[MIX_CHUNKS - SLOTS + m]] + 1)
                    else:
                        sp.wait_ge(used, m - SLOTS + 1)
                    for h in range(2):
                        dst = ring[:, slot, h * HALF:(h + 1) * HALF]
                        if kind == "gu":
                            src = (w_gate, w_up)[h][e, :, q * HALF:(q + 1) * HALF]
                        else:
                            src = w_down[e, :, q * SLOT + h * HALF:q * SLOT + (h + 1) * HALF]
                        sp.dma_start(dst, src).then_inc(landed[slot], 16)

                for q in range(4):
                    load(0, q, slot_of(q), "gu", q)
                for q in range(4):
                    load(1, gu_chunk(1, q), slot_of(gu_chunk(1, q)), "gu", q)
                for q in range(2):
                    load(0, d_chunk(0, q), slot_of(d_chunk(0, q)), "d", q)
                with sp.Fori(2, E) as e:
                    for q in range(4):
                        load(e, gu_chunk(e, q), slot_of(gu_chunk(2, q)), "gu", q)
                    for q in range(2):
                        load(e - 1, d_chunk(e - 1, q), slot_of(d_chunk(1, q)), "d", q)
                for q in range(2):
                    load(E - 1, LAST_D + q, slot_of(LAST_D + q), "d", q)

                def load_piece(e, n, r):
                    for q in range(6):
                        load(e, N_CHUNKS + 6 * n + q, slot_of(N_CHUNKS + q), "gu" if q < 4 else "d", q % 4)
                more_pieces(sp, load_piece)
                sp.wait_ge(s_fin, 2)
                sp.dma_start(O[0][0].rearrange("(i p) d -> p i d", p=P), h_tok[:, 0:2, :]).then_inc(s_end, 16)
                sp.wait_ge(s_fin, 3)
                sp.dma_start(flat(O[1]), h_tok[0:T_S, 2, :]).then_inc(s_end, 16)
                sp.wait_ge(s_end, 32)


            @block.gpsimd
            def _(pool):
                pool.memset(ident[:], 0.0).then_inc(s_seed, 1)
                pool.memset(tri[:], 1.0).then_inc(s_seed, 1)
                pool.memset(ones[:], 1.0 / D).then_inc(s_const, 1)
                pool.memset(ones_h[:], 1.0).then_inc(s_const, 1)
                pool.wait_ge(s_seed, 1)
                pool.affine_select(out=ident[:], in_=ident[:], compare_op=ALU.not_equal, fill=1.0, base=0,
                                   pattern=[[-1, P]], channel_multiplier=1).then_inc(s_const, 1)
                pool.wait_ge(s_seed, 2)
                pool.affine_select(out=tri[:], in_=tri[:], compare_op=ALU.is_gt, fill=0.0, base=0,
                                   pattern=[[1, P]], channel_multiplier=-1).then_inc(s_const, 1)
                pool.iota(slot_no[:], [[0, 2], [1, CAP]], base=0, channel_multiplier=0,
                          allow_small_or_imprecise_dtypes=True).then_inc(s_const, 1)
                pool.dma_start(O[7][0][:, 0:HC - STEPS, :], A["state_conf"][0][:, STEPS:HC, :]).then_inc(s_store, 16)
                for c in range(NT):
                    pool.wait_ge(empt_a, EA(f"vb{c}"))
                    v = vx[:, c, HC:HC + T_P]
                    pool.tensor_tensor(v, v, sg[:, c % 2, 0:T_P], ALU.mult).then_inc(s_v, 1)
                    v = vx[:, c, HC + T_P:].rearrange("p (s t) -> p s t", s=SEQS)[:, :, HC:]
                    pool.tensor_tensor(v, v, sg[:, c % 2, T_P:].rearrange("p (s t) -> p s t", s=SEQS),
                                       ALU.mult).then_inc(s_v, 1)
                pool.wait_ge(s_v, 2 * NT)
                pool.tensor_copy(v_new.rearrange("p c (s t) -> p c s t", s=SEQS),
                                 vx[:, :, HC + T_P:].rearrange("p c (s t) -> p c s t", s=SEQS)[:, :, :, HC:]).then_inc(s_new, 1)
                pool.wait_ge(empt_a, EA("xa7"))
                pool.tensor_copy(xa_new.rearrange("p c (s t) -> p c s t", s=SEQS),
                                 xa[:, :, HA + T_P:].rearrange("p c (s t) -> p c s t", s=SEQS)[:, :, :, STEPS:]).then_inc(s_new, 1)
                pool.wait_ge(empt_a, EA("vp1"))
                pool.dma_start(flat(O[4][0]), st_v[0:HC, 0, :]).then_inc(s_store, 16)
                pool.wait_ge(empt_a, EA("vs1"))
                for s in range(SEQS):
                    pool.dma_start(O[7][0][s, HC - STEPS:, :], st_v[s * STEPS:(s + 1) * STEPS, 1, :]).then_inc(s_store, 16)
                pool.wait_ge(empt_a, EA("xp1"))
                pool.dma_start(flat(O[2][0]), st_x[0:HA, 0, :]).then_inc(s_store, 16)
                pool.wait_ge(empt_a, EA("xs1"))
                pool.dma_start(flat(O[5][0]), st_x[0:SEQS * HA, 1, :]).then_inc(s_store, 16)
                pool.wait_ge(empt_a, EA("ho1"))
                pool.dma_start(O[3][0], st_h[0:1, :]).then_inc(s_store, 16)
                pool.dma_start(O[6][0], st_h[1:1 + SEQS, :]).then_inc(s_store, 16)
                pool.wait_ge(s_m, NT + 1)
                for m, name in enumerate(("b_gate", "b_up", "b_down")):
                    pool.dma_start(bias[m * E:(m + 1) * E, :], A[name][0]).then_inc(s_bias, 16)
                pool.wait_ge(filled, JOB[f"ht{NT - 1}"] + 1)
                for s in range(2):
                    for i in range(TILES):
                        pool.wait_ge(s_split, s * TILES + i + 1)
                        pool.tensor_tensor(h_tok[:, i, :], h_tok[:, i, :], h_split[:, s, i, :], ALU.subtract).then_inc(s_rest, 1)
                pool.wait_ge(empt_v, EV("logits"))
                pool.dma_start(g_fin, A["g_final"].rearrange("(a d) -> a d", a=1).to_broadcast([P, D])).then_inc(s_gfin, 16)
                pool.wait_ge(s_store, N_STORES)

            @block.scalar
            def _(act):
                rows = [("w_conf_dw", W_DW, KC), ("w_conv_a", W_CA, KA), ("b_conv_a", B_CA, 1), ("b_rg_a", B_RA, 1),
                        ("b_rg_x", B_RX, 1), ("rg_lambda", LAM, 1), ("b_conf_dw", B_DW, 1), ("g_conf_ln", G_LN, 1),
                        ("b_conf_ln", B_LN, 1), ("b_conf_pw", B_PW, 1)]
                for name, r, n in rows:
                    src = A[name][0] if n > 1 else A[name]
                    act.dma_start(par_rows[r:r + n, :], src).then_inc(s_par, 16)
                act.dma_start(sta_rows[0:SEQS * HA, :], flat(A["state_conv_a"][0])).then_inc(s_sta, 16)
                act.dma_start(sta_rows[SEQS * HA:SEQS * KA, :], A["state_h"][0]).then_inc(s_sta, 16)
                act.dma_start(stc_rows[0:SEQS * HC // 2],
                              flat(A["state_conf"][0]).rearrange("(h p) d -> p h d", h=2)).then_inc(s_stc, 16)
                act.dma_start(g_mix[:], A["g_mix"][0].rearrange("(p k) -> p k", k=NT)).then_inc(s_gain, 16)
                act.dma_start(g_ffn[:], A["g_ffn"][0].rearrange("(p k) -> p k", k=NT)).then_inc(s_gain, 16)
                act.dma_start(w_rt[:], A["w_router"][0].rearrange("(p k) e -> p k e", k=NT)).then_inc(s_rt, 16)
                act.dma_start(b_rt[:], A["b_router"].to_broadcast([P, E])).then_inc(s_rt, 16)

                def empty(name):
                    act.wait_ge(filled, JOB[name] + 1)
                    return bank(JOB[name])

                act.wait_ge(s_x, 32)
                for i in range(TILES):
                    if i:
                        act.wait_ge(s_sq, i)
                    act.activation(junk, acc[:, i, :], ACT.Square, accum_out=stat[:, i:i + 1]).then_inc(s_sq, 1)
                act.wait_ge(s_ms, 1)
                act.activation(stat[:, 6:9], stat[:, 3:6], ACT.Sqrt).then_inc(s_root, 1)
                for i in range(4):
                    z = empty(f"stc{i}")
                    for c in range(2):
                        dst = vx[:, 2 * i + c, HC + T_P:].rearrange("p (s t) -> p s t", s=SEQS)[:, :, 0:HC]
                        ins = act.copy(dst, z[:, c * SEQS * HC:(c + 1) * SEQS * HC].rearrange("p (s t) -> p s t", s=SEQS))
                    ins.then_inc(empt_a, 1)
                act.wait_ge(s_gain, 32)
                for k in range(0, NT, 2):
                    act.activation(hn[:, k, :], empty(f"hn{k}")[:, 0:T], ACT.Copy, scale=g_mix[:, k:k + 1]).then_inc(empt_a, 1)
                act.wait_ge(s_lam, 1)
                act.activation(lamw[:, 1, :], lamw[:, 0, :], ACT.Exp, scale=-1.0).then_inc(s_lexp, 1)
                for c in range(NT):
                    z = empty(f"va{c}")
                    act.copy(vx[:, c, HC:HC + T_P], z[:, 0:T_P])
                    act.copy(vx[:, c, HC + T_P:].rearrange("p (s t) -> p s t", s=SEQS)[:, :, HC:],
                             z[:, T_P:T].rearrange("p (s t) -> p s t", s=SEQS)).then_inc(empt_a, 1)
                    z = empty(f"vb{c}")
                    if c >= 2:
                        act.wait_ge(s_v, 2 * c - 2)
                    act.activation(sg[:, c % 2, :], z[:, 0:T], ACT.Sigmoid).then_inc(empt_a, 1)
                for c in range(NT):
                    z = empty(f"xa{c}")
                    act.copy(xa[:, c, HA:HA + T_P], z[:, 0:T_P])
                    act.copy(xa[:, c, HA + T_P:].rearrange("p (s t) -> p s t", s=SEQS)[:, :, HA:],
                             z[:, T_P:T].rearrange("p (s t) -> p s t", s=SEQS)).then_inc(empt_a, 1)
                for name, st, b, r in (("vp", st_v, 0, HC), ("vs", st_v, 1, T_S), ("xp", st_x, 0, HA),
                                       ("xs", st_x, 1, SEQS * HA)):
                    for h in range(2):
                        act.copy(st[0:r, b, h * 512:(h + 1) * 512], empty(f"{name}{h}")[0:r, :]).then_inc(empt_a, 1)
                for c in range(NT):
                    act.activation(gate_a[:, c, :], empty(f"ga{c}")[:, 0:T], ACT.Sigmoid).then_inc(empt_a, 1)
                act.wait_ge(s_conv, N_CONV)
                act.wait_ge(s_store, N_STORES - 32)
                for c in range(NT):
                    act.activation(rt[:, c, :], empty(f"r{c}")[:, 0:T], ACT.Sigmoid,
                                   bias=par[:, c, B_RA:B_RA + 1]).then_inc(empt_a, 1)
                    act.activation(ig[:, c, :], empty(f"i{c}")[:, 0:T], ACT.Sigmoid,
                                   bias=par[:, c, B_RX:B_RX + 1]).then_inc(empt_a, 1)
                for c in range(NT):
                    act.activation(gate_b[:, c, :], empty(f"gb{c}")[:, 0:T], ACT.Sigmoid).then_inc(empt_a, 1)
                act.wait_ge(empt_v, EV("mean"))
                for c in range(NT):
                    if c >= 2:
                        act.wait_ge(s_squ, c - 1)
                    act.activation(sg[:, c % 2, :], vc[:, c, :], ACT.Square).then_inc(s_sqv, 1)
                act.wait_ge(s_xc, N_XC)
                act.wait_ge(s_sp, 1)
                act.wait_ge(empt_a, EA(f"i{NT - 1}"))
                for c in range(NT):
                    act.activation(aa[:, c, :], rt[:, c, :], ACT.Exp, scale=lamw[:, 4, c:c + 1]).then_inc(ord_a, 1)
                for c in range(NT):
                    act.wait_ge(ord_a, NT)
                    act.activation(rt[:, c, :], rt[:, c, :], ACT.Tanh, scale=lamw[:, 5, c:c + 1]).then_inc(s_aw, 1)
                act.wait_ge(s_w, 1)
                act.activation(rt[:, :, :], rt[:, :, :], ACT.Sqrt).then_inc(s_rtt, 1)
                act.wait_ge(empt_v, EV("var"))
                act.activation(sg[:, 1, :], sg[:, 0, :], ACT.Sqrt).then_inc(s_root, 1)
                act.wait_ge(s_ln, 1)
                act.wait_ge(s_hs, 1)
                for c in range(NT):
                    act.activation(ig[:, c, :], vc[:, c, :], ACT.Sigmoid, scale=par[:, c, G_LN:G_LN + 1],
                                   bias=par[:, c, B_LN:B_LN + 1]).then_inc(s_sil, 1)
                for h in range(2):
                    act.copy(st_h[0:1 + SEQS, h * 512:(h + 1) * 512], empty(f"ho{h}")[0:1 + SEQS, :]).then_inc(empt_a, 1)

                act.wait_ge(empt_v, EV("out2"))
                act.wait_ge(s_store, N_STORES)
                for i in range(TILES):
                    act.activation(h_tok[:, i, :], acc[:, i, :], ACT.Square, accum_out=stat[:, 12 + i:13 + i]).then_inc(s_sq, 1)
                act.wait_ge(s_ms, 2)
                act.activation(stat[:, 18:21], stat[:, 15:18], ACT.Sqrt).then_inc(s_root, 1)
                for k in range(0, NT, 2):
                    act.activation(h_cm[:, k, :], empty(f"ht{k}")[:, 0:T_PAD], ACT.Copy,
                                   scale=g_ffn[:, k:k + 1]).then_inc(empt_a, 1)
                for i in range(TILES):
                    act.copy(h_split[:, 0, i, :], h_tok[:, i, :]).then_inc(s_split, 1)
                act.wait_ge(s_neg, 1)
                for i in range(TILES):
                    act.activation(comb[:, i, :], lg[:, i, 0:E], ACT.Exp, bias=stat[:, i:i + 1]).then_inc(s_exp, 1)
                for s in (1, 2):
                    for i in range(TILES):
                        act.wait_ge(s_rest, (s - 1) * TILES + i + 1)
                        act.copy(h_split[:, s, i, :], h_tok[:, i, :]).then_inc(s_split, 1)

                def turned(k, b):
                    act.wait_ge(s_htp, k + 1)
                    act.copy(hid_t[:, b, :, :], ps[:, BK_HT, :].rearrange("p (k s) -> p k s", k=NT)).then_inc(s_hts, 1)

                def sigmoid(k):
                    act.wait_ge(s_gc, k + 1)
                    if not (type(k) is int and k == 0):
                        act.wait_ge(s_hid, k)
                    act.activation(sig_e, g_e, ACT.Sigmoid, scale=ALPHA).then_inc(s_sig, 1)

                def selection(k, b):
                    act.wait_ge(s_stp, k + 1)
                    act.copy(sel_t[:, b, :], ps[:, BK_SEL, 0:T_PAD]).then_inc(s_sts, 1)

                def output(k, b, last_chunk):
                    act.wait_ge(used, last_chunk + 1)
                    act.copy(y_e[:, b, :], ps[:, BK_D, :]).then_inc(s_y, 1)

                sigmoid(0)
                selection(0, 0)
                turned(0, 0)
                sigmoid(1)
                output(0, 0, d_chunk(0, 1))
                with act.Fori(1, E // 2) as pair:
                    e = pair * 2
                    for b in range(2):
                        selection(e + (b - 1), 1 - b)
                        turned(e + (b - 1), 1 - b)
                        sigmoid(e + b)
                        output(e + (b - 1), 1 - b, d_chunk(e + (b - 1), 1))
                selection(E - 1, 1)
                turned(E - 1, 1)
                output(E - 1, 1, LAST_D + 1)

                def piece(e, n, r):
                    sigmoid(E + n)
                    selection(E + n, 0)
                    turned(E + n, 0)
                    output(E + n, 0, N_CHUNKS + 6 * n + 5)
                more_pieces(act, piece)

                act.wait_ge(s_sum, 1)
                for i in range(TILES):
                    act.activation(h_tok[:, i, :], acc[:, i, :], ACT.Square, accum_out=stat[:, i:i + 1]).then_inc(s_sq, 1)
                act.wait_ge(s_ms, 3)
                act.activation(stat[:, 6:9], stat[:, 3:6], ACT.Sqrt).then_inc(s_root, 1)

            @block.tensor
            def _(pe):
                def fill(name):
                    j = JOB[name]
                    if j >= 8:
                        if emptied_before(j - 8, "a"):
                            pe.wait_ge(empt_a, emptied_before(j - 8, "a"))
                        if emptied_before(j - 8, "v"):
                            pe.wait_ge(empt_v, emptied_before(j - 8, "v"))
                    return bank(j)

                def turn(dst, src):
                    k = src.shape[0]
                    return nc.tensor.transpose(dst, src, ident[0:k, 0:k])

                pe.wait_ge(s_const, 5)
                pe.wait_ge(s_par, 160)
                z = fill("par")
                for c in range(NT):
                    ins = turn(z[:, c * N_PAR:(c + 1) * N_PAR], par_rows[0:N_PAR, c * P:(c + 1) * P])
                ins.then_inc(filled, 1)
                pe.wait_ge(s_sta, 32)
                z = fill("sta")
                for c in range(NT):
                    ins = turn(z[:, c * 32:(c + 1) * 32], sta_rows[0:32, c * P:(c + 1) * P])
                ins.then_inc(filled, 1)
                pe.wait_ge(s_stc, 16)
                rows = SEQS * HC // 2
                for i in range(4):
                    z = fill(f"stc{i}")
                    for c in range(2):
                        for h in range(2):
                            src = stc_rows[0:rows, h, (2 * i + c) * P:(2 * i + c + 1) * P]
                            ins = turn(z[:, (2 * c + h) * rows:(2 * c + h + 1) * rows], src)
                    ins.then_inc(filled, 1)
                pe.wait_ge(s_xn, TILES)
                for k in range(NT):
                    z = fill(f"hn{k}")
                    for i in range(TILES):
                        n = min(P, T - i * P)
                        ins = turn(z[:, i * P:i * P + n], x_tok[0:n, i, k::NT])
                    ins.then_inc(filled, 1)

                def w_in_job(name, n, h, i):
                    w = slot_half(n, h).rearrange("p (k n) -> p k n", k=NT)
                    z = fill(name)
                    for k in range(NT):
                        ins = nc.tensor.matmul(z[:, 0:T], w[:, k, i * P:(i + 1) * P], hn[:, k, :],
                                               start=(k == 0), stop=(k == NT - 1))
                    ins.then_inc(filled, 1)

                pe.wait_ge(empt_a, EA("hn7"))
                pe.wait_ge(empt_v, EV("hn7"))
                for n in range(4):
                    pe.wait_ge(landed[n % SLOTS], 32 * (n // SLOTS + 1))
                    for i in range(2):
                        w_in_job(f"va{2 * n + i}", n, 0, i)
                        w_in_job(f"vb{2 * n + i}", n, 1, i)

                def w_in_block(name, n0):
                    for n in (n0, n0 + 1):
                        pe.wait_ge(landed[n % SLOTS], 32 * (n // SLOTS + 1))
                        for i in range(4):
                            w_in_job(f"{name}{4 * (n - n0) + i}", n, i // 2, i % 2)

                w_in_block("xa", 4)
                pe.wait_ge(s_v, 2 * NT)
                pe.wait_ge(s_new, 2)
                for name, r, src in (("vp", HC, lambda c: vx[:, c, T_P:T_P + HC]),
                                     ("vs", T_S, lambda c: v_new[:, c, :]),
                                     ("xp", HA, lambda c: xa[:, c, T_P:T_P + HA]),
                                     ("xs", SEQS * HA, lambda c: xa_new[:, c, :])):
                    for h in range(2):
                        z = fill(f"{name}{h}")
                        for c in range(4):
                            ins = turn(z[0:r, c * P:(c + 1) * P], src(4 * h + c))
                        ins.then_inc(filled, 1)
                w_in_block("ga", 6)
                pe.wait_ge(s_conv, N_CONV)
                z = fill("mean")
                for c in range(NT):
                    ins = nc.tensor.matmul(z[:, 0:T], ones[:], vc[:, c, :], start=(c == 0), stop=(c == NT - 1))
                ins.then_inc(filled, 1)
                pe.wait_ge(s_xc, N_XC)
                pe.wait_ge(s_wrg, 32)
                for c in range(NT):
                    for m, name in enumerate(("r", "i")):
                        z = fill(f"{name}{c}")
                        nc.tensor.matmul(z[:, 0:T], w_rg[:, m, c, :], xc[:, c, :], start=True, stop=True).then_inc(filled, 1)
                w_in_block("gb", 8)
                z = fill("var")
                for c in range(NT):
                    pe.wait_ge(s_sqv, c + 1)
                    ins = nc.tensor.matmul(z[:, 0:T], ones[:], sg[:, c % 2, :], start=(c == 0), stop=(c == NT - 1))
                    ins.then_inc(*((s_squ, 1) if c < NT - 1 else (filled, 1)))
                for n in (10, 11):
                    pe.wait_ge(landed[n % SLOTS], 32 * (n // SLOTS + 1))
                pe.wait_ge(s_s, NT)
                w4 = [slot_half(10 + k // 4, k % 4 // 2).rearrange("p (k n) -> p k n", k=2)[:, k % 2] for k in range(NT)]
                for c in range(NT):
                    z = fill(f"pw{c}")
                    for k in range(NT):
                        ins = nc.tensor.matmul(z[:, 0:T], w4[k][:, c * P:(c + 1) * P], vc[:, k, :],
                                               start=(k == 0), stop=(k == NT - 1))
                    ins.then_inc(filled, 1)
                pe.wait_ge(s_hs, 1)
                for h in range(2):
                    z = fill(f"ho{h}")
                    for c in range(4):
                        ins = turn(z[0:1 + SEQS, c * P:(c + 1) * P], xc[:, 4 * h + c, T_P - 1::STEPS])
                    ins.then_inc(filled, 1)
                for n in (12, 13):
                    pe.wait_ge(landed[n % SLOTS], 32 * (n // SLOTS + 1))
                w4 = [slot_half(12 + k // 4, k % 4 // 2).rearrange("p (k n) -> p k n", k=2)[:, k % 2] for k in range(NT)]
                pe.wait_ge(s_m, NT)
                for i in range(2):
                    for h in range(2):
                        z = fill(f"out{i}{h}")
                        for k in range(NT):
                            ins = nc.tensor.matmul(z[:, :], mt[:, k, i * P:(i + 1) * P], w4[k][:, h * 512:(h + 1) * 512],
                                                   start=(k == 0), stop=(k == NT - 1))
                        ins.then_inc(filled, 1)
                z = fill("out2")
                for k in range(NT):
                    for h in range(2):
                        ins = nc.tensor.matmul(z[h * T_S:(h + 1) * T_S, :], mt[:, k, 2 * P:T],
                                               w4[k][:, h * 512:(h + 1) * 512], start=(k == 0), stop=(k == NT - 1))
                ins.then_inc(filled, 1)
                pe.wait_ge(s_hn, TILES)
                for k in range(NT):
                    z = fill(f"ht{k}")
                    for i in range(TILES):
                        ins = turn(z[:, i * P:(i + 1) * P], h_tok[:, i, k::NT])
                    ins.then_inc(filled, 1)
                pe.wait_ge(s_rt, 32)
                pe.wait_ge(empt_a, EA("ht7"))
                pe.wait_ge(empt_v, EV("ht7"))
                z = fill("logits")
                for i in range(TILES):
                    for k in range(NT):
                        ins = nc.tensor.matmul(z[:, i * E:(i + 1) * E], h_cm[:, k, i * P:(i + 1) * P], w_rt[:, k, :],
                                               start=(k == 0), stop=(k == NT - 1))
                ins.then_inc(filled, 1)
                pe.wait_ge(s_mask, 1)
                z = fill("rank")
                for i in range(TILES + 1):
                    for j in range(min(i + 1, TILES)):
                        before = ones_h if j < i else tri
                        ins = nc.tensor.matmul(z[:, i * E:(i + 1) * E], before[:], mask_h[:, j, :],
                                               start=(j == 0), stop=(j == min(i, TILES - 1)))
                ins.then_inc(filled, 1)

                def gather(k, b):
                    pe.wait_ge(s_sel, k + 1)
                    if not (type(k) is int and k == 0):
                        pe.wait_ge(s_xe, k)
                    for t in range(NT):
                        n = 0
                        for s in range(3):
                            for i in range(TILES):
                                ins = nc.tensor.matmul(ps[:, BK_X, t * CAP:(t + 1) * CAP], h_split[:, s, i, t::NT],
                                                       sel[:, b, i, :], start=(n == 0), stop=(n == 3 * TILES - 1))
                                n += 1
                    ins.then_inc(s_xg, 1)

                def gate_up(k, b, slots, fills, spread=None):
                    pe.wait_ge(s_xe, k + 1)
                    pe.wait_ge(s_pick, k + 1)
                    if not (type(k) is int and k == 0):
                        pe.wait_ge(s_gc, k)
                        pe.wait_ge(s_uc, k)
                    for h in range(2):
                        for m in range(2):
                            nc.tensor.matmul(ps[m * CAP:(m + 1) * CAP, BK_GU + h, :], pick[:, b, m, :],
                                             bias[:, h * 512:(h + 1) * 512], start=True, stop=False)
                    for t in range(NT):
                        q = t // 2
                        if t % 2 == 0:
                            pe.wait_ge(landed[slots[q]], fills[q])
                        w = ring[:, slots[q], :].rearrange("p (m k n) -> p m k n", m=2, k=2)
                        for h in range(2):
                            for m in range(2):
                                ins = nc.tensor.matmul(ps[m * CAP:(m + 1) * CAP, BK_GU + h, :], x_e[:, b, t, :],
                                                       w[:, m, t % 2, h * 512:(h + 1) * 512],
                                                       start=False, stop=(t == NT - 1))
                        if t % 2:
                            ins.then_inc(used, 1)
                            if spread is not None and q < TILES:
                                spread(q)

                def turn_both(k, b):
                    pe.wait_ge(s_selw, k + 1)
                    pe.wait_ge(s_hid, k + 1)
                    if not (type(k) is int and k == 0):
                        pe.wait_ge(s_sts, k)
                        pe.wait_ge(s_hts, k)
                    for i in range(TILES):
                        ins = turn(ps[:, BK_SEL, i * P:(i + 1) * P], sel_w[:, b, i].rearrange("p d s -> p (d s)"))
                    ins.then_inc(s_stp, 1)
                    for t in range(NT):
                        ins = turn(ps[:, BK_HT, t * CAP:(t + 1) * CAP], hid[:, t::NT])
                    ins.then_inc(s_htp, 1)

                def down(k, b, slots, fills):
                    pe.wait_ge(s_hts, k + 1)
                    pe.wait_ge(s_pickd, k + 1)
                    if not (type(k) is int and k == 0):
                        pe.wait_ge(s_y, k)
                    for h in range(2):
                        nc.tensor.matmul(ps[h * CAP:(h + 1) * CAP, BK_D, :], pick[:, b, 2, :],
                                         bias[:, h * 512:(h + 1) * 512], start=True, stop=False)
                    for t in range(NT):
                        q = t // 4
                        if t % 4 == 0:
                            pe.wait_ge(landed[slots[q]], fills[q])
                        w = ring[:, slots[q], :].rearrange("p (k n) -> p k n", k=4)
                        for h in range(2):
                            ins = nc.tensor.matmul(ps[h * CAP:(h + 1) * CAP, BK_D, :], hid_t[:, b, t, :],
                                                   w[:, t % 4, h * 512:(h + 1) * 512], start=False, stop=(t == NT - 1))
                        if t % 4 == 3:
                            ins.then_inc(used, 1)

                def spread_tile(k, b, i):
                    if i == 0:
                        pe.wait_ge(s_y, k + 1)
                        pe.wait_ge(s_sts, k + 1)
                    if not (type(k) is int and k == 0 and i == 0):
                        pe.wait_ge(s_add, TILES * k + i)
                    for h in range(2):
                        ins = nc.tensor.matmul(ps[:, BK_OUT + h, :], sel_t[h * CAP:(h + 1) * CAP, b, i * P:(i + 1) * P],
                                               y_e[h * CAP:(h + 1) * CAP, b, :], start=True, stop=True)
                    ins.then_inc(s_sc, 1)

                def slots_from(m0, n):
                    return [slot_of(m0 + q) for q in range(n)]

                def fills_from(m0, n, e=0):
                    return [landed_by(m0 + q, e) for q in range(n)]

                pe.wait_ge(empt_v, EV("rank"))
                pe.wait_ge(empt_a, EA("ht7"))
                pe.wait_ge(s_split, 3 * TILES)
                pe.wait_ge(s_bias, 48)
                gather(0, 0)
                gate_up(0, 0, slots_from(0, 4), fills_from(0, 4))
                gather(1, 1)
                gate_up(1, 1, slots_from(4, 4), fills_from(4, 4))
                turn_both(0, 0)
                gather(2, 0)
                down(0, 0, slots_from(8, 2), fills_from(8, 2))

                def expert(e, b, since, spread=True, last=False):
                    gate_up(e, b, slots_from(gu_chunk(2, 0), 4), fills_from(gu_chunk(2, 0), 4, since),
                            lambda i: spread_tile(e - 2, b, i))
                    turn_both(e - 1, 1 - b)
                    if not last:
                        gather(e + 1, 1 - b)
                    down(e - 1, 1 - b, slots_from(d_chunk(1, 0), 2), fills_from(d_chunk(1, 0), 2, since))

                with pe.Fori(1, E // 2 - 1) as pair:
                    e = pair * 2
                    for b in range(2):
                        expert(e + b, b, e + (b - 2))
                expert(E - 2, 0, E - 4)
                expert(E - 1, 1, E - 3, last=True)
                for i in range(TILES):
                    spread_tile(E - 2, 0, i)
                turn_both(E - 1, 1)
                down(E - 1, 1, slots_from(LAST_D, 2), fills_from(LAST_D, 2))
                for i in range(TILES):
                    spread_tile(E - 1, 1, i)

                def piece(e, n, r):
                    k = E + n
                    gather(k, 0)
                    gate_up(k, 0, slots_from(N_CHUNKS, 4), fills_from(N_CHUNKS, 4, n))
                    turn_both(k, 0)
                    down(k, 0, slots_from(N_CHUNKS + 4, 2), fills_from(N_CHUNKS + 4, 2, n))
                    for i in range(TILES):
                        spread_tile(k, 0, i)
                more_pieces(pe, piece)

            @block.vector
            def _(dve):
                steps = [0]

                def link(ins):
                    steps[0] += 1
                    ins.then_inc(ord_v, 1)
                    dve.wait_ge(ord_v, steps[0])

                def full(name):
                    dve.wait_ge(filled, JOB[name] + 1)
                    return bank(JOB[name])

                V = nc.vector
                V.memset(acc[:, 2, :], 0.0).then_inc(s_zero, 1)
                V.memset(xa[:, :, 0:HA], 0.0)
                V.memset(vx[:, :, 0:HC], 0.0)
                V.memset(lg[:, :, E:], -3.0e38)

                def roots(n, sums, means, root, inv):
                    dve.wait_ge(s_sq, TILES * n)
                    V.tensor_scalar(stat[:, means:means + 3], stat[:, sums:sums + 3], 1.0 / D, EPS, ALU.mult,
                                    ALU.add).then_inc(s_ms, 1)
                    dve.wait_ge(s_root, n if n == 1 else n + 1)
                    link(V.reciprocal(stat[:, inv:inv + 3], stat[:, root:root + 3]))

                roots(1, 0, 3, 6, 9)
                for i in range(TILES):
                    V.tensor_scalar(x_tok[:, i, :], acc[:, i, :], stat[:, 9 + i:10 + i], None, ALU.mult).then_inc(s_xn, 1)
                V.tensor_copy(par[:].rearrange("p c n -> p (c n)"), full("par")[:, 0:NT * N_PAR]).then_inc(empt_v, 1)
                z = full("sta")[:, 0:NT * 32].rearrange("p (c r) -> p c r", c=NT)
                V.tensor_copy(xa[:, :, HA + T_P:].rearrange("p c (s t) -> p c s t", s=SEQS)[:, :, :, 0:HA],
                              z[:, :, 0:SEQS * HA].rearrange("p c (s t) -> p c s t", s=SEQS))
                V.tensor_copy(h0[:], z[:, :, SEQS * HA:]).then_inc(empt_v, 1)
                dve.wait_ge(s_gain, 32)
                for k in range(1, NT, 2):
                    V.tensor_scalar(hn[:, k, :], full(f"hn{k}")[:, 0:T], g_mix[:, k:k + 1], None, ALU.mult).then_inc(empt_v, 1)
                dve.wait_ge(empt_v, EV("par"))
                lam = par[:, :, LAM]
                V.scalar_tensor_tensor(lamw[:, 0, :], lam, -1.0, lam, ALU.mult, ALU.max).then_inc(s_lam, 1)
                dve.wait_ge(s_lexp, 1)
                link(V.tensor_scalar(lamw[:, 2, :], lamw[:, 1, :], 2.0, None, ALU.add))
                link(V.reciprocal(lamw[:, 3, :], lamw[:, 2, :]))
                link(V.tensor_tensor(lamw[:, 2, :], lamw[:, 1, :], lamw[:, 3, :], ALU.mult))
                link(V.tensor_tensor(lamw[:, 3, :], lamw[:, 2, :], lamw[:, 2, :], ALU.mult))
                link(V.tensor_scalar(lamw[:, 0, :], lamw[:, 3, :], 1.0 / 17, None, ALU.mult))
                for n in (15, 13, 11, 9, 7, 5, 3):
                    link(V.scalar_tensor_tensor(lamw[:, 0, :], lamw[:, 0, :], 1.0 / n, lamw[:, 3, :], ALU.add, ALU.mult))
                link(V.scalar_tensor_tensor(lamw[:, 0, :], lamw[:, 0, :], 1.0, lamw[:, 2, :], ALU.add, ALU.mult))
                link(V.tensor_scalar(lamw[:, 1, :], lam, -1.0, 0.0, ALU.mult, ALU.max))
                link(V.scalar_tensor_tensor(lamw[:, 2, :], lamw[:, 0, :], 2.0, lamw[:, 1, :], ALU.mult, ALU.add))
                V.tensor_scalar(lamw[:, 4, :], lamw[:, 2, :], -RG_C, None, ALU.mult)
                V.tensor_scalar(lamw[:, 5, :], lamw[:, 2, :], RG_C / 2, None, ALU.mult).then_inc(s_sp, 1)

                def convolve(c, taps, hist, src, dst, w_row, b_row, done):
                    s4 = src[:, :, hist + T_P:].rearrange("p c (s t) -> p c s t", s=SEQS)
                    d4 = dst[:, :, T_P:].rearrange("p c (s t) -> p c s t", s=SEQS)
                    base = c * (2 * taps)
                    for j in range(taps):
                        for n in range(4):
                            cc = c + n % 2
                            w = par[:, cc, w_row + j:w_row + j + 1]
                            if n < 2:
                                x, y = src[:, cc, j:j + T_P], dst[:, cc, 0:T_P]
                            else:
                                x, y = s4[:, cc, :, j:j + STEPS], d4[:, cc]
                            if j == 0:
                                V.tensor_scalar(y, x, w, par[:, cc, b_row:b_row + 1], ALU.mult, ALU.add).then_inc(done, 1)
                            else:
                                dve.wait_ge(done, base + (4 * (j - 1) + n + 1))
                                V.scalar_tensor_tensor(y, x, w, y, ALU.mult, ALU.add).then_inc(done, 1)

                dve.wait_ge(empt_a, EA("stc3"))
                with dve.Fori(0, NT // 2) as half:
                    c = half * 2
                    dve.wait_ge(s_v, c * 2 + 4)
                    convolve(c, KC, HC, vx, vc, W_DW, B_DW, s_conv)
                with dve.Fori(0, NT // 2) as half:
                    c = half * 2
                    dve.wait_ge(empt_a, c + (EA("xa0") + 1))
                    convolve(c, KA, HA, xa, xc, W_CA, B_CA, s_xc)
                dve.wait_ge(s_conv, N_CONV)
                mean = full("mean")[:, 0:T].unsqueeze(1).to_broadcast([P, NT, T])
                V.tensor_tensor(vc[:, :, :], vc[:, :, :], mean, ALU.subtract).then_inc(empt_v, 1)
                dve.wait_ge(empt_a, EA("i7"))
                dve.wait_ge(s_xc, N_XC)
                link(V.tensor_tensor(ig[:, :, :], ig[:, :, :], xc[:, :, :], ALU.mult))
                dve.wait_ge(s_aw, NT)
                link(V.scalar_tensor_tensor(ig[:, :, :], aa[:, :, :], 1.0, ig[:, :, :], ALU.add, ALU.mult))
                V.scalar_tensor_tensor(xc[:, :, :], aa[:, :, :], 1.0, rt[:, :, :], ALU.add, ALU.mult).then_inc(s_w, 1)
                V.tensor_scalar(sg[:, 0, :], full("var")[:, 0:T], EPS, None, ALU.add).then_inc(empt_v, 1)
                dve.wait_ge(s_w, 1)
                link(V.tensor_scalar(aa[:, :, :], xc[:, :, :], -1.0, 1.0, ALU.mult, ALU.add))
                dve.wait_ge(s_rtt, 1)
                link(V.tensor_tensor(ig[:, :, :], ig[:, :, :], rt[:, :, :], ALU.mult))
                first = slice(T_P, T, STEPS)
                link(V.tensor_tensor(h0[:], h0[:], aa[:, :, first], ALU.mult))
                link(V.tensor_tensor(ig[:, :, first], ig[:, :, first], h0[:], ALU.add))
                V.memset(aa[:, :, first], 0.0)
                link(V.memset(aa[:, :, 0:1], 0.0))
                V.tensor_tensor_scan(xc_w, xa_w[:, 0:TW], ig_w, 0.0, ALU.mult, ALU.add).then_inc(s_hs, 1)
                dve.wait_ge(s_root, 2)
                link(V.reciprocal(sg[:, 0, :], sg[:, 1, :]))
                inv = sg[:, 0, :].unsqueeze(1).to_broadcast([P, NT, T])
                V.tensor_tensor(vc[:, :, :], vc[:, :, :], inv, ALU.mult).then_inc(s_ln, 1)
                dve.wait_ge(s_hs, 1)
                link(V.tensor_tensor(gate_a[:, :, :], gate_a[:, :, :], xc[:, :, :], ALU.mult))
                for c in range(NT):
                    dve.wait_ge(s_sil, c + 1)
                    link(V.tensor_scalar(vc[:, c, :], vc[:, c, :], par[:, c, G_LN:G_LN + 1], par[:, c, B_LN:B_LN + 1],
                                         ALU.mult, ALU.add))
                    V.tensor_tensor(vc[:, c, :], vc[:, c, :], ig[:, c, :], ALU.mult).then_inc(s_s, 1)
                for c in range(NT):
                    V.scalar_tensor_tensor(mt[:, c, :], full(f"pw{c}")[:, 0:T], par[:, c, B_PW:B_PW + 1], gate_b[:, c, :],
                                           ALU.add, ALU.mult).then_inc(empt_v, 1)
                    dve.wait_ge(empt_v, EV(f"pw{c}"))
                    V.tensor_tensor(mt[:, c, :], mt[:, c, :], gate_a[:, c, :], ALU.add).then_inc(s_m, 1)
                V.memset(bias[3 * E:, :], 0.0).then_inc(s_m, 1)
                for i in range(2):
                    for h in range(2):
                        a = acc[:, i, h * 512:(h + 1) * 512]
                        V.tensor_tensor(a, full(f"out{i}{h}"), a, ALU.add).then_inc(empt_v, 1)
                z = full("out2")
                for h in range(2):
                    a = acc[0:T_S, 2, h * 512:(h + 1) * 512]
                    ins = V.tensor_tensor(a, z[h * T_S:(h + 1) * T_S, :], a, ALU.add)
                ins.then_inc(empt_v, 1)
                roots(2, 12, 15, 18, 21)
                for i in range(TILES):
                    V.tensor_scalar(h_tok[:, i, :], acc[:, i, :], stat[:, 21 + i:22 + i], None, ALU.mult).then_inc(s_hn, 1)
                for k in range(1, NT, 2):
                    V.tensor_scalar(h_cm[:, k, :], full(f"ht{k}")[:, 0:T_PAD], g_ffn[:, k:k + 1], None, ALU.mult).then_inc(empt_v, 1)
                dve.wait_ge(s_rt, 32)
                z = full("logits")[:, 0:TILES * E].rearrange("p (i e) -> p i e", i=TILES)
                V.tensor_tensor(lg[:, :, 0:E], z, b_rt[:].unsqueeze(1).to_broadcast([P, TILES, E]), ALU.add).then_inc(empt_v, 1)
                dve.wait_ge(empt_v, EV("logits"))
                for i in range(TILES):
                    ins = V.max(top[:, i, :], lg[:, i, :])
                link(ins)
                V.tensor_scalar(stat[:, 0:3], top[:, :, 0], -1.0, None, ALU.mult).then_inc(s_neg, 1)
                link(V.memset(top[:, :, 4:8], -3.0e38))
                for i in range(TILES):
                    ins = V.match_replace(lgr[:, i, :], top[:, i, :], lg[:, i, :], 3.0e38)
                link(ins)
                link(V.tensor_scalar(mask[:, :, :], lgr[:, :, 0:E], 3.0e38, None, ALU.is_equal))
                V.memset(mask[T_S:2 * T_S, 2, :], 0.0)
                link(V.memset(mask[2 * T_S:, 2, :], 0.0))
                V.tensor_copy(mask_h[:, :, :], mask[:, :, :]).then_inc(s_mask, 1)
                dve.wait_ge(s_exp, TILES)
                link(V.tensor_tensor(comb[:, :, :], comb[:, :, :], mask[:, :, :], ALU.mult))
                link(V.tensor_reduce(stat[:, 12:15], comb[:, :, :], AX_X, ALU.add))
                link(V.tensor_scalar(stat[:, 12:15], stat[:, 12:15], 1.0e-30, None, ALU.max))
                link(V.reciprocal(stat[:, 15:18], stat[:, 12:15]))
                for i in range(TILES):
                    ins = V.tensor_scalar(comb[:, i, :], comb[:, i, :], stat[:, 15 + i:16 + i], None, ALU.mult)
                link(ins)
                z = full("rank")
                zr = z[:, 0:TILES * E].rearrange("p (i e) -> p i e", i=TILES)
                link(V.scalar_tensor_tensor(rank[:, :, :], zr, 1.0, mask[:, :, :], ALU.add, ALU.mult))
                link(V.tensor_scalar(rank[:, :, :], rank[:, :, :], -1.0, None, ALU.add))
                link(V.tensor_copy(cntf[:, 0:E], z[:, TILES * E:(TILES + 1) * E]))
                link(V.tensor_reduce(cntf[:, E:E + 1], cntf[:, 0:E], AX_X, ALU.max))
                V.tensor_copy(counts[:, :], cntf[:, :]).then_inc(s_cnt, 1)
                V.tensor_copy(rnk2[:, :, :], rank[:, :, :]).then_inc(empt_v, 1)
                dve.wait_ge(empt_v, EV("rank"))

                picks = ident[:, :].rearrange("p (m e) -> p m e", e=E)

                def select(e, b, ranks):
                    for i in range(TILES):
                        ins = V.tensor_scalar(sel[:, b, i, :], slot_no[:, 0, :], ranks[:, i, bass.ds(e, 1)], None, ALU.is_equal)
                    ins.then_inc(s_sel, 1)
                    for m in range(2):
                        ins = V.tensor_copy(pick[:, b, m, :], picks[:, m, bass.ds(e, 1)].to_broadcast([P, CAP]))
                    ins.then_inc(s_pick, 1)

                def select_weighted(e, b, ranks):
                    for i in range(TILES):
                        ins = V.tensor_scalar(sel_w[:, b, i, :, :], slot_no[:, :, :], ranks[:, i, bass.ds(e, 1)],
                                              comb[:, i, bass.ds(e, 1)], ALU.is_equal, ALU.mult)
                    ins.then_inc(s_selw, 1)
                    V.tensor_copy(pick[:, b, 2, :], picks[:, 2, bass.ds(e, 1)].to_broadcast([P, CAP])).then_inc(s_pickd, 1)

                gains = g_ffn[:, :].unsqueeze(2).to_broadcast([P, NT, CAP])

                def take_inputs(k, b):
                    dve.wait_ge(s_xg, k + 1)
                    z = ps[:, BK_X, :].rearrange("p (k s) -> p k s", k=NT)
                    V.tensor_tensor(x_e[:, b, :, :], z, gains, ALU.mult).then_inc(s_xe, 1)

                gate_ps = ps[0:CAP, BK_GU:BK_GU + 2, :].rearrange("p h n -> p (h n)")
                up_ps = ps[CAP:2 * CAP, BK_GU:BK_GU + 2, :].rearrange("p h n -> p (h n)")

                def clamp_gate(k, last_chunk):
                    dve.wait_ge(used, last_chunk + 1)
                    if not (type(k) is int and k == 0):
                        dve.wait_ge(s_hid, k)
                    V.tensor_scalar(g_e, gate_ps, LIMIT, None, ALU.min).then_inc(s_gc, 1)

                def clamp_up(k):
                    V.tensor_scalar(u_e, up_ps, LIMIT, -LIMIT, ALU.min, ALU.max).then_inc(s_uc, 1)

                def hidden(k):
                    dve.wait_ge(s_uc, k + 1)
                    dve.wait_ge(s_gc, k + 1)
                    if not (type(k) is int and k == 0):
                        dve.wait_ge(s_htp, k)
                    V.scalar_tensor_tensor(hid, u_e, 1.0, g_e, ALU.add, ALU.mult).then_inc(s_prod, 1)
                    dve.wait_ge(s_prod, k + 1)
                    dve.wait_ge(s_sig, k + 1)
                    V.tensor_tensor(hid, hid, sig_e, ALU.mult).then_inc(s_hid, 1)

                def add_output(k):
                    for i in range(TILES):
                        dve.wait_ge(s_sc, TILES * k + (i + 1))
                        if not (type(k) is int and k == 0):
                            dve.wait_ge(s_add, TILES * k + (i - TILES + 1))
                        V.tensor_tensor(acc[:, i, :], ps[:, BK_OUT:BK_OUT + 2, :].rearrange("p h n -> p (h n)"),
                                        acc[:, i, :], ALU.add).then_inc(s_add, 1)

                select(0, 0, rank)
                select(1, 1, rank)
                take_inputs(0, 0)
                clamp_gate(0, 3)
                take_inputs(1, 1)
                clamp_up(0)
                hidden(0)
                select(2, 0, rank)
                select_weighted(0, 0, rank)

                def expert(e, b, inputs=True, selection=True):
                    clamp_gate(e, gu_chunk(e, 3))
                    if inputs:
                        take_inputs(e + 1, 1 - b)
                    clamp_up(e)
                    hidden(e)
                    add_output(e - 1)
                    if selection:
                        select(e + 2, b, rank)
                    select_weighted(e, b, rank)

                expert(1, 1)
                with dve.Fori(1, E // 2 - 1) as pair:
                    e = pair * 2
                    for b in range(2):
                        expert(e + b, b)
                expert(E - 2, 0, selection=False)
                expert(E - 1, 1, inputs=False, selection=False)
                add_output(E - 1)

                def next_ranks(r):
                    dve.wait_ge(s_cnt, r)
                    V.tensor_scalar(rnk2[:, :, :], rnk2[:, :, :], -float(CAP), None, ALU.add).then_inc(s_cnt, 1)

                def piece(e, n, r):
                    k = E + n
                    dve.wait_ge(s_cnt, r + 1)
                    select(e, 0, rnk2)
                    take_inputs(k, 0)
                    clamp_gate(k, N_CHUNKS + 6 * n + 3)
                    clamp_up(k)
                    hidden(k)
                    select_weighted(e, 0, rnk2)
                    add_output(k)
                more_pieces(dve, piece, next_ranks)

                V.memset(stat[:, 12:13], 0.0).then_inc(s_sum, 1)
                roots(3, 0, 3, 6, 9)
                dve.wait_ge(s_gfin, 16)
                for i in range(TILES):
                    V.scalar_tensor_tensor(h_tok[:, i, :], acc[:, i, :], stat[:, 9 + i:10 + i], g_fin, ALU.mult,
                                           ALU.mult).then_inc(s_fin, 1)


_INS = ["x_prompt", "x_sample", "state_conv_a", "state_h", "state_conf", "g_mix", "w_in", "w_conv_a", "b_conv_a",
        "w_rg_a", "b_rg_a", "w_rg_x", "b_rg_x", "rg_lambda", "w_conf_dw", "b_conf_dw", "g_conf_ln", "b_conf_ln",
        "w_conf_pw", "b_conf_pw", "w_out", "g_ffn", "w_router", "b_router", "w_gate", "b_gate", "w_up", "b_up",
        "w_down", "b_down", "g_final"]
_OUTS = [(1, T_P, D), (SEQS, STEPS, D), (1, 1, HA, D), (1, 1, D), (1, 1, HC, D), (1, SEQS, HA, D), (1, SEQS, D),
         (1, SEQS, HC, D)]


def kernel(**inputs):
    import concourse.bacc as bacc
    from concourse.bass_utils import run_bass_kernel_spmd

    nc = bacc.Bacc("TRN2", target_bir_lowering=False, num_devices=1)
    arrays, given = {}, {}
    for name in _INS:
        a = np.ascontiguousarray(inputs[name])
        arrays[f"in_{name}"] = a
        given[name] = nc.dram_tensor(f"in_{name}", a.shape, mybir.dt.from_np(a.dtype), kind="ExternalInput").ap()
    outs = [nc.dram_tensor(f"out_{i}", shape, F32, kind="ExternalOutput").ap() for i, shape in enumerate(_OUTS)]
    build(nc, given, outs)
    r = run_bass_kernel_spmd(nc, [arrays], core_ids=[0])
    return tuple(r.results[0][f"out_{i}"] for i in range(len(_OUTS)))
```

```python
from contextlib import ExitStack

import numpy as np

import concourse.bass as bass
from concourse import mybir
from concourse.alu_op_type import AluOpType as ALU

ACT = mybir.ActivationFunctionType
F32 = mybir.dt.float32
BF16 = mybir.dt.bfloat16
I32 = mybir.dt.int32
AX_X = mybir.AxisListType.X

P = 128
D = 1024
NT = D // P
T_P = 256
SEQS, STEPS = 8, 4
T_S = SEQS * STEPS
T = T_P + T_S
TILES = 3
T_PAD = TILES * P
KA, KC = 4, 31
HA, HC = KA - 1, KC - 1
E = 32
CAP = 64
EPS = 1e-6
RG_C = 8.0
LIMIT, ALPHA = 7.0, 1.702

W_DW, W_CA, B_CA, B_RA, B_RX, LAM, B_DW, G_LN, B_LN, B_PW = 0, 31, 35, 36, 37, 38, 39, 40, 41, 42
N_PAR = 43

SLOTS = 6
SLOT = 4096
MIX_CHUNKS = 14

TILE_ORDER = (2, 0, 1)

BK_GU, BK_D, BK_X, BK_SEL, BK_HT, BK_OUT = 0, 2, 3, 4, 5, 6
OUT_BANKS = (BK_OUT, BK_GU, BK_SEL)


def mixer_jobs():
    jobs = [("par", "v"), ("sta", "v")]
    jobs += [(f"hn{k}", "av"[k % 2]) for k in range(NT)]
    for c in range(NT):
        jobs += [(f"va{c}", "a"), (f"vb{c}", "a")]
        if c == 0:
            jobs += [(f"stc{i}", "a") for i in range(4)]
    jobs += [(f"xa{c}", "a") for c in range(NT)]
    jobs += [(f"{n}{h}", "a") for n in ("vp", "vs", "xp", "xs") for h in range(2)]
    jobs += [(f"ga{c}", "a") for c in range(NT)]
    jobs += [("mean", "v")]
    jobs += [(f"gb{c}", "a") for c in range(4)]
    jobs += [("var", "v")]
    jobs += [(f"gb{c}", "a") for c in (4, 5)]
    for c in range(NT):
        jobs += [(f"r{c}", "a"), (f"i{c}", "a")]
    jobs += [(f"gb{c}", "a") for c in (6, 7)]
    jobs += [(f"pw{c}", "v") for c in range(NT)]
    jobs += [(f"ho{h}", "a") for h in range(2)]
    jobs += [(n, "v") for n in ("out2", "out00", "out01", "ht2a", "ht2b", "out10", "ht0a", "ht0b", "logits2", "out11",
                                "logits0", "ht1a", "ht1b", "logits1", "rank")]
    return jobs


JOBS = mixer_jobs()
JOB = {name: j for j, (name, _) in enumerate(JOBS)}


def emptied_before(j, who):
    return sum(w == who for _, w in JOBS[:j + 1])


def build(nc, A, O):
    with ExitStack() as ctx:
        def sb(name, shape, dt=F32):
            return ctx.enter_context(nc.sbuf_tensor(name, shape, dt))

        def sem(name):
            return ctx.enter_context(nc.semaphore(name))

        ring = sb("ring", [P, SLOTS, SLOT])
        acc = sb("acc", [P, TILES, D])
        par = sb("par", [P, NT, N_PAR])
        w_rg = sb("w_rg", [P, 2, NT, P])
        w_rt = sb("w_rt", [P, NT, E])
        b_rt = sb("b_rt", [P, E])
        g_mix = sb("g_mix_c", [P, NT])
        g_ffn = sb("g_ffn_c", [P, NT])
        ident = sb("ident", [P, P])
        ones = sb("ones", [P, P])
        slot_no = sb("slot_no", [P, 2, CAP])
        tri = sb("tri", [P, P], BF16)
        ones_h = sb("ones_h", [P, P], BF16)
        h0 = sb("h0", [P, NT, SEQS])
        stat = sb("stat", [P, 8 * TILES])
        lamw = sb("lamw", [P, 6, NT])
        lg = sb("lg", [P, TILES, E + 4])
        lgr = sb("lgr", [P, TILES, E + 4])
        top = sb("top", [P, TILES, 8])
        mask = sb("mask", [P, TILES, E])
        mask_h = sb("mask_h", [P, TILES, E], BF16)
        comb = sb("comb", [P, TILES, E])
        rank = sb("rank", [P, TILES, E])
        rnk2 = sb("rnk2", [P, TILES, E])
        counts = sb("counts", [P, E + 1], I32)
        cntf = sb("cntf", [P, E + 1])

        WS = 21400
        ws = sb("ws", [P, WS])
        at = [0]

        def take(words):
            at[0] += words
            assert at[0] <= WS, at
            return ws[:, at[0] - words:at[0]]

        TW = NT * T
        XA_W, VX_W = HA + T_P + SEQS * (HA + STEPS), HC + T_P + SEQS * (HC + STEPS)
        hn_w = take(TW)
        xa_w = take(NT * XA_W)
        vx_w = take(NT * VX_W)
        ga_w = take(2 * TW)
        vc_w = take(TW)
        xc_w = take(TW)
        ig_w = take(TW)
        sg_w = take(2 * T)

        def by_tile(w, n=T):
            return w[:, 0:NT * n].rearrange("p (c t) -> p c t", c=NT)

        hn = by_tile(hn_w)
        xa = by_tile(xa_w, XA_W)
        vx = by_tile(vx_w, VX_W)
        gate_a = by_tile(ga_w[:, 0:TW])
        gate_b = by_tile(ga_w[:, TW:2 * TW])
        vc = by_tile(vc_w)
        xc = by_tile(xc_w)
        ig = by_tile(ig_w)
        sg = sg_w.rearrange("p (b t) -> p b t", b=2)
        rt = by_tile(vx_w)
        aa = by_tile(xa_w)
        mt = by_tile(ig_w)
        taps_s = xc_w[:, 0:2 * T_S * KC].rearrange("p (b s t j) -> p b s t j", b=2, s=SEQS, t=STEPS)
        x_tok = ga_w[:, 0:TILES * D].rearrange("p (i d) -> p i d", i=TILES)
        junk = vc_w[:, 0:D]
        par_rows = xc_w[:, 0:D]
        sta_rows = xc_w[:, D:2 * D]
        stc_rows = ig_w[:, 0:2 * D].rearrange("p (h d) -> p h d", h=2)
        st_v = ga_w[:, TW:TW + 2 * D].rearrange("p (b d) -> p b d", b=2)
        st_x = ig_w[:, 0:2 * D].rearrange("p (b d) -> p b d", b=2)
        v_new = ig_w[:, 2 * D:2 * D + NT * T_S].rearrange("p (c t) -> p c t", c=NT)
        xa_new = ga_w[:, TW + 2 * D:TW + 2 * D + NT * SEQS * HA].rearrange("p (c t) -> p c t", c=NT)
        silu = [vx_w[:, TW + c * T:TW + (c + 1) * T] for c in range(NT - 1)] + [sg_w[:, T:2 * T]]
        st_h = vx_w[:, TW:TW + D]

        at[0] = 0
        h_tok = take(TILES * D).rearrange("p (i d) -> p i d", i=TILES)
        h_cm_w = take(NT * T_PAD)
        h_cm = h_cm_w.rearrange("p (k t) -> p k t", k=NT)
        spare = ws[:, 0:SLOT]
        g_fin = ws[:, SLOT:SLOT + D]
        h_split = take(3 * TILES * D // 2).bitcast(BF16).rearrange("p (s i d) -> p s i d", s=3, i=TILES)
        x_e = take(2 * NT * CAP).rearrange("p (b k s) -> p b k s", b=2, k=NT)
        hid_t = take(2 * NT * CAP).rearrange("p (b k s) -> p b k s", b=2, k=NT)
        y_e = take(2 * D // 2).rearrange("p (b n) -> p b n", b=2)
        g_e = take(D)[0:CAP]
        sig_e = take(D)[0:CAP]
        u_e = take(D)[0:CAP]
        hid = take(D)[0:CAP]
        sel = take(2 * TILES * CAP // 2).bitcast(BF16).rearrange("p (b i s) -> p b i s", b=2, i=TILES)
        sel_w = take(2 * TILES * 2 * CAP).rearrange("p (b i d s) -> p b i d s", b=2, i=TILES, d=2)
        sel_t = take(2 * T_PAD).rearrange("p (b t) -> p b t", b=2)
        pick = take(2 * 3 * CAP).rearrange("p (b m s) -> p b m s", b=2, m=3)
        at[0] = max(at[0], WS - 2 * T - D)
        bias = take(D)
        ps = ctx.enter_context(nc.psum_tensor("ps", [P, 8, 512], F32))

        def bank(j):
            return ps[:, j % 8, :]

        s_x = [sem(f"x{i}_loaded") for i in range(TILES)]
        s_par = sem("params_loaded")
        s_sta = sem("conv_a_and_h_state_loaded")
        s_stc = sem("conf_state_loaded")
        s_gain = sem("gains_loaded")
        s_rt = sem("router_loaded")
        s_bias = sem("bias_loaded")
        s_bz = sem("rows_without_bias_cleared")
        s_gfin = sem("g_final_loaded")
        s_spare = sem("early_chunk_loaded")
        s_wrg = sem("gate_blocks_loaded")
        landed = [sem(f"slot{s}_landed") for s in range(SLOTS)]
        used = sem("chunks_used")
        filled = sem("psum_filled")
        empt_a = sem("psum_emptied_by_scalar")
        empt_v = sem("psum_emptied_by_vector")
        s_zero = sem("zeros_ready")
        s_const = sem("constants_ready")
        s_seed = sem("constant_seeds_ready")
        ord_v = sem("vector_order")
        ord_a = sem("scalar_order")
        s_sq = sem("squares_summed")
        s_ms = sem("mean_squares_ready")
        s_root = sem("roots_ready")
        s_xn = sem("x_normed")
        s_v = sem("v_ready")
        s_conv = sem("conf_conv_steps")
        s_tap = sem("sample_tap_products_ready")
        s_xc = sem("conv_a_steps")
        s_new = sem("new_columns_packed")
        s_store = sem("output_rows_stored")
        s_sqv = sem("centred_squared")
        s_squ = sem("centred_squares_used")
        s_lam = sem("decay_exponent_ready")
        s_lexp = sem("decay_exponential_ready")
        s_sp = sem("decay_scales_ready")
        s_aw = sem("decay_and_tanh_ready")
        s_w = sem("tanh_used")
        s_rtt = sem("root_of_tanh_ready")
        s_hs = sem("states_ready")
        s_ln = sem("layer_norm_ready")
        s_sil = sem("silu_gate_ready")
        s_s = sem("silu_ready")
        s_m = sem("merged_ready")
        s_hn = sem("h_normed")
        s_split = sem("h_parts_cast")
        s_rest = sem("h_rest_ready")
        s_neg = sem("router_shift_ready")
        s_exp = sem("router_exponentials_ready")
        s_mask = sem("mask_ready")
        s_cnt = sem("counts_ready")
        s_sel = sem("selections_ready")
        s_selw = sem("weighted_selections_ready")
        s_pick = sem("gate_up_bias_picks_ready")
        s_pickd = sem("down_bias_picks_ready")
        s_xg = sem("piece_inputs_gathered")
        s_xe = sem("piece_inputs_in_sbuf")
        s_gc = sem("gate_clamped")
        s_uc = sem("up_clamped")
        s_sig = sem("gate_sigmoid_ready")
        s_prod = sem("gate_up_product_ready")
        s_hid = sem("hidden_ready")
        s_htp = sem("hidden_turned")
        s_hts = sem("hidden_t_in_sbuf")
        s_stp = sem("selection_turned")
        s_sts = sem("selection_t_in_sbuf")
        s_y = sem("piece_output_in_sbuf")
        s_sc = sem("output_spread_to_tokens")
        s_add = sem("output_added")
        s_sum = sem("output_complete")
        s_fin = sem("final_rows_ready")
        s_end = sem("results_stored")

        def flat(ap):
            n = len(ap.shape)
            return ap if n == 2 else ap.rearrange({3: "a b c -> (a b) c", 4: "a b c d -> (a b c) d"}[n])

        w_in = A["w_in"][0].rearrange("(p k) n -> p k n", k=NT)
        w_pw = A["w_conf_pw"][0].rearrange("(k p) n -> p k n", p=P)
        w_out = A["w_out"][0].rearrange("(k p) n -> p k n", p=P)
        w_gate = A["w_gate"][0].rearrange("e (p k) n -> e p (k n)", k=NT)
        w_up = A["w_up"][0].rearrange("e (p k) n -> e p (k n)", k=NT)
        w_down = A["w_down"][0].rearrange("e (p k) n -> e p (k n)", k=NT)
        HALF = SLOT // 2

        def slot_half(n, h):
            return ring[:, n % SLOTS, h * HALF:(h + 1) * HALF]

        def w_in_cols(n, h):
            if n < 4:
                return D + h * D + n * 256
            return [0, 0, 3 * D, 3 * D, 4 * D, 4 * D][n - 4] + (n % 2) * 512 + h * 256

        def gu_chunk(e, q):
            return 6 * e - 2 + q

        def d_chunk(e, q):
            return 6 * e + 8 + q

        LAST_D = 6 * (E - 1) + 4
        N_CHUNKS = LAST_D + 1

        def slot_of(m):
            return (MIX_CHUNKS + m) % SLOTS

        def landed_by(m0, e=0):
            return 32 * ((MIX_CHUNKS + m0) // SLOTS + 1) + 32 * e

        LAST_FILL = ["vb1", "vb3", "vb5", "vb7", "xa3", "xa7", "ga3", "ga7", "gb3", "gb7", "pw7", "pw7", "out11", "out11"]
        EA = lambda name: emptied_before(JOB[name], "a")
        EV = lambda name: emptied_before(JOB[name], "v")
        CONV_MID = 2 * (KC // 2) + 4
        N_STORES = 16 * 14
        N_CONV, N_XC = NT * (KC + 2), 2 * NT * KA

        def longest(eng):
            eng.wait_ge(s_cnt, 1)
            return eng.value_load(counts[0:1, E:E + 1], min_val=0, max_val=T)

        PAR_LOADS = [("w_conf_dw", W_DW, KC), ("w_conv_a", W_CA, KA), ("b_conv_a", B_CA, 1), ("b_rg_a", B_RA, 1),
                     ("b_rg_x", B_RX, 1), ("rg_lambda", LAM, 1), ("b_conf_dw", B_DW, 1), ("g_conf_ln", G_LN, 1),
                     ("b_conf_ln", B_LN, 1), ("b_conf_pw", B_PW, 1)]

        def load_rows(eng, rows):
            for name, r, n in rows:
                eng.dma_start(par_rows[r:r + n, :], A[name][0] if n > 1 else A[name]).then_inc(s_par, 16)

        def more_pieces(eng, most, piece, before=None):
            with eng.If(most > CAP):
                done = eng.alloc_register("pieces_done")
                eng.reg_mov(done, 0)
                with eng.Fori(1, -(-T // CAP)) as r:
                    if before is not None:
                        before(r)
                    with eng.Fori(0, E) as e:
                        count = eng.value_load(counts[0:1, bass.ds(e, 1)], min_val=0, max_val=T)
                        with eng.If(count > r * CAP):
                            piece(e, eng.snap(done), r)
                            eng.reg_add(done, done, 1)

        with nc.Block() as block:

            @block.sync
            def _(sp):
                for i in range(2):
                    sp.dma_start(acc[:, i, :], A["x_prompt"][0, i * P:(i + 1) * P, :]).then_inc(s_x[i], 16)
                sp.wait_ge(s_zero, 1)
                sp.dma_start(acc[0:T_S, 2, :], flat(A["x_sample"])).then_inc(s_x[2], 16)
                load_rows(sp, PAR_LOADS[5:])
                sp.dma_start(sta_rows[0:SEQS * HA, :], flat(A["state_conv_a"][0])).then_inc(s_sta, 16)
                sp.dma_start(sta_rows[SEQS * HA:SEQS * KA, :], A["state_h"][0]).then_inc(s_sta, 16)
                for n in range(MIX_CHUNKS):
                    if n == 1:
                        sp.dma_start(stc_rows[0:SEQS * HC // 2],
                                     flat(A["state_conf"][0]).rearrange("(h p) d -> p h d", h=2)).then_inc(s_stc, 16)
                    if n == 4:
                        for m, name in enumerate(("w_rg_a", "w_rg_x")):
                            sp.dma_start(w_rg[:, m], A[name][0].rearrange("n c d -> c n d")).then_inc(s_wrg, 16)
                        sp.dma_start(w_rt[:], A["w_router"][0].rearrange("(p k) e -> p k e", k=NT)).then_inc(s_rt, 16)
                        sp.dma_start(b_rt[:], A["b_router"].to_broadcast([P, E])).then_inc(s_rt, 16)
                    if n >= SLOTS:
                        sp.wait_ge(filled, JOB[LAST_FILL[n - SLOTS]] + 1)
                    for h in range(2):
                        if n < 10:
                            c = w_in_cols(n, h)
                            dst = slot_half(n, h).rearrange("p (k n) -> p k n", k=NT)
                            sp.dma_start(dst, w_in[:, :, c:c + 256]).then_inc(landed[n % SLOTS], 16)
                        else:
                            w, q = (w_pw, n - 10) if n < 12 else (w_out, n - 12)
                            dst = slot_half(n, h).rearrange("p (k n) -> p k n", k=2)
                            k = 4 * q + 2 * h
                            sp.dma_start(dst, w[:, k:k + 2, :]).then_inc(landed[n % SLOTS], 16)

                def load(e, m, slot, kind, q):
                    if type(m) is int and m < SLOTS:
                        sp.wait_ge(filled, JOB[LAST_FILL[MIX_CHUNKS - SLOTS + m]] + 1)
                    else:
                        sp.wait_ge(used, m - SLOTS + 1)
                    for h in range(2):
                        dst = ring[:, slot, h * HALF:(h + 1) * HALF]
                        if kind == "gu":
                            src = (w_gate, w_up)[h][e, :, q * HALF:(q + 1) * HALF]
                        else:
                            src = w_down[e, :, q * SLOT + h * HALF:q * SLOT + (h + 1) * HALF]
                        sp.dma_start(dst, src).then_inc(landed[slot], 16)

                for q in range(4):
                    load(0, q, slot_of(q), "gu", q)
                sp.wait_ge(filled, JOB["out11"] + 1)
                for m, name in enumerate(("b_gate", "b_up", "b_down")):
                    sp.dma_start(bias[m * E:(m + 1) * E, :], A[name][0]).then_inc(s_bias, 16)
                for q in range(2):
                    load(1, gu_chunk(1, q), slot_of(gu_chunk(1, q)), "gu", q)
                sp.wait_ge(s_split, 3 * TILES)
                sp.wait_ge(filled, JOB["logits1"] + 1)
                for h in range(2):
                    sp.dma_start(spare[:, h * HALF:(h + 1) * HALF],
                                 w_down[E - 1, :, SLOT + h * HALF:SLOT + (h + 1) * HALF]).then_inc(s_spare, 16)
                for q in range(2, 4):
                    load(1, gu_chunk(1, q), slot_of(gu_chunk(1, q)), "gu", q)
                for q in range(2):
                    load(0, d_chunk(0, q), slot_of(d_chunk(0, q)), "d", q)
                most = longest(sp)
                with sp.Fori(2, E) as e:
                    for q in range(4):
                        load(e, gu_chunk(e, q), slot_of(gu_chunk(2, q)), "gu", q)
                    for q in range(2):
                        load(e - 1, d_chunk(e - 1, q), slot_of(d_chunk(1, q)), "d", q)
                load(E - 1, LAST_D, slot_of(LAST_D), "d", 0)

                def load_piece(e, n, r):
                    for q in range(6):
                        load(e, N_CHUNKS + 6 * n + q, slot_of(N_CHUNKS + q), "gu" if q < 4 else "d", q % 4)
                more_pieces(sp, most, load_piece)
                sp.wait_ge(s_fin, 1)
                sp.dma_start(flat(O[1]), h_tok[0:T_S, 2, :]).then_inc(s_end, 16)
                for i in range(2):
                    sp.wait_ge(s_fin, i + 2)
                    sp.dma_start(O[0][0, i * P:(i + 1) * P, :], h_tok[:, i, :]).then_inc(s_end, 16)
                sp.wait_ge(s_end, 48)

            @block.gpsimd
            def _(pool):
                pool.memset(ident[:], 0.0).then_inc(s_seed, 1)
                pool.memset(tri[:], 1.0).then_inc(s_seed, 1)
                pool.memset(ones[:], 1.0 / D).then_inc(s_const, 1)
                pool.memset(ones_h[:], 1.0).then_inc(s_const, 1)
                pool.wait_ge(s_seed, 1)
                pool.affine_select(out=ident[:], in_=ident[:], compare_op=ALU.not_equal, fill=1.0, base=0,
                                   pattern=[[-1, P]], channel_multiplier=1).then_inc(s_const, 1)
                pool.wait_ge(s_seed, 2)
                pool.affine_select(out=tri[:], in_=tri[:], compare_op=ALU.is_gt, fill=0.0, base=0,
                                   pattern=[[1, P]], channel_multiplier=-1).then_inc(s_const, 1)
                pool.iota(slot_no[:], [[0, 2], [1, CAP]], base=0, channel_multiplier=0,
                          allow_small_or_imprecise_dtypes=True).then_inc(s_const, 1)
                for c in range(0, NT, 2):
                    for cc in (c, c + 1):
                        pool.wait_ge(empt_a, EA(f"vb{cc}"))
                        v = vx[:, cc, HC:HC + T_P]
                        pool.tensor_tensor(v, v, sg[:, cc % 2, 0:T_P], ALU.mult).then_inc(s_v, 1)
                        v = vx[:, cc, HC + T_P:].rearrange("p (s t) -> p s t", s=SEQS)[:, :, HC:]
                        pool.tensor_tensor(v, v, sg[:, cc % 2, T_P:].rearrange("p (s t) -> p s t", s=SEQS),
                                           ALU.mult).then_inc(s_v, 1)
                    if c == 0:
                        pool.wait_ge(empt_v, EV("par"))
                        pool.wait_ge(empt_a, EA("stc3"))
                        pool.wait_ge(filled, JOB["sta"] + 1)
                    else:
                        pool.wait_ge(s_conv, (c - 2) * (KC + 2) + CONV_MID)
                    for cc in (c, c + 1):
                        pool.wait_ge(s_v, 2 * cc + 2)
                        v = vx[:, cc, HC + T_P:].rearrange("p (s t) -> p s t", s=SEQS)
                        w = par[:, cc, W_DW:W_DW + KC].unsqueeze(1).to_broadcast([P, SEQS, KC])
                        for t in range(STEPS):
                            ins = pool.tensor_tensor(taps_s[:, cc % 2, :, t, :], v[:, :, t:t + KC], w, ALU.mult)
                        ins.then_inc(s_tap, 1)
                pool.dma_start(O[7][0][:, 0:HC - STEPS, :], A["state_conf"][0][:, STEPS:HC, :]).then_inc(s_store, 16)
                pool.wait_ge(s_v, 2 * NT)
                pool.tensor_copy(v_new.rearrange("p c (s t) -> p c s t", s=SEQS),
                                 vx[:, :, HC + T_P:].rearrange("p c (s t) -> p c s t", s=SEQS)[:, :, :, HC:]).then_inc(s_new, 1)
                pool.wait_ge(empt_a, EA("xa7"))
                pool.tensor_copy(xa_new.rearrange("p c (s t) -> p c s t", s=SEQS),
                                 xa[:, :, HA + T_P:].rearrange("p c (s t) -> p c s t", s=SEQS)[:, :, :, STEPS:]).then_inc(s_new, 1)
                pool.wait_ge(empt_a, EA("vp1"))
                pool.dma_start(flat(O[4][0]), st_v[0:HC, 0, :]).then_inc(s_store, 16)
                pool.wait_ge(empt_a, EA("vs1"))
                for s in range(SEQS):
                    pool.dma_start(O[7][0][s, HC - STEPS:, :], st_v[s * STEPS:(s + 1) * STEPS, 1, :]).then_inc(s_store, 16)
                pool.wait_ge(empt_a, EA("xp1"))
                pool.dma_start(flat(O[2][0]), st_x[0:HA, 0, :]).then_inc(s_store, 16)
                pool.wait_ge(empt_a, EA("xs1"))
                pool.dma_start(flat(O[5][0]), st_x[0:SEQS * HA, 1, :]).then_inc(s_store, 16)
                pool.wait_ge(empt_a, EA("ho1"))
                pool.dma_start(O[3][0], st_h[0:1, :]).then_inc(s_store, 16)
                pool.dma_start(O[6][0], st_h[1:1 + SEQS, :]).then_inc(s_store, 16)
                for n, i in enumerate(TILE_ORDER):
                    if n == 2:
                        pool.wait_ge(filled, JOB["out11"] + 1)
                        pool.wait_ge(s_rest, 4)
                        pool.memset(bias[3 * E:, :], 0.0).then_inc(s_bz, 1)
                        pool.wait_ge(s_bz, 1)
                    pool.wait_ge(filled, JOB[f"ht{i}b"] + 1)
                    for s in range(2):
                        pool.wait_ge(s_split, 3 * n + s + 1)
                        pool.tensor_tensor(h_tok[:, i, :], h_tok[:, i, :], h_split[:, s, i, :], ALU.subtract).then_inc(s_rest, 1)
                pool.wait_ge(filled, JOB["logits1"] + 1)
                pool.dma_start(g_fin, A["g_final"].rearrange("(a d) -> a d", a=1).to_broadcast([P, D])).then_inc(s_gfin, 16)
                pool.wait_ge(s_store, N_STORES)

            @block.scalar
            def _(act):
                act.dma_start(g_mix[:], A["g_mix"][0].rearrange("(p k) -> p k", k=NT)).then_inc(s_gain, 16)
                load_rows(act, PAR_LOADS[:5])
                act.dma_start(g_ffn[:], A["g_ffn"][0].rearrange("(p k) -> p k", k=NT)).then_inc(s_gain, 16)

                def empty(name):
                    act.wait_ge(filled, JOB[name] + 1)
                    return bank(JOB[name])

                def square(i, dst, sums):
                    act.activation(dst, acc[:, i, :], ACT.Square, accum_out=stat[:, sums + i:sums + i + 1]).then_inc(s_sq, 1)

                def root(i, n, means):
                    act.wait_ge(s_ms, n)
                    act.activation(stat[:, means + 3 + i:means + 4 + i], stat[:, means + i:means + i + 1],
                                   ACT.Sqrt).then_inc(s_root, 1)

                for i in range(TILES):
                    act.wait_ge(s_x[i], 16)
                    if i:
                        act.wait_ge(s_sq, i)
                    square(i, junk, 0)
                for i in range(TILES):
                    root(i, i + 1, 3)
                act.wait_ge(s_gain, 32)
                for k in range(0, NT, 2):
                    act.activation(hn[:, k, :], empty(f"hn{k}")[:, 0:T], ACT.Copy, scale=g_mix[:, k:k + 1]).then_inc(empt_a, 1)
                act.wait_ge(s_lam, 1)
                act.activation(lamw[:, 1, :], lamw[:, 0, :], ACT.Exp, scale=-1.0).then_inc(s_lexp, 1)
                for c in range(NT):
                    z = empty(f"va{c}")
                    act.copy(vx[:, c, HC:HC + T_P], z[:, 0:T_P])
                    act.copy(vx[:, c, HC + T_P:].rearrange("p (s t) -> p s t", s=SEQS)[:, :, HC:],
                             z[:, T_P:T].rearrange("p (s t) -> p s t", s=SEQS)).then_inc(empt_a, 1)
                    z = empty(f"vb{c}")
                    if c >= 2:
                        act.wait_ge(s_v, 2 * c - 2)
                    act.activation(sg[:, c % 2, :], z[:, 0:T], ACT.Sigmoid).then_inc(empt_a, 1)
                    if c == 0:
                        for i in range(4):
                            z = empty(f"stc{i}")
                            for c in range(2):
                                dst = vx[:, 2 * i + c, HC + T_P:].rearrange("p (s t) -> p s t", s=SEQS)[:, :, 0:HC]
                                ins = act.copy(dst, z[:, c * SEQS * HC:(c + 1) * SEQS * HC].rearrange("p (s t) -> p s t", s=SEQS))
                            ins.then_inc(empt_a, 1)
                for c in range(NT):
                    z = empty(f"xa{c}")
                    act.copy(xa[:, c, HA:HA + T_P], z[:, 0:T_P])
                    act.copy(xa[:, c, HA + T_P:].rearrange("p (s t) -> p s t", s=SEQS)[:, :, HA:],
                             z[:, T_P:T].rearrange("p (s t) -> p s t", s=SEQS)).then_inc(empt_a, 1)
                for name, st, b, r in (("vp", st_v, 0, HC), ("vs", st_v, 1, T_S), ("xp", st_x, 0, HA),
                                       ("xs", st_x, 1, SEQS * HA)):
                    for h in range(2):
                        act.copy(st[0:r, b, h * 512:(h + 1) * 512], empty(f"{name}{h}")[0:r, :]).then_inc(empt_a, 1)
                for c in range(NT):
                    act.activation(gate_a[:, c, :], empty(f"ga{c}")[:, 0:T], ACT.Sigmoid).then_inc(empt_a, 1)
                act.wait_ge(empt_v, EV("mean"))
                for c in range(NT):
                    if c >= 2:
                        act.wait_ge(s_squ, c - 1)
                    act.activation(sg[:, c % 2, :], vc[:, c, :], ACT.Square).then_inc(s_sqv, 1)
                act.wait_ge(s_store, N_STORES - 32)
                for c in range(4):
                    act.activation(gate_b[:, c, :], empty(f"gb{c}")[:, 0:T], ACT.Sigmoid).then_inc(empt_a, 1)
                act.wait_ge(empt_v, EV("var"))
                act.activation(sg[:, 1, :], sg[:, 0, :], ACT.Sqrt).then_inc(s_root, 1)
                act.wait_ge(s_ln, 1)
                for c in range(NT):
                    act.activation(silu[c], vc[:, c, :], ACT.Sigmoid, scale=par[:, c, G_LN:G_LN + 1],
                                   bias=par[:, c, B_LN:B_LN + 1]).then_inc(s_sil, 1)
                for c in (4, 5):
                    act.activation(gate_b[:, c, :], empty(f"gb{c}")[:, 0:T], ACT.Sigmoid).then_inc(empt_a, 1)
                for c in range(NT):
                    act.activation(rt[:, c, :], empty(f"r{c}")[:, 0:T], ACT.Sigmoid,
                                   bias=par[:, c, B_RA:B_RA + 1]).then_inc(empt_a, 1)
                    act.activation(ig[:, c, :], empty(f"i{c}")[:, 0:T], ACT.Sigmoid,
                                   bias=par[:, c, B_RX:B_RX + 1]).then_inc(empt_a, 1)
                for c in (6, 7):
                    act.activation(gate_b[:, c, :], empty(f"gb{c}")[:, 0:T], ACT.Sigmoid).then_inc(empt_a, 1)
                act.wait_ge(s_xc, N_XC)
                act.wait_ge(s_sp, 1)
                act.wait_ge(empt_a, EA(f"i{NT - 1}"))
                for c in range(NT):
                    act.activation(aa[:, c, :], rt[:, c, :], ACT.Exp, scale=lamw[:, 4, c:c + 1]).then_inc(ord_a, 1)
                for c in range(NT):
                    act.wait_ge(ord_a, NT)
                    act.activation(rt[:, c, :], rt[:, c, :], ACT.Tanh, scale=lamw[:, 5, c:c + 1]).then_inc(s_aw, 1)
                act.wait_ge(s_w, 1)
                act.activation(rt[:, :, :], rt[:, :, :], ACT.Sqrt).then_inc(s_rtt, 1)
                act.wait_ge(s_s, NT)
                for h in range(2):
                    act.copy(st_h[0:1 + SEQS, h * 512:(h + 1) * 512], empty(f"ho{h}")[0:1 + SEQS, :]).then_inc(empt_a, 1)

                for n, i in enumerate(TILE_ORDER):
                    act.wait_ge(empt_v, EV(f"out{i}1" if i < 2 else "out2"))
                    square(i, h_tok[:, i, :], 12)
                    root(i, TILES + n + 1, 15)
                    act.wait_ge(s_hn, n + 1)
                    act.wait_ge(s_store, N_STORES)
                    for s in range(3):
                        if s:
                            act.wait_ge(s_rest, 2 * n + s)
                        act.copy(h_split[:, s, i, :], h_tok[:, i, :]).then_inc(s_split, 1)
                for n, i in enumerate(TILE_ORDER):
                    act.wait_ge(s_neg, n + 1)
                    act.activation(comb[:, i, :], lg[:, i, 0:E], ACT.Exp, bias=stat[:, i:i + 1]).then_inc(s_exp, 1)

                def turned(k, b):
                    act.wait_ge(s_htp, k + 1)
                    act.copy(hid_t[:, b, :, :], ps[:, BK_HT, :].rearrange("p (k s) -> p k s", k=NT)).then_inc(s_hts, 1)

                def sigmoid(k):
                    act.wait_ge(s_gc, k + 1)
                    if not (type(k) is int and k == 0):
                        act.wait_ge(s_hid, k)
                    act.activation(sig_e, g_e, ACT.Sigmoid, scale=ALPHA).then_inc(s_sig, 1)

                def selection(k, b):
                    act.wait_ge(s_stp, k + 1)
                    act.copy(sel_t[:, b, :], ps[:, BK_SEL, 0:T_PAD]).then_inc(s_sts, 1)

                def output(k, b, last_chunk):
                    act.wait_ge(used, last_chunk + 1)
                    act.copy(y_e[:, b, :], ps[:, BK_D, :]).then_inc(s_y, 1)

                sigmoid(0)
                selection(0, 0)
                turned(0, 0)
                sigmoid(1)
                output(0, 0, d_chunk(0, 1))
                most = longest(act)
                with act.Fori(1, E // 2) as pair:
                    e = pair * 2
                    for b in range(2):
                        selection(e + (b - 1), 1 - b)
                        turned(e + (b - 1), 1 - b)
                        sigmoid(e + b)
                        output(e + (b - 1), 1 - b, d_chunk(e + (b - 1), 1))
                selection(E - 1, 1)
                turned(E - 1, 1)
                output(E - 1, 1, LAST_D)

                def piece(e, n, r):
                    sigmoid(E + n)
                    selection(E + n, 0)
                    turned(E + n, 0)
                    output(E + n, 0, N_CHUNKS + 6 * n + 5)
                more_pieces(act, most, piece)

                act.wait_ge(s_sum, 1)
                for n, i in enumerate(TILE_ORDER):
                    square(i, h_tok[:, i, :], 0)
                for n, i in enumerate(TILE_ORDER):
                    root(i, 2 * TILES + n + 1, 3)

            @block.tensor
            def _(pe):
                def fill(name):
                    j = JOB[name]
                    if j >= 8:
                        if emptied_before(j - 8, "a"):
                            pe.wait_ge(empt_a, emptied_before(j - 8, "a"))
                        if emptied_before(j - 8, "v"):
                            pe.wait_ge(empt_v, emptied_before(j - 8, "v"))
                    return bank(j)

                def turn(dst, src):
                    k = src.shape[0]
                    return nc.tensor.transpose(dst, src, ident[0:k, 0:k])

                pe.wait_ge(s_const, 5)
                pe.wait_ge(s_par, 160)
                z = fill("par")
                for c in range(NT):
                    ins = turn(z[:, c * N_PAR:(c + 1) * N_PAR], par_rows[0:N_PAR, c * P:(c + 1) * P])
                ins.then_inc(filled, 1)
                pe.wait_ge(s_sta, 32)
                z = fill("sta")
                for c in range(NT):
                    ins = turn(z[:, c * 32:(c + 1) * 32], sta_rows[0:32, c * P:(c + 1) * P])
                ins.then_inc(filled, 1)
                pe.wait_ge(s_xn, TILES)
                for k in range(NT):
                    z = fill(f"hn{k}")
                    for i in range(TILES):
                        n = min(P, T - i * P)
                        ins = turn(z[:, i * P:i * P + n], x_tok[0:n, i, k::NT])
                    ins.then_inc(filled, 1)

                def w_in_job(name, n, h, i):
                    w = slot_half(n, h).rearrange("p (k n) -> p k n", k=NT)
                    z = fill(name)
                    for k in range(NT):
                        ins = nc.tensor.matmul(z[:, 0:T], w[:, k, i * P:(i + 1) * P], hn[:, k, :],
                                               start=(k == 0), stop=(k == NT - 1))
                    ins.then_inc(filled, 1)

                def turn_conf_state():
                    pe.wait_ge(s_stc, 16)
                    rows = SEQS * HC // 2
                    for i in range(4):
                        z = fill(f"stc{i}")
                        for c in range(2):
                            for h in range(2):
                                src = stc_rows[0:rows, h, (2 * i + c) * P:(2 * i + c + 1) * P]
                                ins = turn(z[:, (2 * c + h) * rows:(2 * c + h + 1) * rows], src)
                        ins.then_inc(filled, 1)

                pe.wait_ge(empt_a, EA("hn6"))
                pe.wait_ge(empt_v, EV("hn7"))
                for n in range(4):
                    pe.wait_ge(landed[n % SLOTS], 32 * (n // SLOTS + 1))
                    for i in range(2):
                        w_in_job(f"va{2 * n + i}", n, 0, i)
                        w_in_job(f"vb{2 * n + i}", n, 1, i)
                        if n == 0 and i == 0:
                            turn_conf_state()

                def w_in_block(name, n0, tiles=range(NT)):
                    for c in tiles:
                        n = n0 + c // 4
                        pe.wait_ge(landed[n % SLOTS], 32 * (n // SLOTS + 1))
                        w_in_job(f"{name}{c}", n, c % 4 // 2, c % 2)

                w_in_block("xa", 4)
                pe.wait_ge(s_v, 2 * NT)
                pe.wait_ge(s_new, 2)
                for name, r, src in (("vp", HC, lambda c: vx[:, c, T_P:T_P + HC]),
                                     ("vs", T_S, lambda c: v_new[:, c, :]),
                                     ("xp", HA, lambda c: xa[:, c, T_P:T_P + HA]),
                                     ("xs", SEQS * HA, lambda c: xa_new[:, c, :])):
                    for h in range(2):
                        z = fill(f"{name}{h}")
                        for c in range(4):
                            ins = turn(z[0:r, c * P:(c + 1) * P], src(4 * h + c))
                        ins.then_inc(filled, 1)
                w_in_block("ga", 6)
                pe.wait_ge(s_conv, N_CONV)
                z = fill("mean")
                for c in range(NT):
                    ins = nc.tensor.matmul(z[:, 0:T], ones[:], vc[:, c, :], start=(c == 0), stop=(c == NT - 1))
                ins.then_inc(filled, 1)
                w_in_block("gb", 8, range(4))
                z = fill("var")
                for c in range(NT):
                    pe.wait_ge(s_sqv, c + 1)
                    ins = nc.tensor.matmul(z[:, 0:T], ones[:], sg[:, c % 2, :], start=(c == 0), stop=(c == NT - 1))
                    ins.then_inc(*((s_squ, 1) if c < NT - 1 else (filled, 1)))
                w_in_block("gb", 8, (4, 5))
                pe.wait_ge(s_xc, N_XC)
                pe.wait_ge(s_wrg, 32)
                for c in range(NT):
                    for m, name in enumerate(("r", "i")):
                        z = fill(f"{name}{c}")
                        nc.tensor.matmul(z[:, 0:T], w_rg[:, m, c, :], xc[:, c, :], start=True, stop=True).then_inc(filled, 1)
                w_in_block("gb", 8, (6, 7))
                for n in (10, 11):
                    pe.wait_ge(landed[n % SLOTS], 32 * (n // SLOTS + 1))
                pe.wait_ge(s_s, NT)
                w4 = [slot_half(10 + k // 4, k % 4 // 2).rearrange("p (k n) -> p k n", k=2)[:, k % 2] for k in range(NT)]
                for c in range(NT):
                    z = fill(f"pw{c}")
                    for k in range(NT):
                        ins = nc.tensor.matmul(z[:, 0:T], w4[k][:, c * P:(c + 1) * P], vc[:, k, :],
                                               start=(k == 0), stop=(k == NT - 1))
                    ins.then_inc(filled, 1)
                pe.wait_ge(s_hs, 1)
                for h in range(2):
                    z = fill(f"ho{h}")
                    for c in range(4):
                        ins = turn(z[0:1 + SEQS, c * P:(c + 1) * P], xc[:, 4 * h + c, T_P - 1::STEPS])
                    ins.then_inc(filled, 1)
                for n in (12, 13):
                    pe.wait_ge(landed[n % SLOTS], 32 * (n // SLOTS + 1))
                w4 = [slot_half(12 + k // 4, k % 4 // 2).rearrange("p (k n) -> p k n", k=2)[:, k % 2] for k in range(NT)]
                pe.wait_ge(s_m, NT)

                def out_rows(i, halves=(0, 1)):
                    for h in halves:
                        z = fill(f"out{i}{h}")
                        for k in range(NT):
                            ins = nc.tensor.matmul(z[:, :], mt[:, k, i * P:(i + 1) * P], w4[k][:, h * 512:(h + 1) * 512],
                                                   start=(k == 0), stop=(k == NT - 1))
                        ins.then_inc(filled, 1)

                def turn_h(i):
                    pe.wait_ge(s_hn, TILE_ORDER.index(i) + 1)
                    for h in range(2):
                        z = fill(f"ht{i}{'ab'[h]}")
                        for k in range(4):
                            ins = turn(z[:, k * P:(k + 1) * P], h_tok[:, i, 4 * h + k::NT])
                        ins.then_inc(filled, 1)

                def logits(i):
                    pe.wait_ge(s_rt, 32)
                    pe.wait_ge(empt_v, EV(f"ht{i}b"))
                    z = fill(f"logits{i}")
                    for k in range(NT):
                        ins = nc.tensor.matmul(z[:, 0:E], h_cm[:, k, i * P:(i + 1) * P], w_rt[:, k, :],
                                               start=(k == 0), stop=(k == NT - 1))
                    ins.then_inc(filled, 1)

                z = fill("out2")
                for k in range(NT):
                    for h in range(2):
                        ins = nc.tensor.matmul(z[h * T_S:(h + 1) * T_S, :], mt[:, k, 2 * P:T],
                                               w4[k][:, h * 512:(h + 1) * 512], start=(k == 0), stop=(k == NT - 1))
                ins.then_inc(filled, 1)
                out_rows(0)
                turn_h(2)
                out_rows(1, (0,))
                turn_h(0)
                logits(2)
                out_rows(1, (1,))
                logits(0)
                turn_h(1)
                logits(1)
                pe.wait_ge(s_mask, TILES)
                z = fill("rank")
                for i in range(TILES + 1):
                    for j in range(min(i + 1, TILES)):
                        before = ones_h if j < i else tri
                        ins = nc.tensor.matmul(z[:, i * E:(i + 1) * E], before[:], mask_h[:, j, :],
                                               start=(j == 0), stop=(j == min(i, TILES - 1)))
                ins.then_inc(filled, 1)

                def gather(k, b):
                    pe.wait_ge(s_sel, k + 1)
                    if not (type(k) is int and k == 0):
                        pe.wait_ge(s_xe, k)
                    for t in range(NT):
                        n = 0
                        for s in range(3):
                            for i in range(TILES):
                                ins = nc.tensor.matmul(ps[:, BK_X, t * CAP:(t + 1) * CAP], h_split[:, s, i, t::NT],
                                                       sel[:, b, i, :], start=(n == 0), stop=(n == 3 * TILES - 1))
                                n += 1
                    ins.then_inc(s_xg, 1)

                def gate_up(k, b, slots, fills, spread=None):
                    pe.wait_ge(s_xe, k + 1)
                    pe.wait_ge(s_pick, k + 1)
                    if not (type(k) is int and k == 0):
                        pe.wait_ge(s_gc, k)
                        pe.wait_ge(s_uc, k)
                    for h in range(2):
                        for m in range(2):
                            nc.tensor.matmul(ps[m * CAP:(m + 1) * CAP, BK_GU + h, :], pick[:, b, m, :],
                                             bias[:, h * 512:(h + 1) * 512], start=True, stop=False)
                    for t in range(NT):
                        q = t // 2
                        if t % 2 == 0:
                            pe.wait_ge(landed[slots[q]], fills[q])
                        w = ring[:, slots[q], :].rearrange("p (m k n) -> p m k n", m=2, k=2)
                        for h in range(2):
                            for m in range(2):
                                ins = nc.tensor.matmul(ps[m * CAP:(m + 1) * CAP, BK_GU + h, :], x_e[:, b, t, :],
                                                       w[:, m, t % 2, h * 512:(h + 1) * 512],
                                                       start=False, stop=(t == NT - 1))
                        if t % 2:
                            ins.then_inc(used, 1)
                            if spread is not None and q < TILES:
                                spread(q)

                def turn_both(k, b):
                    pe.wait_ge(s_selw, k + 1)
                    pe.wait_ge(s_hid, k + 1)
                    if not (type(k) is int and k == 0):
                        pe.wait_ge(s_sts, k)
                        pe.wait_ge(s_hts, k)
                    for i in range(TILES):
                        ins = turn(ps[:, BK_SEL, i * P:(i + 1) * P], sel_w[:, b, i].rearrange("p d s -> p (d s)"))
                    ins.then_inc(s_stp, 1)
                    for t in range(NT):
                        ins = turn(ps[:, BK_HT, t * CAP:(t + 1) * CAP], hid[:, t::NT])
                    ins.then_inc(s_htp, 1)

                def down(k, b, slots, fills, between=None):
                    pe.wait_ge(s_hts, k + 1)
                    pe.wait_ge(s_pickd, k + 1)
                    if not (type(k) is int and k == 0):
                        pe.wait_ge(s_y, k)
                    for h in range(2):
                        nc.tensor.matmul(ps[h * CAP:(h + 1) * CAP, BK_D, :], pick[:, b, 2, :],
                                         bias[:, h * 512:(h + 1) * 512], start=True, stop=False)
                    order = (0, 1) if len(slots) == 2 else (1, 0)
                    for q in order:
                        if q < len(slots):
                            pe.wait_ge(landed[slots[q]], fills[q])
                            w = ring[:, slots[q], :]
                        else:
                            pe.wait_ge(s_spare, 32)
                            w = spare
                        w = w.rearrange("p (k n) -> p k n", k=4)
                        for t in range(4):
                            for h in range(2):
                                ins = nc.tensor.matmul(ps[h * CAP:(h + 1) * CAP, BK_D, :], hid_t[:, b, 4 * q + t, :],
                                                       w[:, t, h * 512:(h + 1) * 512],
                                                       start=False, stop=(q == order[1] and t == 3))
                        if q < len(slots):
                            ins.then_inc(used, 1)
                        if q == order[0] and between is not None:
                            between()

                def spread_tile(k, b, i, bk=None):
                    if i == 0:
                        pe.wait_ge(s_y, k + 1)
                        pe.wait_ge(s_sts, k + 1)
                    if bk is None:
                        bk = BK_OUT
                        if not (type(k) is int and k == 0 and i == 0):
                            pe.wait_ge(s_add, TILES * k + i)
                    for h in range(2):
                        ins = nc.tensor.matmul(ps[:, bk + h, :], sel_t[h * CAP:(h + 1) * CAP, b, i * P:(i + 1) * P],
                                               y_e[h * CAP:(h + 1) * CAP, b, :], start=True, stop=True)
                    ins.then_inc(s_sc, 1)

                def slots_from(m0, n):
                    return [slot_of(m0 + q) for q in range(n)]

                def fills_from(m0, n, e=0):
                    return [landed_by(m0 + q, e) for q in range(n)]

                assert JOB["rank"] % 8 != BK_X
                pe.wait_ge(empt_v, EV("logits1"))
                pe.wait_ge(s_split, 3 * TILES)
                pe.wait_ge(s_bz, 1)
                pe.wait_ge(s_bias, 48)
                gather(0, 0)
                pe.wait_ge(empt_v, EV("rank"))
                gate_up(0, 0, slots_from(0, 4), fills_from(0, 4))
                gather(1, 1)
                gate_up(1, 1, slots_from(4, 4), fills_from(4, 4))
                turn_both(0, 0)
                gather(2, 0)
                down(0, 0, slots_from(8, 2), fills_from(8, 2))

                def expert(e, b, since, spread=True, last=False):
                    gate_up(e, b, slots_from(gu_chunk(2, 0), 4), fills_from(gu_chunk(2, 0), 4, since),
                            lambda i: spread_tile(e - 2, b, i))
                    turn_both(e - 1, 1 - b)
                    if not last:
                        gather(e + 1, 1 - b)
                    down(e - 1, 1 - b, slots_from(d_chunk(1, 0), 2), fills_from(d_chunk(1, 0), 2, since))

                most = longest(pe)
                with pe.Fori(1, E // 2 - 1) as pair:
                    e = pair * 2
                    for b in range(2):
                        expert(e + b, b, e + (b - 2))
                expert(E - 2, 0, E - 4)
                expert(E - 1, 1, E - 3, last=True)
                turn_both(E - 1, 1)

                def spread_before_last():
                    pe.wait_ge(s_add, TILES * (E - 2))
                    spread_tile(E - 2, 0, 0, OUT_BANKS[0])
                    spread_tile(E - 2, 0, 1, OUT_BANKS[1])
                    pe.wait_ge(s_sts, E)
                    pe.wait_ge(s_hts, E)
                    spread_tile(E - 2, 0, 2, OUT_BANKS[2])
                pe.wait_ge(s_gc, E)
                pe.wait_ge(s_uc, E)
                down(E - 1, 1, slots_from(LAST_D, 1), fills_from(LAST_D, 1), spread_before_last)
                for i in range(TILES):
                    pe.wait_ge(s_add, TILES * (E - 2) + i + 1)
                    spread_tile(E - 1, 1, i, OUT_BANKS[i])

                def piece(e, n, r):
                    k = E + n
                    pe.wait_ge(s_add, TILES * k)
                    gather(k, 0)
                    gate_up(k, 0, slots_from(N_CHUNKS, 4), fills_from(N_CHUNKS, 4, n))
                    turn_both(k, 0)
                    down(k, 0, slots_from(N_CHUNKS + 4, 2), fills_from(N_CHUNKS + 4, 2, n))
                    for i in range(TILES):
                        spread_tile(k, 0, i)
                more_pieces(pe, most, piece)

            @block.vector
            def _(dve):
                steps = [0]

                def link(ins):
                    steps[0] += 1
                    ins.then_inc(ord_v, 1)
                    dve.wait_ge(ord_v, steps[0])

                def full(name):
                    dve.wait_ge(filled, JOB[name] + 1)
                    return bank(JOB[name])

                V = nc.vector
                V.memset(acc[:, 2, :], 0.0).then_inc(s_zero, 1)
                V.memset(xa[:, :, 0:HA], 0.0)
                V.memset(vx[:, :, 0:HC], 0.0)
                V.memset(lg[:, :, E:], -3.0e38)

                def inverse_root(i, n, sums):
                    m = sums + 3 + i
                    dve.wait_ge(s_sq, n)
                    V.tensor_scalar(stat[:, m:m + 1], stat[:, m - 3:m - 2], 1.0 / D, EPS, ALU.mult, ALU.add).then_inc(s_ms, 1)
                    dve.wait_ge(s_root, n if n <= TILES else n + 1)
                    link(V.reciprocal(stat[:, m + 6:m + 7], stat[:, m + 3:m + 4]))
                    return stat[:, m + 6:m + 7]

                for i in range(TILES):
                    inv = inverse_root(i, i + 1, 0)
                    V.tensor_scalar(x_tok[:, i, :], acc[:, i, :], inv, None, ALU.mult).then_inc(s_xn, 1)
                V.tensor_copy(par[:].rearrange("p c n -> p (c n)"), full("par")[:, 0:NT * N_PAR]).then_inc(empt_v, 1)
                z = full("sta")[:, 0:NT * 32].rearrange("p (c r) -> p c r", c=NT)
                V.tensor_copy(xa[:, :, HA + T_P:].rearrange("p c (s t) -> p c s t", s=SEQS)[:, :, :, 0:HA],
                              z[:, :, 0:SEQS * HA].rearrange("p c (s t) -> p c s t", s=SEQS))
                V.tensor_copy(h0[:], z[:, :, SEQS * HA:]).then_inc(empt_v, 1)
                dve.wait_ge(s_gain, 32)
                for k in range(1, NT, 2):
                    V.tensor_scalar(hn[:, k, :], full(f"hn{k}")[:, 0:T], g_mix[:, k:k + 1], None, ALU.mult).then_inc(empt_v, 1)
                dve.wait_ge(empt_v, EV("par"))
                lam = par[:, :, LAM]
                V.scalar_tensor_tensor(lamw[:, 0, :], lam, -1.0, lam, ALU.mult, ALU.max).then_inc(s_lam, 1)
                dve.wait_ge(s_lexp, 1)
                link(V.tensor_scalar(lamw[:, 2, :], lamw[:, 1, :], 2.0, None, ALU.add))
                link(V.reciprocal(lamw[:, 3, :], lamw[:, 2, :]))
                link(V.tensor_tensor(lamw[:, 2, :], lamw[:, 1, :], lamw[:, 3, :], ALU.mult))
                link(V.tensor_tensor(lamw[:, 3, :], lamw[:, 2, :], lamw[:, 2, :], ALU.mult))
                link(V.tensor_scalar(lamw[:, 0, :], lamw[:, 3, :], 1.0 / 17, None, ALU.mult))
                for n in (15, 13, 11, 9, 7, 5, 3):
                    link(V.scalar_tensor_tensor(lamw[:, 0, :], lamw[:, 0, :], 1.0 / n, lamw[:, 3, :], ALU.add, ALU.mult))
                link(V.scalar_tensor_tensor(lamw[:, 0, :], lamw[:, 0, :], 1.0, lamw[:, 2, :], ALU.add, ALU.mult))
                link(V.tensor_scalar(lamw[:, 1, :], lam, -1.0, 0.0, ALU.mult, ALU.max))
                link(V.scalar_tensor_tensor(lamw[:, 2, :], lamw[:, 0, :], 2.0, lamw[:, 1, :], ALU.mult, ALU.add))
                V.tensor_scalar(lamw[:, 4, :], lamw[:, 2, :], -RG_C, None, ALU.mult)
                V.tensor_scalar(lamw[:, 5, :], lamw[:, 2, :], RG_C / 2, None, ALU.mult).then_inc(s_sp, 1)

                def convolve(c, taps, hist, src, dst, w_row, b_row, done):
                    s4 = src[:, :, hist + T_P:].rearrange("p c (s t) -> p c s t", s=SEQS)
                    d4 = dst[:, :, T_P:].rearrange("p c (s t) -> p c s t", s=SEQS)
                    base = c * (2 * taps)
                    for j in range(taps):
                        for n in range(4):
                            cc = c + n % 2
                            w = par[:, cc, w_row + j:w_row + j + 1]
                            if n < 2:
                                x, y = src[:, cc, j:j + T_P], dst[:, cc, 0:T_P]
                            else:
                                x, y = s4[:, cc, :, j:j + STEPS], d4[:, cc]
                            if j == 0:
                                V.tensor_scalar(y, x, w, par[:, cc, b_row:b_row + 1], ALU.mult, ALU.add).then_inc(done, 1)
                            else:
                                dve.wait_ge(done, base + (4 * (j - 1) + n + 1))
                                V.scalar_tensor_tensor(y, x, w, y, ALU.mult, ALU.add).then_inc(done, 1)

                with dve.Fori(0, NT // 2) as half:
                    c = half * 2
                    dve.wait_ge(s_v, c * 2 + 4)
                    base = c * (KC + 2)
                    for j in range(KC):
                        past = 0
                        if j == KC // 2:
                            dve.wait_ge(s_tap, c + 2)
                            for n in range(2):
                                V.tensor_reduce(vc[:, c + n, T_P:].rearrange("p (s t) -> p s t", s=SEQS),
                                                taps_s[:, n], AX_X, ALU.add).then_inc(s_conv, 1)
                            for n in range(2):
                                dve.wait_ge(s_conv, base + (CONV_MID - 3 + n))
                                V.tensor_scalar(vc[:, c + n, T_P:], vc[:, c + n, T_P:], par[:, c + n, B_DW:B_DW + 1], None,
                                                ALU.add).then_inc(s_conv, 1)
                            past = 4
                        elif j > KC // 2:
                            past = 4
                        for n in range(2):
                            w = par[:, c + n, W_DW + j:W_DW + j + 1]
                            x, y = vx[:, c + n, j:j + T_P], vc[:, c + n, 0:T_P]
                            if j == 0:
                                V.tensor_scalar(y, x, w, par[:, c + n, B_DW:B_DW + 1], ALU.mult, ALU.add).then_inc(s_conv, 1)
                            else:
                                dve.wait_ge(s_conv, base + (2 * (j - 1) + n + 1 + (past if j != KC // 2 else 0)))
                                V.scalar_tensor_tensor(y, x, w, y, ALU.mult, ALU.add).then_inc(s_conv, 1)
                dve.wait_ge(empt_a, EA("xa1"))
                convolve(0, KA, HA, xa, xc, W_CA, B_CA, s_xc)
                dve.wait_ge(s_conv, N_CONV)
                mean = full("mean")[:, 0:T].unsqueeze(1).to_broadcast([P, NT, T])
                V.tensor_tensor(vc[:, :, :], vc[:, :, :], mean, ALU.subtract).then_inc(empt_v, 1)
                with dve.Fori(1, NT // 2) as half:
                    c = half * 2
                    dve.wait_ge(empt_a, c + (EA("xa0") + 1))
                    convolve(c, KA, HA, xa, xc, W_CA, B_CA, s_xc)
                V.tensor_scalar(sg[:, 0, :], full("var")[:, 0:T], EPS, None, ALU.add).then_inc(empt_v, 1)
                dve.wait_ge(s_root, TILES + 1)
                link(V.reciprocal(sg[:, 0, :], sg[:, 1, :]))
                inv = sg[:, 0, :].unsqueeze(1).to_broadcast([P, NT, T])
                V.tensor_tensor(vc[:, :, :], vc[:, :, :], inv, ALU.mult).then_inc(s_ln, 1)
                dve.wait_ge(s_ln, 1)
                for c in range(NT):
                    dve.wait_ge(s_sil, c + 1)
                    link(V.tensor_scalar(vc[:, c, :], vc[:, c, :], par[:, c, G_LN:G_LN + 1], par[:, c, B_LN:B_LN + 1],
                                         ALU.mult, ALU.add))
                    V.tensor_tensor(vc[:, c, :], vc[:, c, :], silu[c], ALU.mult).then_inc(s_s, 1)
                dve.wait_ge(empt_a, EA("i7"))
                dve.wait_ge(s_xc, N_XC)
                link(V.tensor_tensor(ig[:, :, :], ig[:, :, :], xc[:, :, :], ALU.mult))
                dve.wait_ge(s_aw, NT)
                V.scalar_tensor_tensor(xc[:, :, :], aa[:, :, :], 1.0, rt[:, :, :], ALU.add, ALU.mult).then_inc(s_w, 1)
                link(V.scalar_tensor_tensor(ig[:, :, :], aa[:, :, :], 1.0, ig[:, :, :], ALU.add, ALU.mult))
                dve.wait_ge(s_w, 1)
                link(V.tensor_scalar(aa[:, :, :], xc[:, :, :], -1.0, 1.0, ALU.mult, ALU.add))
                dve.wait_ge(s_rtt, 1)
                link(V.tensor_tensor(ig[:, :, :], ig[:, :, :], rt[:, :, :], ALU.mult))
                first = slice(T_P, T, STEPS)
                link(V.tensor_tensor(h0[:], h0[:], aa[:, :, first], ALU.mult))
                link(V.tensor_tensor(ig[:, :, first], ig[:, :, first], h0[:], ALU.add))
                V.memset(aa[:, :, first], 0.0)
                link(V.memset(aa[:, :, 0:1], 0.0))
                V.tensor_tensor_scan(xc_w, xa_w[:, 0:TW], ig_w, 0.0, ALU.mult, ALU.add).then_inc(s_hs, 1)
                dve.wait_ge(s_hs, 1)
                link(V.tensor_tensor(gate_a[:, :, :], gate_a[:, :, :], xc[:, :, :], ALU.mult))
                for c in range(NT):
                    V.scalar_tensor_tensor(mt[:, c, :], full(f"pw{c}")[:, 0:T], par[:, c, B_PW:B_PW + 1], gate_b[:, c, :],
                                           ALU.add, ALU.mult).then_inc(empt_v, 1)
                    dve.wait_ge(empt_v, EV(f"pw{c}"))
                    V.tensor_tensor(mt[:, c, :], mt[:, c, :], gate_a[:, c, :], ALU.add).then_inc(s_m, 1)
                gain = g_ffn[:, :].unsqueeze(2).to_broadcast([P, NT, P])

                def complete(i, halves=(0, 1)):
                    for h in halves:
                        rows = T_S if i == 2 else P
                        z = full("out2")[h * T_S:(h + 1) * T_S, :] if i == 2 else full(f"out{i}{h}")
                        a = acc[0:rows, i, h * 512:(h + 1) * 512]
                        ins = V.tensor_tensor(a, z, a, ALU.add)
                        if i < 2:
                            ins.then_inc(empt_v, 1)
                    if i == 2:
                        ins.then_inc(empt_v, 1)

                def norm(i):
                    inv = inverse_root(i, TILES + TILE_ORDER.index(i) + 1, 12)
                    V.tensor_scalar(h_tok[:, i, :], acc[:, i, :], inv, None, ALU.mult).then_inc(s_hn, 1)

                def take_turned(i):
                    for h in range(2):
                        z = full(f"ht{i}{'ab'[h]}")[:, :].rearrange("p (k t) -> p k t", k=4)
                        V.tensor_tensor(h_cm[:, 4 * h:4 * h + 4, i * P:(i + 1) * P], z, gain[:, 4 * h:4 * h + 4, :],
                                        ALU.mult).then_inc(empt_v, 1)

                def choose(i):
                    V.tensor_tensor(lg[:, i, 0:E], full(f"logits{i}")[:, 0:E], b_rt[:], ALU.add).then_inc(empt_v, 1)
                    dve.wait_ge(empt_v, EV(f"logits{i}"))
                    link(V.max(top[:, i, :], lg[:, i, :]))
                    V.tensor_scalar(stat[:, i:i + 1], top[:, i, 0:1], -1.0, None, ALU.mult).then_inc(s_neg, 1)
                    dve.wait_ge(s_neg, TILE_ORDER.index(i) + 1)
                    link(V.memset(top[:, i, 4:8], -3.0e38))
                    link(V.match_replace(lgr[:, i, :], top[:, i, :], lg[:, i, :], 3.0e38))
                    link(V.tensor_scalar(mask[:, i, :], lgr[:, i, 0:E], 3.0e38, None, ALU.is_equal))
                    if i == 2:
                        V.memset(mask[T_S:2 * T_S, 2, :], 0.0)
                        link(V.memset(mask[2 * T_S:, 2, :], 0.0))
                    V.tensor_copy(mask_h[:, i, :], mask[:, i, :]).then_inc(s_mask, 1)

                dve.wait_ge(s_rt, 32)
                complete(2)
                norm(2)
                complete(0)
                norm(0)
                take_turned(2)
                complete(1, (0,))
                take_turned(0)
                choose(2)
                complete(1, (1,))
                norm(1)
                choose(0)
                take_turned(1)
                choose(1)
                z = full("rank")
                zr = z[:, 0:TILES * E].rearrange("p (i e) -> p i e", i=TILES)
                link(V.scalar_tensor_tensor(rank[:, :, :], zr, 1.0, mask[:, :, :], ALU.add, ALU.mult))
                link(V.tensor_scalar(rank[:, :, :], rank[:, :, :], -1.0, None, ALU.add))

                picks = ident[:, :].rearrange("p (m e) -> p m e", e=E)

                def select(e, b, ranks):
                    for i in range(TILES):
                        ins = V.tensor_scalar(sel[:, b, i, :], slot_no[:, 0, :], ranks[:, i, bass.ds(e, 1)], None, ALU.is_equal)
                    ins.then_inc(s_sel, 1)
                    for m in range(2):
                        ins = V.tensor_copy(pick[:, b, m, :], picks[:, m, bass.ds(e, 1)].to_broadcast([P, CAP]))
                    ins.then_inc(s_pick, 1)

                def select_weighted(e, b, ranks):
                    for i in range(TILES):
                        ins = V.tensor_scalar(sel_w[:, b, i, :, :], slot_no[:, :, :], ranks[:, i, bass.ds(e, 1)],
                                              comb[:, i, bass.ds(e, 1)], ALU.is_equal, ALU.mult)
                    ins.then_inc(s_selw, 1)
                    V.tensor_copy(pick[:, b, 2, :], picks[:, 2, bass.ds(e, 1)].to_broadcast([P, CAP])).then_inc(s_pickd, 1)

                gains = g_ffn[:, :].unsqueeze(2).to_broadcast([P, NT, CAP])

                def take_inputs(k, b):
                    dve.wait_ge(s_xg, k + 1)
                    z = ps[:, BK_X, :].rearrange("p (k s) -> p k s", k=NT)
                    V.tensor_tensor(x_e[:, b, :, :], z, gains, ALU.mult).then_inc(s_xe, 1)

                gate_ps = ps[0:CAP, BK_GU:BK_GU + 2, :].rearrange("p h n -> p (h n)")
                up_ps = ps[CAP:2 * CAP, BK_GU:BK_GU + 2, :].rearrange("p h n -> p (h n)")

                def clamp_gate(k, last_chunk):
                    dve.wait_ge(used, last_chunk + 1)
                    if not (type(k) is int and k == 0):
                        dve.wait_ge(s_hid, k)
                    V.tensor_scalar(g_e, gate_ps, LIMIT, None, ALU.min).then_inc(s_gc, 1)

                def clamp_up(k):
                    V.tensor_scalar(u_e, up_ps, LIMIT, -LIMIT, ALU.min, ALU.max).then_inc(s_uc, 1)

                def hidden(k):
                    dve.wait_ge(s_uc, k + 1)
                    dve.wait_ge(s_gc, k + 1)
                    if not (type(k) is int and k == 0):
                        dve.wait_ge(s_htp, k)
                    V.scalar_tensor_tensor(hid, u_e, 1.0, g_e, ALU.add, ALU.mult).then_inc(s_prod, 1)
                    dve.wait_ge(s_prod, k + 1)
                    dve.wait_ge(s_sig, k + 1)
                    V.tensor_tensor(hid, hid, sig_e, ALU.mult).then_inc(s_hid, 1)

                def add_output(k, banks=(BK_OUT,) * TILES):
                    for i in range(TILES):
                        dve.wait_ge(s_sc, TILES * k + (i + 1))
                        if not (type(k) is int and k == 0):
                            dve.wait_ge(s_add, TILES * k + (i - TILES + 1))
                        V.tensor_tensor(acc[:, i, :], ps[:, banks[i]:banks[i] + 2, :].rearrange("p h n -> p (h n)"),
                                        acc[:, i, :], ALU.add).then_inc(s_add, 1)

                select(0, 0, rank)
                select(1, 1, rank)
                z = full("rank")
                link(V.tensor_copy(cntf[:, 0:E], z[:, TILES * E:(TILES + 1) * E]))
                link(V.tensor_reduce(cntf[:, E:E + 1], cntf[:, 0:E], AX_X, ALU.max))
                V.tensor_copy(counts[:, :], cntf[:, :]).then_inc(s_cnt, 1)
                V.tensor_copy(rnk2[:, :, :], rank[:, :, :]).then_inc(empt_v, 1)
                dve.wait_ge(empt_v, EV("rank"))
                take_inputs(0, 0)
                dve.wait_ge(s_exp, TILES)
                link(V.tensor_tensor(comb[:, :, :], comb[:, :, :], mask[:, :, :], ALU.mult))
                link(V.tensor_reduce(stat[:, 3:6], comb[:, :, :], AX_X, ALU.add))
                link(V.tensor_scalar(stat[:, 3:6], stat[:, 3:6], 1.0e-30, None, ALU.max))
                link(V.reciprocal(stat[:, 6:9], stat[:, 3:6]))
                for i in range(TILES):
                    ins = V.tensor_scalar(comb[:, i, :], comb[:, i, :], stat[:, 6 + i:7 + i], None, ALU.mult)
                link(ins)
                clamp_gate(0, 3)
                take_inputs(1, 1)
                clamp_up(0)
                hidden(0)
                select(2, 0, rank)
                select_weighted(0, 0, rank)

                def expert(e, b, selection=True):
                    clamp_gate(e, gu_chunk(e, 3))
                    take_inputs(e + 1, 1 - b)
                    clamp_up(e)
                    hidden(e)
                    add_output(e - 1)
                    if selection:
                        select(e + 2, b, rank)
                    select_weighted(e, b, rank)

                expert(1, 1)
                most = longest(dve)
                with dve.Fori(1, E // 2 - 1) as pair:
                    e = pair * 2
                    for b in range(2):
                        expert(e + b, b)
                expert(E - 2, 0, selection=False)
                clamp_gate(E - 1, gu_chunk(E - 1, 3))
                clamp_up(E - 1)
                hidden(E - 1)
                select_weighted(E - 1, 1, rank)
                add_output(E - 2, OUT_BANKS)
                add_output(E - 1, OUT_BANKS)

                def next_ranks(r):
                    dve.wait_ge(s_cnt, r)
                    V.tensor_scalar(rnk2[:, :, :], rnk2[:, :, :], -float(CAP), None, ALU.add).then_inc(s_cnt, 1)

                def piece(e, n, r):
                    k = E + n
                    dve.wait_ge(s_cnt, r + 1)
                    select(e, 0, rnk2)
                    take_inputs(k, 0)
                    clamp_gate(k, N_CHUNKS + 6 * n + 3)
                    clamp_up(k)
                    hidden(k)
                    select_weighted(e, 0, rnk2)
                    add_output(k)
                more_pieces(dve, most, piece, next_ranks)

                V.memset(stat[:, 12:13], 0.0).then_inc(s_sum, 1)
                dve.wait_ge(s_gfin, 16)
                for n, i in enumerate(TILE_ORDER):
                    inv = inverse_root(i, 2 * TILES + n + 1, 0)
                    V.scalar_tensor_tensor(h_tok[:, i, :], acc[:, i, :], inv, g_fin, ALU.mult, ALU.mult).then_inc(s_fin, 1)


_INS = ["x_prompt", "x_sample", "state_conv_a", "state_h", "state_conf", "g_mix", "w_in", "w_conv_a", "b_conv_a",
        "w_rg_a", "b_rg_a", "w_rg_x", "b_rg_x", "rg_lambda", "w_conf_dw", "b_conf_dw", "g_conf_ln", "b_conf_ln",
        "w_conf_pw", "b_conf_pw", "w_out", "g_ffn", "w_router", "b_router", "w_gate", "b_gate", "w_up", "b_up",
        "w_down", "b_down", "g_final"]
_OUTS = [(1, T_P, D), (SEQS, STEPS, D), (1, 1, HA, D), (1, 1, D), (1, 1, HC, D), (1, SEQS, HA, D), (1, SEQS, D),
         (1, SEQS, HC, D)]


def kernel(**inputs):
    import concourse.bacc as bacc
    from concourse.bass_utils import run_bass_kernel_spmd

    nc = bacc.Bacc("TRN2", target_bir_lowering=False, num_devices=1)
    arrays, given = {}, {}
    for name in _INS:
        a = np.ascontiguousarray(inputs[name])
        arrays[f"in_{name}"] = a
        given[name] = nc.dram_tensor(f"in_{name}", a.shape, mybir.dt.from_np(a.dtype), kind="ExternalInput").ap()
    outs = [nc.dram_tensor(f"out_{i}", shape, F32, kind="ExternalOutput").ap() for i, shape in enumerate(_OUTS)]
    build(nc, given, outs)
    r = run_bass_kernel_spmd(nc, [arrays], core_ids=[0])
    return tuple(r.results[0][f"out_{i}"] for i in range(len(_OUTS)))
```

```python
from contextlib import ExitStack

import numpy as np

import concourse.bass as bass
from concourse import mybir
from concourse.alu_op_type import AluOpType as ALU

ACT = mybir.ActivationFunctionType
F32 = mybir.dt.float32
BF16 = mybir.dt.bfloat16
I32 = mybir.dt.int32
AX_X = mybir.AxisListType.X

P = 128
D = 1024
NT = D // P
T_P = 256
SEQS, STEPS = 8, 4
T_S = SEQS * STEPS
T = T_P + T_S
TILES = 3
T_PAD = TILES * P
KA, KC = 4, 31
HA, HC = KA - 1, KC - 1
E = 32
CAP = 64
EPS = 1e-6
RG_C = 8.0
LIMIT, ALPHA = 7.0, 1.702

W_DW, W_CA, B_CA, B_RA, B_RX, LAM, B_DW, G_LN, B_LN, B_PW = 0, 31, 35, 36, 37, 38, 39, 40, 41, 42
N_PAR = 43

SLOTS = 6
SLOT = 4096
MIX_CHUNKS = 14

EARLY = E - 4
TILE_ORDER = (2, 0, 1)

BK_GU, BK_D, BK_X, BK_SEL, BK_HT, BK_OUT = 0, 2, 3, 4, 5, 6
OUT_BANKS = (BK_OUT, BK_GU, BK_SEL)


def mixer_jobs():
    jobs = [(f"hn{k}", "av"[k % 2]) for k in range(NT)]
    for c in range(NT):
        jobs += [(f"va{c}", "a"), (f"vb{c}", "a")]
        if c == 0:
            jobs += [("par", "v"), ("sta", "v")] + [(f"stc{i}", "a") for i in range(4)]
    jobs += [(f"xa{c}", "a") for c in range(NT)]
    jobs += [(f"ga{c}", "a") for c in range(4)]
    jobs += [(f"{n}{h}", "a") for n in ("vp", "vs", "xp", "xs") for h in range(2)]
    jobs += [(f"ga{c}", "a") for c in range(4, NT)]
    jobs += [("gb0", "a"), ("mean", "v")]
    jobs += [(f"gb{c}", "a") for c in (1, 2, 3)]
    jobs += [("var", "v")]
    jobs += [(f"gb{c}", "a") for c in (4, 5, 6, 7)]
    for c in range(NT):
        jobs += [(f"r{c}", "a"), (f"i{c}", "a")]
    jobs += [(f"pw{c}", "v") for c in range(NT)]
    jobs += [(f"ho{h}", "a") for h in range(2)]
    jobs += [(n, "v") for n in ("out2", "out00", "ht2a", "ht2b", "out01", "logits2", "out10", "ht0a", "ht0b", "out11",
                                "logits0", "ht1a", "ht1b", "logits1", "rank")]
    return jobs


JOBS = mixer_jobs()
JOB = {name: j for j, (name, _) in enumerate(JOBS)}


def emptied_before(j, who):
    return sum(w == who for _, w in JOBS[:j + 1])


def build(nc, A, O):
    with ExitStack() as ctx:
        def sb(name, shape, dt=F32):
            return ctx.enter_context(nc.sbuf_tensor(name, shape, dt))

        def sem(name):
            return ctx.enter_context(nc.semaphore(name))

        ring = sb("ring", [P, SLOTS, SLOT])
        acc = sb("acc", [P, TILES, D])
        par = sb("par", [P, NT, N_PAR])
        w_rg = sb("w_rg", [P, 2, NT, P])
        w_rt = sb("w_rt", [P, NT, E])
        b_rt = sb("b_rt", [P, E])
        g_mix = sb("g_mix_c", [P, NT])
        g_ffn = sb("g_ffn_c", [P, NT])
        ident = sb("ident", [P, P])
        ones = sb("ones", [P, P])
        slot_no = sb("slot_no", [P, CAP])
        tri = sb("tri", [P, P], BF16)
        ones_h = sb("ones_h", [P, P], BF16)
        h0 = sb("h0", [P, NT, SEQS])
        stat = sb("stat", [P, 8 * TILES])
        lamw = sb("lamw", [P, 6, NT])
        lg = sb("lg", [P, TILES, E + 4])
        lgr = sb("lgr", [P, TILES, E + 4])
        top = sb("top", [P, TILES, 8])
        mask = sb("mask", [P, TILES, E])
        mask_h = sb("mask_h", [P, TILES, E], BF16)
        comb = sb("comb", [P, TILES, E])
        rank = sb("rank", [P, TILES, E])
        rnk2 = sb("rnk2", [P, TILES, E])
        counts = sb("counts", [P, E + 1], I32)
        cntf = sb("cntf", [P, E + 1])

        WS = 21504
        ws = sb("ws", [P, WS])
        at = [0]

        def take(words):
            at[0] += words
            assert at[0] <= WS, at
            return ws[:, at[0] - words:at[0]]

        TW = NT * T
        XA_W, VX_W = HA + T_P + SEQS * (HA + STEPS), HC + T_P + SEQS * (HC + STEPS)
        hn_w = take(TW)
        xa_w = take(NT * XA_W)
        vx_w = take(NT * VX_W)
        ga_w = take(2 * TW)
        vc_w = take(TW)
        xc_w = take(TW)
        ig_w = take(TW)
        sg_w = take(2 * T)

        def by_tile(w, n=T):
            return w[:, 0:NT * n].rearrange("p (c t) -> p c t", c=NT)

        hn = by_tile(hn_w)
        xa = by_tile(xa_w, XA_W)
        vx = by_tile(vx_w, VX_W)
        gate_a = by_tile(ga_w[:, 0:TW])
        gate_b = by_tile(ga_w[:, TW:2 * TW])
        vc = by_tile(vc_w)
        xc = by_tile(xc_w)
        ig = by_tile(ig_w)
        sg = sg_w.rearrange("p (b t) -> p b t", b=2)
        rt = by_tile(vx_w)
        aa = by_tile(xa_w)
        mt = by_tile(ig_w)
        taps_s = xc_w[:, 0:2 * T_S * KC].rearrange("p (b s t j) -> p b s t j", b=2, s=SEQS, t=STEPS)
        x_tok = ga_w[:, 0:TILES * D].rearrange("p (i d) -> p i d", i=TILES)
        junk = vc_w[:, 0:D]
        par_rows = xc_w[:, 0:D]
        sta_rows = xc_w[:, D:2 * D]
        stc_rows = ig_w[:, 0:2 * D].rearrange("p (h d) -> p h d", h=2)
        st_v = ga_w[:, TW:TW + 2 * D].rearrange("p (b d) -> p b d", b=2)
        st_x = ig_w[:, 0:2 * D].rearrange("p (b d) -> p b d", b=2)
        v_new = ig_w[:, 2 * D:2 * D + NT * T_S].rearrange("p (c t) -> p c t", c=NT)
        xa_new = ga_w[:, TW + 2 * D:TW + 2 * D + NT * SEQS * HA].rearrange("p (c t) -> p c t", c=NT)
        silu = [vx_w[:, TW + c * T:TW + (c + 1) * T] for c in range(NT - 1)] + [sg_w[:, T:2 * T]]
        v_sum = xc_w[:, 2 * T_S * KC:2 * T_S * KC + T]
        v_sq = silu[0:NT - 1] + [sg_w[:, 0:T]]

        at[0] = 0
        h_tok = take(TILES * D).rearrange("p (i d) -> p i d", i=TILES)
        h_cm_w = take(NT * T_PAD)
        h_cm = h_cm_w.rearrange("p (k t) -> p k t", k=NT)
        spare = ws[:, 0:SLOT]
        g_fin = ws[:, SLOT:SLOT + D]
        w_rg_w = w_rg[:].rearrange("p m c n -> p (m c n)")
        h_split = take(3 * TILES * D // 2).bitcast(BF16).rearrange("p (s i d) -> p s i d", s=3, i=TILES)
        x_e = take(2 * NT * CAP).rearrange("p (b k s) -> p b k s", b=2, k=NT)
        hid_t_w = take(2 * NT * CAP)
        hid_t = hid_t_w.rearrange("p (b k s) -> p b k s", b=2, k=NT)
        st_h = hid_t_w[:, 0:D]
        y_e = take(D)
        first_gu = ws[:, at[0]:at[0] + SLOT]
        g_e = take(D)[0:CAP]
        sig_e = take(D)[0:CAP]
        u_e = take(D)[0:CAP]
        hid = take(D)[0:CAP]
        sel = take(2 * TILES * CAP // 2).bitcast(BF16).rearrange("p (b i s) -> p b i s", b=2, i=TILES)
        sel_w = take(TILES * 2 * CAP).rearrange("p (i d s) -> p i d s", i=TILES, d=2)
        sel_t = take(T_PAD)
        pick = take(2 * 3 * CAP).rearrange("p (b m s) -> p b m s", b=2, m=3)
        spare_row = take(D)
        at[0] = max(at[0], WS - D)
        bias = take(D)
        early_down = [w_rg_w[:, 0:D], w_rg_w[:, D:2 * D], ws[:, SLOT + D:SLOT + 2 * D], spare_row]
        early_down += [spare[:, k * D:(k + 1) * D] for k in range(4)]
        ps = ctx.enter_context(nc.psum_tensor("ps", [P, 8, 512], F32))

        def bank(j):
            return ps[:, j % 8, :]

        s_x = [sem(f"x{i}_loaded") for i in range(TILES)]
        s_par = sem("params_loaded")
        s_sta = sem("conv_a_and_h_state_loaded")
        s_stc = sem("conf_state_loaded")
        s_gain = sem("g_mix_loaded")
        s_rt = sem("router_and_g_ffn_loaded")
        s_bias = sem("bias_loaded")
        s_bz = sem("rows_without_bias_cleared")
        s_gfin = sem("g_final_loaded")
        s_early = sem("early_down_rows_loaded")
        s_first = sem("first_chunk_loaded")
        s_wrg = sem("gate_blocks_loaded")
        landed = [sem(f"slot{s}_landed") for s in range(SLOTS)]
        used = sem("chunks_used")
        filled = sem("psum_filled")
        empt_a = sem("psum_emptied_by_scalar")
        empt_v = sem("psum_emptied_by_vector")
        s_zero = sem("zeros_ready")
        s_const = sem("constants_ready")
        s_seed = sem("constant_seeds_ready")
        ord_v = sem("vector_order")
        ord_a = sem("scalar_order")
        s_sq = sem("squares_summed")
        s_ms = sem("mean_squares_ready")
        s_root = sem("roots_ready")
        s_xn = sem("x_normed")
        s_v = sem("v_ready")
        s_conv = sem("conf_conv_steps")
        s_tap = sem("sample_tap_products_ready")
        s_xc = sem("conv_a_steps")
        s_new = sem("new_columns_packed")
        s_store = sem("output_rows_stored")
        s_sqv = sem("centred_squared")
        s_vsum = sem("tiles_summed")
        s_vsq = sem("squares_summed_over_tiles")
        s_lam = sem("decay_exponent_ready")
        s_lexp = sem("decay_exponential_ready")
        s_sp = sem("decay_scales_ready")
        s_aw = sem("decay_and_tanh_ready")
        s_w = sem("tanh_used")
        s_rtt = sem("root_of_tanh_ready")
        s_hs = sem("states_ready")
        s_ln = sem("layer_norm_ready")
        s_sil = sem("silu_gate_ready")
        s_s = sem("silu_ready")
        s_m = sem("merged_ready")
        s_hn = sem("h_normed")
        s_split = sem("h_parts_cast")
        s_rest = sem("h_rest_ready")
        s_neg = sem("router_shift_ready")
        s_exp = sem("router_exponentials_ready")
        s_mask = sem("mask_ready")
        s_cnt = sem("counts_ready")
        s_sel = sem("selections_ready")
        s_selw = sem("weighted_selections_ready")
        s_pick = sem("gate_up_bias_picks_ready")
        s_pickd = sem("down_bias_picks_ready")
        s_xg = sem("piece_inputs_gathered")
        s_xe = sem("piece_inputs_in_sbuf")
        s_gc = sem("gate_clamped")
        s_uc = sem("up_clamped")
        s_gu0 = sem("first_gate_up_complete")
        s_dearly = sem("early_down_complete")
        s_sig = sem("gate_sigmoid_ready")
        s_prod = sem("gate_up_product_ready")
        s_hid = sem("hidden_ready")
        s_htp = sem("hidden_turned")
        s_hts = sem("hidden_t_in_sbuf")
        s_stp = sem("selection_turned")
        s_sts = sem("selection_t_in_sbuf")
        s_y = sem("piece_output_in_sbuf")
        s_sc = sem("output_spread_to_tokens")
        s_add = sem("output_added")
        s_sum = sem("output_complete")
        s_fin = sem("final_rows_ready")
        s_end = sem("results_stored")

        def flat(ap):
            n = len(ap.shape)
            return ap if n == 2 else ap.rearrange({3: "a b c -> (a b) c", 4: "a b c d -> (a b c) d"}[n])

        w_in = A["w_in"][0].rearrange("(p k) n -> p k n", k=NT)
        w_pw = A["w_conf_pw"][0].rearrange("(k p) n -> p k n", p=P)
        w_out = A["w_out"][0].rearrange("(k p) n -> p k n", p=P)
        w_gate = A["w_gate"][0].rearrange("e (p k) n -> e p (k n)", k=NT)
        w_up = A["w_up"][0].rearrange("e (p k) n -> e p (k n)", k=NT)
        w_down = A["w_down"][0].rearrange("e (p k) n -> e p (k n)", k=NT)
        HALF = SLOT // 2

        def slot_half(n, h):
            return ring[:, n % SLOTS, h * HALF:(h + 1) * HALF]

        def w_in_cols(n, h):
            if n < 4:
                return D + h * D + n * 256
            return [0, 0, 3 * D, 3 * D, 4 * D, 4 * D][n - 4] + (n % 2) * 512 + h * 256

        def later(e, n):
            return 2 if type(e) is int and e > n else 0

        def gu_chunk(e, q):
            return 6 * e - 3 + q - later(e, EARLY + 1)

        def d_chunk(e, q):
            return 6 * e + 7 + q - later(e, EARLY) - (4 if type(e) is int and e == E - 1 else 0)

        N_CHUNKS = d_chunk(E - 1, 1) + 1

        def slot_of(m):
            return (MIX_CHUNKS + m) % SLOTS

        def landed_by(m0, e=0):
            return 32 * ((MIX_CHUNKS + m0) // SLOTS + 1) + 32 * e

        LAST_FILL = ["vb1", "vb3", "vb5", "vb7", "xa3", "xa7", "ga3", "ga7", "gb3", "gb7", "pw7", "pw7", "out10", "out11"]
        EA = lambda name: emptied_before(JOB[name], "a")
        EV = lambda name: emptied_before(JOB[name], "v")
        CONV_MID = 2 * (KC // 2) + 4
        N_STORES = 16 * 14
        N_CONV, N_XC = NT * (KC + 2), 2 * NT * KA

        def longest(eng):
            eng.wait_ge(s_cnt, 1)
            return eng.value_load(counts[0:1, E:E + 1], min_val=0, max_val=T)

        def more_pieces(eng, most, piece, before=None, after=None):
            with eng.If(most > CAP):
                done = eng.alloc_register("pieces_done")
                eng.reg_mov(done, 0)
                with eng.Fori(1, -(-T // CAP)) as r:
                    if before is not None:
                        before(r)
                    with eng.Fori(0, E) as e:
                        count = eng.value_load(counts[0:1, bass.ds(e, 1)], min_val=0, max_val=T)
                        with eng.If(count > r * CAP):
                            piece(e, eng.snap(done), r)
                            eng.reg_add(done, done, 1)
                if after is not None:
                    after()

        with nc.Block() as block:

            @block.sync
            def _(sp):
                for i in range(2):
                    sp.dma_start(acc[:, i, :], A["x_prompt"][0, i * P:(i + 1) * P, :]).then_inc(s_x[i], 16)
                sp.wait_ge(s_zero, 1)
                sp.dma_start(acc[0:T_S, 2, :], flat(A["x_sample"])).then_inc(s_x[2], 16)
                for n in range(MIX_CHUNKS):
                    if n == 1:
                        sp.dma_start(sta_rows[0:SEQS * HA, :], flat(A["state_conv_a"][0])).then_inc(s_sta, 16)
                        sp.dma_start(sta_rows[SEQS * HA:SEQS * KA, :], A["state_h"][0]).then_inc(s_sta, 16)
                        sp.dma_start(stc_rows[0:SEQS * HC // 2],
                                     flat(A["state_conf"][0]).rearrange("(h p) d -> p h d", h=2)).then_inc(s_stc, 16)
                        sp.wait_ge(s_par, 160)
                    if n == 4:
                        for m, name in enumerate(("w_rg_a", "w_rg_x")):
                            sp.dma_start(w_rg[:, m], A[name][0].rearrange("n c d -> c n d")).then_inc(s_wrg, 16)
                        sp.dma_start(w_rt[:], A["w_router"][0].rearrange("(p k) e -> p k e", k=NT)).then_inc(s_rt, 16)
                        sp.dma_start(b_rt[:], A["b_router"].to_broadcast([P, E])).then_inc(s_rt, 16)
                        sp.dma_start(g_ffn[:], A["g_ffn"][0].rearrange("(p k) -> p k", k=NT)).then_inc(s_rt, 16)
                    if n >= SLOTS:
                        sp.wait_ge(filled, JOB[LAST_FILL[n - SLOTS]] + 1)
                    for h in range(2):
                        if n < 10:
                            c = w_in_cols(n, h)
                            dst = slot_half(n, h).rearrange("p (k n) -> p k n", k=NT)
                            sp.dma_start(dst, w_in[:, :, c:c + 256]).then_inc(landed[n % SLOTS], 16)
                        elif n < 12:
                            k = 4 * (n - 10) + 2 * h
                            dst = slot_half(n, h).rearrange("p (k n) -> p k n", k=2)
                            sp.dma_start(dst, w_pw[:, k:k + 2, :]).then_inc(landed[n % SLOTS], 16)
                        else:
                            dst = slot_half(n, h).rearrange("p (k n) -> p k n", k=4)
                            cols = slice((n - 12) * 512, (n - 11) * 512)
                            sp.dma_start(dst, w_out[:, 4 * h:4 * h + 4, cols]).then_inc(landed[n % SLOTS], 16)

                def load(e, m, slot, kind, q):
                    if type(m) is int and m < SLOTS:
                        sp.wait_ge(filled, JOB[LAST_FILL[MIX_CHUNKS - SLOTS + m]] + 1)
                    else:
                        sp.wait_ge(used, m - SLOTS + 1)
                    for h in range(2):
                        dst = ring[:, slot, h * HALF:(h + 1) * HALF]
                        if kind == "gu":
                            src = (w_gate, w_up)[h][e, :, q * HALF:(q + 1) * HALF]
                        else:
                            src = w_down[e, :, q * SLOT + h * HALF:q * SLOT + (h + 1) * HALF]
                        sp.dma_start(dst, src).then_inc(landed[slot], 16)

                def load_gu(e, q):
                    m = q - 1 if e == 0 else gu_chunk(e, q)
                    load(e, m, slot_of(m), "gu", q)

                load_gu(0, 1)
                sp.wait_ge(filled, JOB["i7"] + 1)
                for k in range(2):
                    sp.dma_start(early_down[k], w_down[EARLY, :, k * D:(k + 1) * D]).then_inc(s_early, 16)
                load_gu(0, 2)
                load_gu(0, 3)
                load_gu(1, 0)
                sp.wait_ge(filled, JOB["ho1"] + 1)
                sp.wait_ge(s_m, NT)
                for h in range(2):
                    sp.dma_start(first_gu[:, h * HALF:(h + 1) * HALF], (w_gate, w_up)[h][0, :, 0:HALF]).then_inc(s_first, 16)
                load_gu(1, 1)
                sp.wait_ge(filled, JOB["out11"] + 1)
                for m, name in enumerate(("b_gate", "b_up", "b_down")):
                    sp.dma_start(bias[m * E:(m + 1) * E, :], A[name][0]).then_inc(s_bias, 16)
                load_gu(1, 2)
                def load_early(k):
                    sp.dma_start(early_down[k], w_down[EARLY, :, k * D:(k + 1) * D]).then_inc(s_early, 16)

                load_early(3)
                sp.wait_ge(filled, JOB["logits1"] + 1)
                load_early(2)
                sp.wait_ge(s_split, 3 * TILES)
                for h in range(2):
                    sp.dma_start(spare[:, h * HALF:(h + 1) * HALF],
                                 w_down[EARLY, :, SLOT + h * HALF:SLOT + (h + 1) * HALF]).then_inc(s_early, 16)
                load_gu(1, 3)
                for q in range(2):
                    load(0, d_chunk(0, q), slot_of(d_chunk(0, q)), "d", q)
                most = longest(sp)
                with sp.Fori(2, EARLY + 1) as e:
                    for q in range(4):
                        load(e, gu_chunk(e, q), slot_of(gu_chunk(2, q)), "gu", q)
                    for q in range(2):
                        load(e - 1, d_chunk(e - 1, q), slot_of(d_chunk(1, q)), "d", q)
                for e in range(EARLY + 1, E):
                    for q in range(4):
                        load_gu(e, q)
                    for q in range(2 if e - 1 != EARLY else 0):
                        load(e - 1, d_chunk(e - 1, q), slot_of(d_chunk(e - 1, q)), "d", q)
                for q in range(2):
                    load(E - 1, d_chunk(E - 1, q), slot_of(d_chunk(E - 1, q)), "d", q)

                def load_piece(e, n, r):
                    for q in range(6):
                        load(e, N_CHUNKS + 6 * n + q, slot_of(N_CHUNKS + q), "gu" if q < 4 else "d", q % 4)
                more_pieces(sp, most, load_piece, after=lambda: sp.wait_ge(s_fin, 2 * TILES))
                for i in range(TILES):
                    sp.wait_ge(s_fin, i + 1)
                    dst = O[0][0, i * P:(i + 1) * P, :] if i < 2 else flat(O[1])
                    sp.dma_start(dst, h_tok[0:min(P, T - i * P), i, :]).then_inc(s_end, 16)
                sp.wait_ge(s_end, 48)

            @block.gpsimd
            def _(pool):
                pool.memset(ident[:], 0.0).then_inc(s_seed, 1)
                pool.memset(tri[:], 1.0).then_inc(s_seed, 1)
                pool.memset(ones[:], 1.0 / D).then_inc(s_const, 1)
                pool.memset(ones_h[:], 1.0).then_inc(s_const, 1)
                pool.wait_ge(s_seed, 1)
                pool.affine_select(out=ident[:], in_=ident[:], compare_op=ALU.not_equal, fill=1.0, base=0,
                                   pattern=[[-1, P]], channel_multiplier=1).then_inc(s_const, 1)
                pool.wait_ge(s_seed, 2)
                pool.affine_select(out=tri[:], in_=tri[:], compare_op=ALU.is_gt, fill=0.0, base=0,
                                   pattern=[[1, P]], channel_multiplier=-1).then_inc(s_const, 1)
                pool.iota(slot_no[:], [[1, CAP]], base=0, channel_multiplier=0,
                          allow_small_or_imprecise_dtypes=True).then_inc(s_const, 1)
                for name, r, n in (("w_conf_dw", W_DW, KC), ("w_conv_a", W_CA, KA), ("b_conv_a", B_CA, 1),
                                   ("b_rg_a", B_RA, 1), ("b_rg_x", B_RX, 1), ("rg_lambda", LAM, 1), ("b_conf_dw", B_DW, 1),
                                   ("g_conf_ln", G_LN, 1), ("b_conf_ln", B_LN, 1), ("b_conf_pw", B_PW, 1)):
                    pool.dma_start(par_rows[r:r + n, :], A[name][0] if n > 1 else A[name]).then_inc(s_par, 16)
                for c in range(0, NT, 2):
                    for cc in (c, c + 1):
                        pool.wait_ge(empt_a, EA(f"vb{cc}"))
                        v = vx[:, cc, HC:HC + T_P]
                        pool.tensor_tensor(v, v, sg[:, cc % 2, 0:T_P], ALU.mult).then_inc(s_v, 1)
                        v = vx[:, cc, HC + T_P:].rearrange("p (s t) -> p s t", s=SEQS)[:, :, HC:]
                        pool.tensor_tensor(v, v, sg[:, cc % 2, T_P:].rearrange("p (s t) -> p s t", s=SEQS),
                                           ALU.mult).then_inc(s_v, 1)
                    if c == 0:
                        pool.wait_ge(empt_v, EV("par"))
                        pool.wait_ge(empt_a, EA("stc3"))
                        pool.wait_ge(filled, JOB["sta"] + 1)
                    else:
                        pool.wait_ge(s_conv, (c - 2) * (KC + 2) + CONV_MID)
                    for cc in (c, c + 1):
                        pool.wait_ge(s_v, 2 * cc + 2)
                        v = vx[:, cc, HC + T_P:].rearrange("p (s t) -> p s t", s=SEQS)
                        w = par[:, cc, W_DW:W_DW + KC].unsqueeze(1).to_broadcast([P, SEQS, KC])
                        for t in range(STEPS):
                            ins = pool.tensor_tensor(taps_s[:, cc % 2, :, t, :], v[:, :, t:t + KC], w, ALU.mult)
                        ins.then_inc(s_tap, 1)
                pool.dma_start(O[7][0][:, 0:HC - STEPS, :], A["state_conf"][0][:, STEPS:HC, :]).then_inc(s_store, 16)
                pool.wait_ge(s_v, 2 * NT)
                pool.tensor_copy(v_new.rearrange("p c (s t) -> p c s t", s=SEQS),
                                 vx[:, :, HC + T_P:].rearrange("p c (s t) -> p c s t", s=SEQS)[:, :, :, HC:]).then_inc(s_new, 1)
                pool.wait_ge(empt_a, EA("xa7"))
                pool.tensor_copy(xa_new.rearrange("p c (s t) -> p c s t", s=SEQS),
                                 xa[:, :, HA + T_P:].rearrange("p c (s t) -> p c s t", s=SEQS)[:, :, :, STEPS:]).then_inc(s_new, 1)
                pool.wait_ge(empt_a, EA("vp1"))
                pool.dma_start(flat(O[4][0]), st_v[0:HC, 0, :]).then_inc(s_store, 16)
                pool.wait_ge(empt_a, EA("vs1"))
                for s in range(SEQS):
                    pool.dma_start(O[7][0][s, HC - STEPS:, :], st_v[s * STEPS:(s + 1) * STEPS, 1, :]).then_inc(s_store, 16)
                pool.wait_ge(empt_a, EA("xp1"))
                pool.dma_start(flat(O[2][0]), st_x[0:HA, 0, :]).then_inc(s_store, 16)
                pool.wait_ge(empt_a, EA("xs1"))
                pool.dma_start(flat(O[5][0]), st_x[0:SEQS * HA, 1, :]).then_inc(s_store, 16)
                for c in range(1, NT):
                    if c == 1 or c % 2 == 0:
                        pool.wait_ge(s_conv, (c // 2 + 1) * 2 * (KC + 2))
                    if c > 1:
                        pool.wait_ge(s_vsum, c - 1)
                    pool.tensor_tensor(v_sum, vc[:, 0, :] if c == 1 else v_sum, vc[:, c, :], ALU.add).then_inc(s_vsum, 1)
                for c in range(1, NT):
                    pool.wait_ge(s_sqv, c + 1)
                    if c > 1:
                        pool.wait_ge(s_vsq, c - 1)
                    pool.tensor_tensor(v_sq[0], v_sq[0], v_sq[c], ALU.add).then_inc(s_vsq, 1)
                pool.wait_ge(empt_a, EA("ho1"))
                pool.dma_start(O[3][0], st_h[0:1, :]).then_inc(s_store, 16)
                pool.dma_start(O[6][0], st_h[1:1 + SEQS, :]).then_inc(s_store, 16)
                for n, i in enumerate(TILE_ORDER):
                    if n == 2:
                        pool.wait_ge(filled, JOB["out11"] + 1)
                        pool.wait_ge(s_rest, 4)
                        pool.memset(bias[3 * E:, :], 0.0).then_inc(s_bz, 1)
                        pool.wait_ge(s_bz, 1)
                    pool.wait_ge(filled, JOB[f"ht{i}b"] + 1)
                    for s in range(2):
                        pool.wait_ge(s_split, 3 * n + s + 1)
                        pool.tensor_tensor(h_tok[:, i, :], h_tok[:, i, :], h_split[:, s, i, :], ALU.subtract).then_inc(s_rest, 1)
                pool.wait_ge(filled, JOB["logits1"] + 1)
                pool.dma_start(g_fin, A["g_final"].rearrange("(a d) -> a d", a=1).to_broadcast([P, D])).then_inc(s_gfin, 16)
                pool.wait_ge(s_store, N_STORES)

            @block.scalar
            def _(act):
                act.dma_start(g_mix[:], A["g_mix"][0].rearrange("(p k) -> p k", k=NT)).then_inc(s_gain, 16)
                act.wait_ge(s_const, 1)
                act.activation(stat[:, 8 * TILES - 1:], ones[:, 0:1], ACT.Sqrt)
                def empty(name):
                    act.wait_ge(filled, JOB[name] + 1)
                    return bank(JOB[name])

                def square(i, dst, sums):
                    act.activation(dst, acc[:, i, :], ACT.Square, accum_out=stat[:, sums + i:sums + i + 1]).then_inc(s_sq, 1)

                def root(i, n, means):
                    act.wait_ge(s_ms, n)
                    act.activation(stat[:, means + 3 + i:means + 4 + i], stat[:, means + i:means + i + 1],
                                   ACT.Sqrt).then_inc(s_root, 1)

                for i in range(TILES):
                    act.wait_ge(s_x[i], 16)
                    if i:
                        act.wait_ge(s_sq, i)
                    square(i, junk, 0)
                    root(i, i + 1, 3)
                act.wait_ge(s_gain, 16)
                for k in range(0, NT, 2):
                    act.activation(hn[:, k, :], empty(f"hn{k}")[:, 0:T], ACT.Copy, scale=g_mix[:, k:k + 1]).then_inc(empt_a, 1)
                for c in range(NT):
                    z = empty(f"va{c}")
                    act.copy(vx[:, c, HC:HC + T_P], z[:, 0:T_P])
                    act.copy(vx[:, c, HC + T_P:].rearrange("p (s t) -> p s t", s=SEQS)[:, :, HC:],
                             z[:, T_P:T].rearrange("p (s t) -> p s t", s=SEQS)).then_inc(empt_a, 1)
                    z = empty(f"vb{c}")
                    if c >= 2:
                        act.wait_ge(s_v, 2 * c - 2)
                    act.activation(sg[:, c % 2, :], z[:, 0:T], ACT.Sigmoid).then_inc(empt_a, 1)
                    if c == 0:
                        for i in range(4):
                            z = empty(f"stc{i}")
                            for h in range(2):
                                dst = vx[:, 2 * i + h, HC + T_P:].rearrange("p (s t) -> p s t", s=SEQS)[:, :, 0:HC]
                                ins = act.copy(dst, z[:, h * SEQS * HC:(h + 1) * SEQS * HC].rearrange("p (s t) -> p s t", s=SEQS))
                            ins.then_inc(empt_a, 1)
                        act.wait_ge(s_lam, 1)
                        act.activation(lamw[:, 1, :], lamw[:, 0, :], ACT.Exp, scale=-1.0).then_inc(s_lexp, 1)
                for c in range(NT):
                    z = empty(f"xa{c}")
                    act.copy(xa[:, c, HA:HA + T_P], z[:, 0:T_P])
                    act.copy(xa[:, c, HA + T_P:].rearrange("p (s t) -> p s t", s=SEQS)[:, :, HA:],
                             z[:, T_P:T].rearrange("p (s t) -> p s t", s=SEQS)).then_inc(empt_a, 1)
                for c in range(4):
                    act.activation(gate_a[:, c, :], empty(f"ga{c}")[:, 0:T], ACT.Sigmoid).then_inc(empt_a, 1)
                for name, st, b, r in (("vp", st_v, 0, HC), ("vs", st_v, 1, T_S), ("xp", st_x, 0, HA),
                                       ("xs", st_x, 1, SEQS * HA)):
                    for h in range(2):
                        act.copy(st[0:r, b, h * 512:(h + 1) * 512], empty(f"{name}{h}")[0:r, :]).then_inc(empt_a, 1)
                for c in range(4, NT):
                    act.activation(gate_a[:, c, :], empty(f"ga{c}")[:, 0:T], ACT.Sigmoid).then_inc(empt_a, 1)
                act.wait_ge(empt_v, EV("mean"))
                for c in range(NT):
                    act.activation(v_sq[c], vc[:, c, :], ACT.Square).then_inc(s_sqv, 1)
                act.wait_ge(s_store, N_STORES - 32)
                for c in range(4):
                    act.activation(gate_b[:, c, :], empty(f"gb{c}")[:, 0:T], ACT.Sigmoid).then_inc(empt_a, 1)
                act.wait_ge(empt_v, EV("var"))
                act.activation(sg[:, 1, :], sg[:, 0, :], ACT.Sqrt).then_inc(s_root, 1)
                act.wait_ge(s_ln, 1)
                for c in range(NT):
                    act.activation(silu[c], vc[:, c, :], ACT.Sigmoid, scale=par[:, c, G_LN:G_LN + 1],
                                   bias=par[:, c, B_LN:B_LN + 1]).then_inc(s_sil, 1)
                for c in (4, 5, 6, 7):
                    act.activation(gate_b[:, c, :], empty(f"gb{c}")[:, 0:T], ACT.Sigmoid).then_inc(empt_a, 1)
                for c in range(NT):
                    act.activation(rt[:, c, :], empty(f"r{c}")[:, 0:T], ACT.Sigmoid,
                                   bias=par[:, c, B_RA:B_RA + 1]).then_inc(empt_a, 1)
                    act.activation(ig[:, c, :], empty(f"i{c}")[:, 0:T], ACT.Sigmoid,
                                   bias=par[:, c, B_RX:B_RX + 1]).then_inc(empt_a, 1)
                act.wait_ge(s_xc, N_XC)
                act.wait_ge(s_sp, 1)
                act.wait_ge(empt_a, EA(f"i{NT - 1}"))
                for c in range(NT):
                    act.activation(aa[:, c, :], rt[:, c, :], ACT.Exp, scale=lamw[:, 4, c:c + 1]).then_inc(ord_a, 1)
                for c in range(NT):
                    act.wait_ge(ord_a, NT)
                    act.activation(rt[:, c, :], rt[:, c, :], ACT.Tanh, scale=lamw[:, 5, c:c + 1]).then_inc(s_aw, 1)
                act.wait_ge(s_w, 1)
                act.activation(rt[:, :, :], rt[:, :, :], ACT.Sqrt).then_inc(s_rtt, 1)
                act.wait_ge(s_m, NT)
                for h in range(2):
                    act.copy(st_h[0:1 + SEQS, h * 512:(h + 1) * 512], empty(f"ho{h}")[0:1 + SEQS, :]).then_inc(empt_a, 1)

                for n, i in enumerate(TILE_ORDER):
                    act.wait_ge(empt_v, EV(f"out{i}1" if i < 2 else "out2"))
                    square(i, h_tok[:, i, :], 12)
                    root(i, TILES + n + 1, 15)
                    act.wait_ge(s_hn, n + 1)
                    for s in range(3):
                        if s:
                            act.wait_ge(s_rest, 2 * n + s)
                        act.copy(h_split[:, s, i, :], h_tok[:, i, :]).then_inc(s_split, 1)
                for n, i in enumerate(TILE_ORDER):
                    act.wait_ge(s_neg, n + 1)
                    act.activation(comb[:, i, :], lg[:, i, 0:E], ACT.Exp, bias=stat[:, i:i + 1]).then_inc(s_exp, 1)

                def turned(k, b):
                    act.wait_ge(s_htp, k + 1)
                    act.copy(hid_t[:, b, :, :], ps[:, BK_HT, :].rearrange("p (k s) -> p k s", k=NT)).then_inc(s_hts, 1)

                def sigmoid(k):
                    act.wait_ge(s_gc, k + 1)
                    if not (type(k) is int and k == 0):
                        act.wait_ge(s_hid, k)
                    act.activation(sig_e, g_e, ACT.Sigmoid, scale=ALPHA).then_inc(s_sig, 1)

                def selection(g):
                    act.wait_ge(s_stp, g + 1)
                    act.copy(sel_t, ps[:, BK_SEL, 0:T_PAD]).then_inc(s_sts, 1)

                def output(k, d, last_chunk, bk=BK_D):
                    if type(k) is int and k == EARLY:
                        act.wait_ge(s_dearly, 1)
                    else:
                        act.wait_ge(used, last_chunk + 1)
                    for h in range(2):
                        ins = act.copy(y_e[d * CAP:(d + 1) * CAP, h * 512:(h + 1) * 512], ps[h * CAP:(h + 1) * CAP, bk, :])
                    ins.then_inc(s_y, 1)

                sigmoid(0)
                act.wait_ge(s_store, N_STORES)
                turned(0, 0)
                sigmoid(1)
                output(0, 0, d_chunk(0, 1))

                def expert(e, b, pair):
                    if b == 0:
                        selection(pair - 1)
                    turned(e - 1, 1 - b)
                    sigmoid(e)
                    if type(e) is not int or e < E - 1:
                        output(e - 1, 1 - b, d_chunk(e - 1, 1))

                most = longest(act)
                with act.Fori(1, EARLY // 2) as pair:
                    for b in range(2):
                        expert(pair * 2 + b, b, pair)
                for e in range(EARLY, E):
                    expert(e, e % 2, e // 2)
                selection(E // 2 - 1)
                turned(E - 1, 1)
                output(E - 2, 0, d_chunk(E - 2, 1))
                output(E - 1, 1, d_chunk(E - 1, 1), BK_X)

                def piece(e, n, r):
                    sigmoid(E + n)
                    selection(E // 2 + n)
                    turned(E + n, 0)
                    output(E + n, 0, N_CHUNKS + 6 * n + 5)
                for i in range(TILES):
                    act.wait_ge(s_add, TILES * (E // 2 - 1) + i + 1)
                    square(i, h_tok[:, i, :], 0)
                    if i:
                        root(i - 1, 2 * TILES + i, 3)
                root(TILES - 1, 3 * TILES, 3)

                def norm_again():
                    act.wait_ge(s_sum, 1)
                    for i in range(TILES):
                        square(i, h_tok[:, i, :], 0)
                        root(i, 3 * TILES + i + 1, 3)
                more_pieces(act, most, piece, after=norm_again)

            @block.tensor
            def _(pe):
                def fill(name):
                    j = JOB[name]
                    if j >= 8:
                        if emptied_before(j - 8, "a"):
                            pe.wait_ge(empt_a, emptied_before(j - 8, "a"))
                        if emptied_before(j - 8, "v"):
                            pe.wait_ge(empt_v, emptied_before(j - 8, "v"))
                    return bank(j)

                def turn(dst, src):
                    k = src.shape[0]
                    return nc.tensor.transpose(dst, src, ident[0:k, 0:k])

                pe.wait_ge(s_const, 5)
                pe.wait_ge(s_xn, TILES)
                for k in range(NT):
                    z = fill(f"hn{k}")
                    for i in range(TILES):
                        n = min(P, T - i * P)
                        ins = turn(z[:, i * P:i * P + n], x_tok[0:n, i, k::NT])
                    ins.then_inc(filled, 1)

                def w_in_job(name, n, h, i):
                    w = slot_half(n, h).rearrange("p (k n) -> p k n", k=NT)
                    z = fill(name)
                    for k in range(NT):
                        ins = nc.tensor.matmul(z[:, 0:T], w[:, k, i * P:(i + 1) * P], hn[:, k, :],
                                               start=(k == 0), stop=(k == NT - 1))
                    ins.then_inc(filled, 1)

                def turn_rows():
                    pe.wait_ge(s_par, 160)
                    z = fill("par")
                    for c in range(NT):
                        ins = turn(z[:, c * N_PAR:(c + 1) * N_PAR], par_rows[0:N_PAR, c * P:(c + 1) * P])
                    ins.then_inc(filled, 1)
                    pe.wait_ge(s_sta, 32)
                    z = fill("sta")
                    for c in range(NT):
                        ins = turn(z[:, c * 32:(c + 1) * 32], sta_rows[0:32, c * P:(c + 1) * P])
                    ins.then_inc(filled, 1)
                    pe.wait_ge(s_stc, 16)
                    rows = SEQS * HC // 2
                    for i in range(4):
                        z = fill(f"stc{i}")
                        for c in range(2):
                            for h in range(2):
                                src = stc_rows[0:rows, h, (2 * i + c) * P:(2 * i + c + 1) * P]
                                ins = turn(z[:, (2 * c + h) * rows:(2 * c + h + 1) * rows], src)
                        ins.then_inc(filled, 1)

                pe.wait_ge(empt_a, EA("hn6"))
                pe.wait_ge(empt_v, EV("hn7"))
                for n in range(4):
                    pe.wait_ge(landed[n % SLOTS], 32 * (n // SLOTS + 1))
                    for i in range(2):
                        w_in_job(f"va{2 * n + i}", n, 0, i)
                        w_in_job(f"vb{2 * n + i}", n, 1, i)
                        if n == 0 and i == 0:
                            turn_rows()

                def w_in_block(name, n0, tiles=range(NT)):
                    for c in tiles:
                        n = n0 + c // 4
                        pe.wait_ge(landed[n % SLOTS], 32 * (n // SLOTS + 1))
                        w_in_job(f"{name}{c}", n, c % 4 // 2, c % 2)

                w_in_block("xa", 4)
                w_in_block("ga", 6, range(4))
                pe.wait_ge(s_v, 2 * NT)
                pe.wait_ge(s_new, 2)
                for name, r, src in (("vp", HC, lambda c: vx[:, c, T_P:T_P + HC]),
                                     ("vs", T_S, lambda c: v_new[:, c, :]),
                                     ("xp", HA, lambda c: xa[:, c, T_P:T_P + HA]),
                                     ("xs", SEQS * HA, lambda c: xa_new[:, c, :])):
                    for h in range(2):
                        z = fill(f"{name}{h}")
                        for c in range(4):
                            ins = turn(z[0:r, c * P:(c + 1) * P], src(4 * h + c))
                        ins.then_inc(filled, 1)
                w_in_block("ga", 6, range(4, NT))
                w_in_block("gb", 8, (0,))
                pe.wait_ge(s_vsum, NT - 1)
                nc.tensor.matmul(fill("mean")[:, 0:T], ones[:], v_sum, start=True, stop=True).then_inc(filled, 1)
                w_in_block("gb", 8, (1, 2, 3))
                z = fill("var")
                pe.wait_ge(s_vsq, NT - 1)
                nc.tensor.matmul(z[:, 0:T], ones[:], v_sq[0], start=True, stop=True).then_inc(filled, 1)
                w_in_block("gb", 8, (4, 5, 6, 7))
                pe.wait_ge(s_xc, N_XC)
                pe.wait_ge(s_wrg, 32)
                for c in range(NT):
                    for m, name in enumerate(("r", "i")):
                        z = fill(f"{name}{c}")
                        nc.tensor.matmul(z[:, 0:T], w_rg[:, m, c, :], xc[:, c, :], start=True, stop=True).then_inc(filled, 1)
                for n in (10, 11):
                    pe.wait_ge(landed[n % SLOTS], 32 * (n // SLOTS + 1))
                pe.wait_ge(s_s, NT)
                w4 = [slot_half(10 + k // 4, k % 4 // 2).rearrange("p (k n) -> p k n", k=2)[:, k % 2] for k in range(NT)]
                for c in range(NT):
                    z = fill(f"pw{c}")
                    for k in range(NT):
                        ins = nc.tensor.matmul(z[:, 0:T], w4[k][:, c * P:(c + 1) * P], vc[:, k, :],
                                               start=(k == 0), stop=(k == NT - 1))
                    ins.then_inc(filled, 1)
                pe.wait_ge(s_hs, 1)
                for h in range(2):
                    z = fill(f"ho{h}")
                    for c in range(4):
                        ins = turn(z[0:1 + SEQS, c * P:(c + 1) * P], xc[:, 4 * h + c, T_P - 1::STEPS])
                    ins.then_inc(filled, 1)
                for n in (12, 13):
                    pe.wait_ge(landed[n % SLOTS], 32 * (n // SLOTS + 1))

                def w_out_cols(k, h):
                    return slot_half(12 + h, k // 4).rearrange("p (k n) -> p k n", k=4)[:, k % 4]

                pe.wait_ge(s_m, NT)

                def out_rows(i, halves=(0, 1)):
                    for h in halves:
                        z = fill(f"out{i}{h}")
                        for k in range(NT):
                            ins = nc.tensor.matmul(z[:, :], mt[:, k, i * P:(i + 1) * P], w_out_cols(k, h),
                                                   start=(k == 0), stop=(k == NT - 1))
                        ins.then_inc(filled, 1)

                def keep_warm(z, n):
                    for _ in range(n):
                        nc.tensor.matmul(z[:, 0:P], ident[:], ident[:], start=True, stop=True)

                def turn_h(i, warm=0):
                    keep_warm(fill(f"ht{i}a"), warm)
                    pe.wait_ge(s_hn, TILE_ORDER.index(i) + 1)
                    for h in range(2):
                        z = fill(f"ht{i}{'ab'[h]}")
                        for k in range(4):
                            ins = turn(z[:, k * P:(k + 1) * P], h_tok[:, i, 4 * h + k::NT])
                        ins.then_inc(filled, 1)

                def logits(i, warm=0):
                    pe.wait_ge(s_rt, 48)
                    z = fill(f"logits{i}")
                    keep_warm(z, warm)
                    for k in range(NT):
                        if k % 4 == 0:
                            pe.wait_ge(empt_v, EV(f"ht{i}{'ab'[k // 4]}"))
                        ins = nc.tensor.matmul(z[:, 0:E], h_cm[:, k, i * P:(i + 1) * P], w_rt[:, k, :],
                                               start=(k == 0), stop=(k == NT - 1))
                    ins.then_inc(filled, 1)

                z = fill("out2")
                for k in range(NT):
                    for c in range(4):
                        ins = nc.tensor.matmul(z[c * T_S:(c + 1) * T_S, 0:256], mt[:, k, 2 * P:T],
                                               w_out_cols(k, c // 2)[:, c % 2 * 256:(c % 2 + 1) * 256],
                                               start=(k == 0), stop=(k == NT - 1))
                ins.then_inc(filled, 1)
                out_rows(0, (0,))
                turn_h(2)
                out_rows(0, (1,))
                logits(2)
                out_rows(1, (0,))
                turn_h(0)
                out_rows(1, (1,))
                logits(0)
                turn_h(1, 8)
                logits(1, 5)
                z = fill("rank")
                keep_warm(z, 7)
                pe.wait_ge(s_mask, TILES)
                for i in range(TILES + 1):
                    for j in range(min(i + 1, TILES)):
                        before = ones_h if j < i else tri
                        ins = nc.tensor.matmul(z[:, i * E:(i + 1) * E], before[:], mask_h[:, j, :],
                                               start=(j == 0), stop=(j == min(i, TILES - 1)))
                ins.then_inc(filled, 1)

                def gather(k, b):
                    pe.wait_ge(s_sel, k + 1)
                    if not (type(k) is int and k == 0):
                        pe.wait_ge(s_xe, k)
                    for t in range(NT):
                        n = 0
                        for s in range(3):
                            for i in range(TILES):
                                ins = nc.tensor.matmul(ps[:, BK_X, t * CAP:(t + 1) * CAP], h_split[:, s, i, t::NT],
                                                       sel[:, b, i, :], start=(n == 0), stop=(n == 3 * TILES - 1))
                                n += 1
                    ins.then_inc(s_xg, 1)

                def gate_up_bias(k, b, bk=BK_GU):
                    pe.wait_ge(s_pick, k + 1)
                    if not (type(k) is int and k < 2):
                        pe.wait_ge(s_gc, k)
                        pe.wait_ge(s_uc, k)
                    for h in range(2):
                        for m in range(2):
                            nc.tensor.matmul(ps[m * CAP:(m + 1) * CAP, bk + h, :], pick[:, b, m, :],
                                             bias[:, h * 512:(h + 1) * 512], start=True, stop=False)

                def gate_up_rows(b, q, w, last=False, bk=BK_GU):
                    w = w.rearrange("p (m k n) -> p m k n", m=2, k=2)
                    for t in range(2):
                        for h in range(2):
                            for m in range(2):
                                ins = nc.tensor.matmul(ps[m * CAP:(m + 1) * CAP, bk + h, :], x_e[:, b, 2 * q + t, :],
                                                       w[:, m, t, h * 512:(h + 1) * 512],
                                                       start=False, stop=(last and t == 1))
                    return ins

                def gate_up_chunk(b, q, slot, fill, bk=BK_GU, last=None):
                    pe.wait_ge(landed[slot], fill)
                    gate_up_rows(b, q, ring[:, slot, :], q == 3 if last is None else last, bk).then_inc(used, 1)

                def gate_up(k, b, slots, fills, spread=None, early_waits=None):
                    gate_up_bias(k, b)
                    pe.wait_ge(s_xe, k + 1)
                    for q in range(4):
                        gate_up_chunk(b, q, slots[q], fills[q])
                        if spread is not None and q < TILES:
                            if q == TILES - 1:
                                early_waits()
                            spread(q)

                def turn_selection(k, g):
                    pe.wait_ge(s_selw, k + 1)
                    if not (type(g) is int and g == 0):
                        pe.wait_ge(s_sts, g)
                    for i in range(TILES):
                        ins = turn(ps[:, BK_SEL, i * P:(i + 1) * P], sel_w[:, i].rearrange("p d s -> p (d s)"))
                    ins.then_inc(s_stp, 1)

                def hidden_ready(k):
                    pe.wait_ge(s_hid, k + 1)
                    if not (type(k) is int and k == 0):
                        pe.wait_ge(s_hts, k)

                def turn_hidden(k):
                    for t in range(NT):
                        ins = turn(ps[:, BK_HT, t * CAP:(t + 1) * CAP], hid[:, t::NT])
                    ins.then_inc(s_htp, 1)

                def down_bias(k, b, bk=BK_D):
                    pe.wait_ge(s_hts, k + 1)
                    pe.wait_ge(s_pickd, k + 1)
                    if not (type(k) is int and k == 0):
                        if bk == BK_D:
                            pe.wait_ge(s_y, k)
                        else:
                            pe.wait_ge(s_xe, k + 1)
                    for h in range(2):
                        nc.tensor.matmul(ps[h * CAP:(h + 1) * CAP, bk, :], pick[:, b, 2, :],
                                         bias[:, h * 512:(h + 1) * 512], start=True, stop=False)

                def down_rows(b, k0, rows, bk=BK_D):
                    for k, w in enumerate(rows, k0):
                        for h in range(2):
                            ins = nc.tensor.matmul(ps[h * CAP:(h + 1) * CAP, bk, :], hid_t[:, b, k, :],
                                                   w[:, h * 512:(h + 1) * 512], start=False, stop=(k == NT - 1))
                    return ins

                def down_chunk(b, q, slot, fill, bk=BK_D):
                    pe.wait_ge(landed[slot], fill)
                    down_rows(b, 4 * q, [ring[:, slot, t * D:(t + 1) * D] for t in range(4)], bk).then_inc(used, 1)

                def down(k, b, slots, fills):
                    down_bias(k, b)
                    for q in range(2):
                        down_chunk(b, q, slots[q], fills[q])

                def spread_tile(k, g, i, rows=P, bk=None):
                    if i == 0:
                        pe.wait_ge(s_y, k + 1)
                        pe.wait_ge(s_sts, g + 1)
                    if bk is None:
                        bk = BK_OUT
                        if not (type(g) is int and g == 0 and i == 0):
                            pe.wait_ge(s_add, TILES * g + i)
                    for h in range(2):
                        ins = nc.tensor.matmul(ps[:, bk + h, :], sel_t[0:rows, i * P:(i + 1) * P],
                                               y_e[0:rows, h * 512:(h + 1) * 512], start=True, stop=True)
                    ins.then_inc(s_sc, 1)

                def slots_from(m0, n):
                    return [slot_of(m0 + q) for q in range(n)]

                def fills_from(m0, n, e=0):
                    return [landed_by(m0 + q, e) for q in range(n)]

                assert JOB["rank"] % 8 != BK_X
                pe.wait_ge(empt_v, EV("logits1"))
                keep_warm(ps[:, BK_X, :], 6)
                pe.wait_ge(s_split, 3 * TILES)
                pe.wait_ge(s_bz, 1)
                pe.wait_ge(s_bias, 48)
                gather(0, 0)
                pe.wait_ge(empt_v, EV("rank"))
                keep_warm(ps[:, BK_GU, :], 4)
                slots, fills = slots_from(0, 7), fills_from(0, 7)
                gate_up_bias(0, 0)
                pe.wait_ge(s_xe, 1)
                for q in range(1, 4):
                    gate_up_chunk(0, q, slots[q - 1], fills[q - 1], last=False)
                gather(1, 1)
                gate_up_bias(1, 1, BK_OUT)
                pe.wait_ge(s_xe, 2)
                gate_up_chunk(1, 0, slots[3], fills[3], BK_OUT)
                pe.wait_ge(s_first, 32)
                gate_up_rows(0, 0, first_gu, True).then_inc(s_gu0, 1)
                for q in range(1, 4):
                    gate_up_chunk(1, q, slots[3 + q], fills[3 + q], BK_OUT)
                hidden_ready(0)
                turn_hidden(0)
                gather(2, 0)
                down(0, 0, slots_from(d_chunk(0, 0), 2), fills_from(d_chunk(0, 0), 2))

                def ring_place(chunk, e, n, since):
                    if type(e) is int:
                        return slots_from(chunk(e, 0), n), fills_from(chunk(e, 0), n)
                    first = 2 if chunk is gu_chunk else 1
                    return slots_from(chunk(first, 0), n), fills_from(chunk(first, 0), n, since)

                def expert(e, b, pair, since=None):
                    gate_up(e, b, *ring_place(gu_chunk, e, 4, since),
                            (lambda i: spread_tile(e - 2, pair - 1, i)) if b else None,
                            (lambda: hidden_ready(e - 1)) if b else None)
                    if b == 0:
                        hidden_ready(e - 1)
                        turn_selection(e - 1, pair - 1)
                    turn_hidden(e - 1)
                    if type(e) is not int or e < E - 1:
                        gather(e + 1, 1 - b)
                        if type(e) is int and e - 1 == EARLY:
                            down_bias(EARLY, 1 - b)
                            pe.wait_ge(s_early, 96)
                            down_rows(1 - b, 0, early_down).then_inc(s_dearly, 1)
                        else:
                            down(e - 1, 1 - b, *ring_place(d_chunk, e - 1, 2, since))

                most = longest(pe)
                for b in range(2):
                    expert(2 + b, b, 1)
                with pe.Fori(2, EARLY // 2) as pair:
                    for b in range(2):
                        expert(pair * 2 + b, b, pair, pair * 2 + (b - 2))
                for e in range(EARLY, E):
                    expert(e, e % 2, e // 2)
                slots, fills = ring_place(d_chunk, E - 2, 2, None)
                down_bias(E - 2, 0)
                down_chunk(0, 0, slots[0], fills[0])
                hidden_ready(E - 1)
                turn_selection(E - 1, E // 2 - 1)
                turn_hidden(E - 1)
                down_chunk(0, 1, slots[1], fills[1])
                slots, fills = ring_place(d_chunk, E - 1, 2, None)
                down_bias(E - 1, 1, BK_X)
                down_chunk(1, 0, slots[0], fills[0], BK_X)
                pe.wait_ge(s_gc, E)
                pe.wait_ge(s_uc, E)
                keep_warm(ps[:, BK_GU, :], 8)
                down_chunk(1, 1, slots[1], fills[1], BK_X)
                pe.wait_ge(s_add, TILES * (E // 2 - 1))
                pe.wait_ge(s_hts, E)
                for i in range(TILES):
                    spread_tile(E - 1, E // 2 - 1, i, bk=OUT_BANKS[i])

                def piece(e, n, r):
                    k, g = E + n, E // 2 + n
                    pe.wait_ge(s_add, TILES * g)
                    gather(k, 0)
                    gate_up(k, 0, slots_from(N_CHUNKS, 4), fills_from(N_CHUNKS, 4, n))
                    hidden_ready(k)
                    turn_selection(k, g)
                    turn_hidden(k)
                    down(k, 0, slots_from(N_CHUNKS + 4, 2), fills_from(N_CHUNKS + 4, 2, n))
                    for i in range(TILES):
                        spread_tile(k, g, i, rows=CAP)
                more_pieces(pe, most, piece)

            @block.vector
            def _(dve):
                steps = [0]

                def link(ins):
                    steps[0] += 1
                    ins.then_inc(ord_v, 1)
                    dve.wait_ge(ord_v, steps[0])

                def full(name):
                    dve.wait_ge(filled, JOB[name] + 1)
                    return bank(JOB[name])

                V = nc.vector
                V.memset(acc[:, 2, :], 0.0).then_inc(s_zero, 1)
                V.memset(xa[:, :, 0:HA], 0.0)
                V.memset(vx[:, :, 0:HC], 0.0)
                V.memset(lg[:, :, E:], -3.0e38)

                def mean_square(i, n, sums):
                    m = sums + 3 + i
                    dve.wait_ge(s_sq, n)
                    V.tensor_scalar(stat[:, m:m + 1], stat[:, m - 3:m - 2], 1.0 / D, EPS, ALU.mult, ALU.add).then_inc(s_ms, 1)

                def inverse(i, n, sums):
                    m = sums + 3 + i
                    dve.wait_ge(s_root, n if n <= TILES else n + 1)
                    link(V.reciprocal(stat[:, m + 6:m + 7], stat[:, m + 3:m + 4]))
                    return stat[:, m + 6:m + 7]

                def inverse_root(i, n, sums):
                    mean_square(i, n, sums)
                    return inverse(i, n, sums)

                for i in range(TILES):
                    inv = inverse_root(i, i + 1, 0)
                    V.tensor_scalar(x_tok[:, i, :], acc[:, i, :], inv, None, ALU.mult).then_inc(s_xn, 1)
                dve.wait_ge(s_gain, 16)
                for k in range(1, NT, 2):
                    V.tensor_scalar(hn[:, k, :], full(f"hn{k}")[:, 0:T], g_mix[:, k:k + 1], None, ALU.mult).then_inc(empt_v, 1)
                V.tensor_copy(par[:].rearrange("p c n -> p (c n)"), full("par")[:, 0:NT * N_PAR]).then_inc(empt_v, 1)
                z = full("sta")[:, 0:NT * 32].rearrange("p (c r) -> p c r", c=NT)
                V.tensor_copy(xa[:, :, HA + T_P:].rearrange("p c (s t) -> p c s t", s=SEQS)[:, :, :, 0:HA],
                              z[:, :, 0:SEQS * HA].rearrange("p c (s t) -> p c s t", s=SEQS))
                V.tensor_copy(h0[:], z[:, :, SEQS * HA:]).then_inc(empt_v, 1)
                dve.wait_ge(empt_v, EV("par"))
                lam = par[:, :, LAM]
                V.scalar_tensor_tensor(lamw[:, 0, :], lam, -1.0, lam, ALU.mult, ALU.max).then_inc(s_lam, 1)
                dve.wait_ge(s_lexp, 1)
                link(V.tensor_scalar(lamw[:, 2, :], lamw[:, 1, :], 2.0, None, ALU.add))
                link(V.reciprocal(lamw[:, 3, :], lamw[:, 2, :]))
                link(V.tensor_tensor(lamw[:, 2, :], lamw[:, 1, :], lamw[:, 3, :], ALU.mult))
                link(V.tensor_tensor(lamw[:, 3, :], lamw[:, 2, :], lamw[:, 2, :], ALU.mult))
                link(V.tensor_scalar(lamw[:, 0, :], lamw[:, 3, :], 1.0 / 17, None, ALU.mult))
                for n in (15, 13, 11, 9, 7, 5, 3):
                    link(V.scalar_tensor_tensor(lamw[:, 0, :], lamw[:, 0, :], 1.0 / n, lamw[:, 3, :], ALU.add, ALU.mult))
                link(V.scalar_tensor_tensor(lamw[:, 0, :], lamw[:, 0, :], 1.0, lamw[:, 2, :], ALU.add, ALU.mult))
                link(V.tensor_scalar(lamw[:, 1, :], lam, -1.0, 0.0, ALU.mult, ALU.max))
                link(V.scalar_tensor_tensor(lamw[:, 2, :], lamw[:, 0, :], 2.0, lamw[:, 1, :], ALU.mult, ALU.add))
                V.tensor_scalar(lamw[:, 4, :], lamw[:, 2, :], -RG_C, None, ALU.mult)
                V.tensor_scalar(lamw[:, 5, :], lamw[:, 2, :], RG_C / 2, None, ALU.mult).then_inc(s_sp, 1)

                def convolve(c, taps, hist, src, dst, w_row, b_row, done):
                    s4 = src[:, :, hist + T_P:].rearrange("p c (s t) -> p c s t", s=SEQS)
                    d4 = dst[:, :, T_P:].rearrange("p c (s t) -> p c s t", s=SEQS)
                    base = c * (2 * taps)
                    for j in range(taps):
                        for n in range(4):
                            cc = c + n % 2
                            w = par[:, cc, w_row + j:w_row + j + 1]
                            if n < 2:
                                x, y = src[:, cc, j:j + T_P], dst[:, cc, 0:T_P]
                            else:
                                x, y = s4[:, cc, :, j:j + STEPS], d4[:, cc]
                            if j == 0:
                                V.tensor_scalar(y, x, w, par[:, cc, b_row:b_row + 1], ALU.mult, ALU.add).then_inc(done, 1)
                            else:
                                dve.wait_ge(done, base + (4 * (j - 1) + n + 1))
                                V.scalar_tensor_tensor(y, x, w, y, ALU.mult, ALU.add).then_inc(done, 1)

                with dve.Fori(0, NT // 2) as half:
                    c = half * 2
                    dve.wait_ge(s_v, c * 2 + 4)
                    base = c * (KC + 2)
                    for j in range(KC):
                        past = 0
                        if j == KC // 2:
                            dve.wait_ge(s_tap, c + 2)
                            for n in range(2):
                                V.tensor_reduce(vc[:, c + n, T_P:].rearrange("p (s t) -> p s t", s=SEQS),
                                                taps_s[:, n], AX_X, ALU.add).then_inc(s_conv, 1)
                            for n in range(2):
                                dve.wait_ge(s_conv, base + (CONV_MID - 3 + n))
                                V.tensor_scalar(vc[:, c + n, T_P:], vc[:, c + n, T_P:], par[:, c + n, B_DW:B_DW + 1], None,
                                                ALU.add).then_inc(s_conv, 1)
                            past = 4
                        elif j > KC // 2:
                            past = 4
                        for n in range(2):
                            w = par[:, c + n, W_DW + j:W_DW + j + 1]
                            x, y = vx[:, c + n, j:j + T_P], vc[:, c + n, 0:T_P]
                            if j == 0:
                                V.tensor_scalar(y, x, w, par[:, c + n, B_DW:B_DW + 1], ALU.mult, ALU.add).then_inc(s_conv, 1)
                            else:
                                dve.wait_ge(s_conv, base + (2 * (j - 1) + n + 1 + (past if j != KC // 2 else 0)))
                                V.scalar_tensor_tensor(y, x, w, y, ALU.mult, ALU.add).then_inc(s_conv, 1)
                dve.wait_ge(empt_a, EA("xa1"))
                convolve(0, KA, HA, xa, xc, W_CA, B_CA, s_xc)
                dve.wait_ge(s_conv, N_CONV)
                mean = full("mean")[:, 0:T].unsqueeze(1).to_broadcast([P, NT, T])
                V.tensor_tensor(vc[:, :, :], vc[:, :, :], mean, ALU.subtract).then_inc(empt_v, 1)
                with dve.Fori(1, NT // 2) as half:
                    c = half * 2
                    dve.wait_ge(empt_a, c + (EA("xa0") + 1))
                    convolve(c, KA, HA, xa, xc, W_CA, B_CA, s_xc)
                V.tensor_scalar(sg[:, 0, :], full("var")[:, 0:T], EPS, None, ALU.add).then_inc(empt_v, 1)
                dve.wait_ge(s_root, TILES + 1)
                link(V.reciprocal(sg[:, 0, :], sg[:, 1, :]))
                inv = sg[:, 0, :].unsqueeze(1).to_broadcast([P, NT, T])
                V.tensor_tensor(vc[:, :, :], vc[:, :, :], inv, ALU.mult).then_inc(s_ln, 1)
                dve.wait_ge(s_ln, 1)
                for c in range(NT):
                    dve.wait_ge(s_sil, c + 1)
                    link(V.tensor_scalar(vc[:, c, :], vc[:, c, :], par[:, c, G_LN:G_LN + 1], par[:, c, B_LN:B_LN + 1],
                                         ALU.mult, ALU.add))
                    V.tensor_tensor(vc[:, c, :], vc[:, c, :], silu[c], ALU.mult).then_inc(s_s, 1)
                dve.wait_ge(empt_a, EA("i7"))
                dve.wait_ge(s_xc, N_XC)
                link(V.tensor_tensor(ig[:, :, :], ig[:, :, :], xc[:, :, :], ALU.mult))
                dve.wait_ge(s_aw, NT)
                V.scalar_tensor_tensor(xc[:, :, :], aa[:, :, :], 1.0, rt[:, :, :], ALU.add, ALU.mult).then_inc(s_w, 1)
                link(V.scalar_tensor_tensor(ig[:, :, :], aa[:, :, :], 1.0, ig[:, :, :], ALU.add, ALU.mult))
                dve.wait_ge(s_w, 1)
                link(V.tensor_scalar(aa[:, :, :], xc[:, :, :], -1.0, 1.0, ALU.mult, ALU.add))
                dve.wait_ge(s_rtt, 1)
                link(V.tensor_tensor(ig[:, :, :], ig[:, :, :], rt[:, :, :], ALU.mult))
                first = slice(T_P, T, STEPS)
                link(V.tensor_tensor(h0[:], h0[:], aa[:, :, first], ALU.mult))
                link(V.tensor_tensor(ig[:, :, first], ig[:, :, first], h0[:], ALU.add))
                V.memset(aa[:, :, first], 0.0)
                link(V.memset(aa[:, :, 0:1], 0.0))
                V.tensor_tensor_scan(xc_w, xa_w[:, 0:TW], ig_w, 0.0, ALU.mult, ALU.add).then_inc(s_hs, 1)
                dve.wait_ge(s_hs, 1)
                link(V.tensor_tensor(gate_a[:, :, :], gate_a[:, :, :], xc[:, :, :], ALU.mult))
                for c in range(NT):
                    V.scalar_tensor_tensor(mt[:, c, :], full(f"pw{c}")[:, 0:T], par[:, c, B_PW:B_PW + 1], gate_b[:, c, :],
                                           ALU.add, ALU.mult).then_inc(empt_v, 1)
                    dve.wait_ge(empt_v, EV(f"pw{c}"))
                    V.tensor_tensor(mt[:, c, :], mt[:, c, :], gate_a[:, c, :], ALU.add).then_inc(s_m, 1)
                gain = g_ffn[:, :].unsqueeze(2).to_broadcast([P, NT, P])

                def complete(i, halves=(0, 1)):
                    if i == 2:
                        z = full("out2")
                        for c in range(4):
                            a = acc[0:T_S, 2, c * 256:(c + 1) * 256]
                            ins = V.tensor_tensor(a, z[c * T_S:(c + 1) * T_S, 0:256], a, ALU.add)
                        ins.then_inc(empt_v, 1)
                        return
                    for h in halves:
                        a = acc[:, i, h * 512:(h + 1) * 512]
                        V.tensor_tensor(a, full(f"out{i}{h}"), a, ALU.add).then_inc(empt_v, 1)

                def norm(i):
                    inv = inverse_root(i, TILES + TILE_ORDER.index(i) + 1, 12)
                    V.tensor_scalar(h_tok[:, i, :], acc[:, i, :], inv, None, ALU.mult).then_inc(s_hn, 1)

                def take_turned(i):
                    for h in range(2):
                        z = full(f"ht{i}{'ab'[h]}")[:, :].rearrange("p (k t) -> p k t", k=4)
                        V.tensor_tensor(h_cm[:, 4 * h:4 * h + 4, i * P:(i + 1) * P], z, gain[:, 4 * h:4 * h + 4, :],
                                        ALU.mult).then_inc(empt_v, 1)

                def choose(i):
                    V.tensor_tensor(lg[:, i, 0:E], full(f"logits{i}")[:, 0:E], b_rt[:], ALU.add).then_inc(empt_v, 1)
                    dve.wait_ge(empt_v, EV(f"logits{i}"))
                    link(V.max(top[:, i, :], lg[:, i, :]))
                    V.tensor_scalar(stat[:, i:i + 1], top[:, i, 0:1], -1.0, None, ALU.mult).then_inc(s_neg, 1)
                    dve.wait_ge(s_neg, TILE_ORDER.index(i) + 1)
                    link(V.memset(top[:, i, 4:8], -3.0e38))
                    link(V.match_replace(lgr[:, i, :], top[:, i, :], lg[:, i, :], 3.0e38))
                    link(V.tensor_scalar(mask[:, i, :], lgr[:, i, 0:E], 3.0e38, None, ALU.is_equal))
                    if i == 2:
                        V.memset(mask[T_S:2 * T_S, 2, :], 0.0)
                        link(V.memset(mask[2 * T_S:, 2, :], 0.0))
                    V.tensor_copy(mask_h[:, i, :], mask[:, i, :]).then_inc(s_mask, 1)

                dve.wait_ge(s_rt, 48)
                complete(2)
                norm(2)
                complete(0, (0,))
                take_turned(2)
                complete(0, (1,))
                norm(0)
                choose(2)
                complete(1, (0,))
                take_turned(0)
                complete(1, (1,))
                norm(1)
                choose(0)
                take_turned(1)
                choose(1)
                z = full("rank")
                zr = z[:, 0:TILES * E].rearrange("p (i e) -> p i e", i=TILES)
                link(V.scalar_tensor_tensor(rank[:, :, :], zr, 1.0, mask[:, :, :], ALU.add, ALU.mult))
                link(V.tensor_scalar(rank[:, :, :], rank[:, :, :], -1.0, None, ALU.add))

                picks = ident[:, :].rearrange("p (m e) -> p m e", e=E)

                def select(e, b, ranks):
                    for i in range(TILES):
                        ins = V.tensor_scalar(sel[:, b, i, :], slot_no[:, :], ranks[:, i, bass.ds(e, 1)], None, ALU.is_equal)
                    ins.then_inc(s_sel, 1)
                    for m in range(2):
                        ins = V.tensor_copy(pick[:, b, m, :], picks[:, m, bass.ds(e, 1)].to_broadcast([P, CAP]))
                    ins.then_inc(s_pick, 1)

                def select_weighted(e, d, g, ranks):
                    if d == 0 and not (type(g) is int and g == 0):
                        dve.wait_ge(s_stp, g)
                    for i in range(TILES):
                        ins = V.tensor_scalar(sel_w[:, i, d, :], slot_no[:, :], ranks[:, i, bass.ds(e, 1)],
                                              comb[:, i, bass.ds(e, 1)], ALU.is_equal, ALU.mult)
                    ins.then_inc(s_selw, 1)
                    V.tensor_copy(pick[:, d, 2, :], picks[:, 2, bass.ds(e, 1)].to_broadcast([P, CAP])).then_inc(s_pickd, 1)

                gains = g_ffn[:, :].unsqueeze(2).to_broadcast([P, NT, CAP])

                def take_inputs(k, b):
                    dve.wait_ge(s_xg, k + 1)
                    z = ps[:, BK_X, :].rearrange("p (k s) -> p k s", k=NT)
                    V.tensor_tensor(x_e[:, b, :, :], z, gains, ALU.mult).then_inc(s_xe, 1)

                def pair_ps(m, k):
                    bk = BK_OUT if type(k) is int and k == 1 else BK_GU
                    return ps[m * CAP:(m + 1) * CAP, bk:bk + 2, :].rearrange("p h n -> p (h n)")

                def clamp_gate(k, last_chunk):
                    if type(k) is int and k == 0:
                        dve.wait_ge(s_gu0, 1)
                    else:
                        dve.wait_ge(used, last_chunk + 1)
                        dve.wait_ge(s_hid, k)
                    V.tensor_scalar(g_e, pair_ps(0, k), LIMIT, None, ALU.min).then_inc(s_gc, 1)

                def clamp_up(k):
                    V.tensor_scalar(u_e, pair_ps(1, k), LIMIT, -LIMIT, ALU.min, ALU.max).then_inc(s_uc, 1)

                def hidden(k):
                    dve.wait_ge(s_uc, k + 1)
                    dve.wait_ge(s_gc, k + 1)
                    if not (type(k) is int and k == 0):
                        dve.wait_ge(s_htp, k)
                    V.scalar_tensor_tensor(hid, u_e, 1.0, g_e, ALU.add, ALU.mult).then_inc(s_prod, 1)
                    dve.wait_ge(s_prod, k + 1)
                    dve.wait_ge(s_sig, k + 1)
                    V.tensor_tensor(hid, hid, sig_e, ALU.mult).then_inc(s_hid, 1)

                def add_tile(g, i, bk=BK_OUT):
                    dve.wait_ge(s_sc, TILES * g + (i + 1))
                    if not (type(g) is int and g == 0):
                        dve.wait_ge(s_add, TILES * g + (i - TILES + 1))
                    V.tensor_tensor(acc[:, i, :], ps[:, bk:bk + 2, :].rearrange("p h n -> p (h n)"),
                                    acc[:, i, :], ALU.add).then_inc(s_add, 1)

                def add_output(g):
                    for i in range(TILES):
                        add_tile(g, i)

                select(0, 0, rank)
                select(1, 1, rank)
                z = full("rank")
                link(V.tensor_copy(cntf[:, 0:E], z[:, TILES * E:(TILES + 1) * E]))
                link(V.tensor_reduce(cntf[:, E:E + 1], cntf[:, 0:E], AX_X, ALU.max))
                V.tensor_copy(counts[:, :], cntf[:, :]).then_inc(s_cnt, 1)
                V.tensor_copy(rnk2[:, :, :], rank[:, :, :]).then_inc(empt_v, 1)
                dve.wait_ge(empt_v, EV("rank"))
                take_inputs(0, 0)
                dve.wait_ge(s_exp, TILES)
                link(V.tensor_tensor(comb[:, :, :], comb[:, :, :], mask[:, :, :], ALU.mult))
                link(V.tensor_reduce(stat[:, 3:6], comb[:, :, :], AX_X, ALU.add))
                link(V.tensor_scalar(stat[:, 3:6], stat[:, 3:6], 1.0e-30, None, ALU.max))
                link(V.reciprocal(stat[:, 6:9], stat[:, 3:6]))
                for i in range(TILES):
                    ins = V.tensor_scalar(comb[:, i, :], comb[:, i, :], stat[:, 6 + i:7 + i], None, ALU.mult)
                link(ins)
                take_inputs(1, 1)
                clamp_gate(0, None)
                clamp_up(0)
                hidden(0)
                select(2, 0, rank)
                select_weighted(0, 0, 0, rank)

                def expert(e, b, pair):
                    clamp_gate(e, gu_chunk(e, 3))
                    take_inputs(e + 1, 1 - b)
                    clamp_up(e)
                    hidden(e)
                    if type(e) is not int or e < E - 2:
                        select(e + 2, b, rank)
                    select_weighted(e, b, pair, rank)
                    if b == 0:
                        add_output(pair - 1)

                expert(1, 1, 0)
                most = longest(dve)
                for b in range(2):
                    expert(2 + b, b, 1)
                with dve.Fori(2, E // 2 - 1) as pair:
                    for b in range(2):
                        expert(pair * 2 + b, b, pair)
                expert(E - 2, 0, E // 2 - 1)
                clamp_gate(E - 1, gu_chunk(E - 1, 3))
                clamp_up(E - 1)
                hidden(E - 1)
                select_weighted(E - 1, 1, E // 2 - 1, rank)
                add_tile(E // 2 - 1, 0, OUT_BANKS[0])
                add_tile(E // 2 - 1, 1, OUT_BANKS[1])
                mean_square(0, 2 * TILES + 1, 0)
                add_tile(E // 2 - 1, 2, OUT_BANKS[2])
                mean_square(1, 2 * TILES + 2, 0)

                def next_ranks(r):
                    dve.wait_ge(s_cnt, r)
                    V.tensor_scalar(rnk2[:, :, :], rnk2[:, :, :], -float(CAP), None, ALU.add).then_inc(s_cnt, 1)

                def piece(e, n, r):
                    k = E + n
                    dve.wait_ge(s_cnt, r + 1)
                    select(e, 0, rnk2)
                    take_inputs(k, 0)
                    clamp_gate(k, N_CHUNKS + 6 * n + 3)
                    clamp_up(k)
                    hidden(k)
                    select_weighted(e, 0, E // 2 + n, rnk2)
                    add_output(E // 2 + n)
                def norm_rows(i, n):
                    V.scalar_tensor_tensor(h_tok[:, i, :], acc[:, i, :], inverse(i, n, 0), g_fin, ALU.mult,
                                           ALU.mult).then_inc(s_fin, 1)

                def norm_again():
                    dve.wait_ge(s_fin, TILES)
                    V.memset(stat[:, 12:13], 0.0).then_inc(s_sum, 1)
                    for i in range(TILES):
                        mean_square(i, 3 * TILES + i + 1, 0)
                        norm_rows(i, 3 * TILES + i + 1)

                dve.wait_ge(s_gfin, 16)
                norm_rows(0, 2 * TILES + 1)
                mean_square(2, 2 * TILES + 3, 0)
                norm_rows(1, 2 * TILES + 2)
                norm_rows(2, 2 * TILES + 3)
                more_pieces(dve, most, piece, next_ranks, norm_again)


_INS = ["x_prompt", "x_sample", "state_conv_a", "state_h", "state_conf", "g_mix", "w_in", "w_conv_a", "b_conv_a",
        "w_rg_a", "b_rg_a", "w_rg_x", "b_rg_x", "rg_lambda", "w_conf_dw", "b_conf_dw", "g_conf_ln", "b_conf_ln",
        "w_conf_pw", "b_conf_pw", "w_out", "g_ffn", "w_router", "b_router", "w_gate", "b_gate", "w_up", "b_up",
        "w_down", "b_down", "g_final"]
_OUTS = [(1, T_P, D), (SEQS, STEPS, D), (1, 1, HA, D), (1, 1, D), (1, 1, HC, D), (1, SEQS, HA, D), (1, SEQS, D),
         (1, SEQS, HC, D)]


def kernel(**inputs):
    import concourse.bacc as bacc
    from concourse.bass_utils import run_bass_kernel_spmd

    nc = bacc.Bacc("TRN2", target_bir_lowering=False, num_devices=1)
    arrays, given = {}, {}
    for name in _INS:
        a = np.ascontiguousarray(inputs[name])
        arrays[f"in_{name}"] = a
        given[name] = nc.dram_tensor(f"in_{name}", a.shape, mybir.dt.from_np(a.dtype), kind="ExternalInput").ap()
    outs = [nc.dram_tensor(f"out_{i}", shape, F32, kind="ExternalOutput").ap() for i, shape in enumerate(_OUTS)]
    build(nc, given, outs)
    r = run_bass_kernel_spmd(nc, [arrays], core_ids=[0])
    return tuple(r.results[0][f"out_{i}"] for i in range(len(_OUTS)))
```
